# Optimizing a Trainium2 kernel written in Bass

```python
import math
import jax, jax.numpy as jnp
from jax import lax
import numpy as np

D_MODEL = 1024
BATCH = 1
SEQ = 256
DEPTH = 2

PLE_DIM = 256
CHUNK = 128
EPS = 1e-6
N_BRANCH = 2
M_HEADS = 4
M_QK = 128
M_V = 256
M_INNER = M_HEADS * M_V
S_INNER = 2 * D_MODEL
S_HEADDIM = 64
S_HEADS = S_INNER // S_HEADDIM
S_GROUPS = 4
S_STATE = 128
S_CONV = 4
S_CONV_DIM = S_INNER + 2 * S_GROUPS * S_STATE
D_FF = 2816
SPLIT_SIZES = (M_HEADS * M_QK, M_HEADS * M_QK, M_INNER, M_INNER, M_HEADS, M_HEADS,
               S_INNER, S_CONV_DIM, S_HEADS, N_BRANCH * D_MODEL)
D_IN = 2 * M_HEADS * M_QK + 2 * M_INNER + 2 * M_HEADS + S_INNER + S_CONV_DIM + S_HEADS + N_BRANCH * D_MODEL

kernel_name = "hybrid_mlstm_ssd_macaron_trunk"

def rmsnorm(x, g):
    xf = x.astype(jnp.float32)
    r = lax.rsqrt(jnp.mean(xf * xf, axis=-1, keepdims=True) + EPS)
    return (xf * r).astype(x.dtype) * g

def swiglu(u, w1, w3, w2):
    return (jax.nn.silu(u @ w1) * (u @ w3)) @ w2

def causal_dwconv(x, w, b):
    c = x.shape[-1]
    y = lax.conv_general_dilated(x, w[:, None, :].astype(x.dtype), window_strides=(1,),
                                 padding=[(S_CONV - 1, 0)], dimension_numbers=("NWC", "WIO", "NWC"),
                                 feature_group_count=c)
    return y + b

def mlstm_chunkwise(q, k, v, i_pre, f_pre):
    bsz, s_len, nh, dk = q.shape
    dv = v.shape[-1]
    L = CHUNK
    nc = s_len // L
    f32 = jnp.float32
    q = q.reshape(bsz, nc, L, nh, dk) * (dk ** -0.5)
    k = k.reshape(bsz, nc, L, nh, dk)
    v = v.reshape(bsz, nc, L, nh, dv)
    log_i = jnp.moveaxis(i_pre.astype(f32).reshape(bsz, nc, L, nh), 3, 2)
    log_f = jnp.moveaxis(jax.nn.log_sigmoid(f_pre.astype(f32)).reshape(bsz, nc, L, nh), 3, 2)
    bcum = jnp.cumsum(log_f, axis=-1)
    gtot = bcum[..., -1]
    causal = jnp.tril(jnp.ones((L, L), dtype=bool))
    dlog = jnp.where(causal, bcum[..., :, None] - bcum[..., None, :] + log_i[..., None, :], -jnp.inf)

    a = gtot[..., None] - bcum + log_i
    m_loc = jnp.max(a, axis=-1)
    wa = jnp.exp(a - m_loc[..., None]).astype(v.dtype)
    c_loc = jnp.einsum('bchs,bcshk,bcshv->bchkv', wa, k, v)
    n_loc = jnp.einsum('bchs,bcshk->bchk', wa, k)

    def step(carry, inp):
        c_st, n_st, m_st = carry
        cl, nl, ml, gc = inp
        m_new = jnp.maximum(gc + m_st, ml)
        sp = jnp.exp(gc + m_st - m_new)
        sl = jnp.exp(ml - m_new)
        c_new = sp[..., None, None] * c_st + sl[..., None, None] * cl
        n_new = sp[..., None] * n_st + sl[..., None] * nl
        return (c_new, n_new, m_new), (c_st, n_st, m_st)

    init = (jnp.zeros((bsz, nh, dk, dv), f32), jnp.zeros((bsz, nh, dk), f32), jnp.zeros((bsz, nh), f32))
    _, (c_start, n_start, m_start) = lax.scan(
        step, init, (jnp.moveaxis(c_loc, 1, 0), jnp.moveaxis(n_loc, 1, 0),
                     jnp.moveaxis(m_loc, 1, 0), jnp.moveaxis(gtot, 1, 0)))
    c_start = jnp.moveaxis(c_start, 0, 1)
    n_start = jnp.moveaxis(n_start, 0, 1)
    m_start = jnp.moveaxis(m_start, 0, 1)

    m_inter = bcum + m_start[..., None]
    m_t = jnp.maximum(jnp.max(dlog, axis=-1), m_inter)
    w_intra = jnp.exp(dlog - m_t[..., None])
    w_inter = jnp.moveaxis(jnp.exp(m_inter - m_t), 3, 2)
    sc = jnp.einsum('bcthk,bcshk->bchts', q, k) * w_intra.astype(q.dtype)
    num = (jnp.einsum('bchts,bcshv->bcthv', sc, v)
           + jnp.einsum('bcthk,bchkv->bcthv', q, c_start.astype(q.dtype)) * w_inter[..., None])
    den = (jnp.moveaxis(jnp.sum(sc.astype(f32), axis=-1), 3, 2)
           + w_inter * jnp.einsum('bcthk,bchk->bcth', q, n_start.astype(q.dtype)))
    floor = jnp.exp(-jnp.moveaxis(m_t, 3, 2))
    h = num / jnp.maximum(jnp.abs(den), floor)[..., None]
    return h.reshape(bsz, s_len, nh, dv).astype(v.dtype)

def ssd_chunked(x, dt, a_neg, bm, cm):
    bsz, s_len, nh, hp = x.shape
    ng, ns = bm.shape[-2:]
    ne = nh // ng
    L = CHUNK
    nc = s_len // L
    xw = (x * dt[..., None].astype(x.dtype)).reshape(bsz, nc, L, ng, ne, hp)
    acs = jnp.cumsum((dt * a_neg).reshape(bsz, nc, L, ng, ne), axis=2)
    ah = jnp.transpose(acs, (0, 1, 3, 4, 2))
    bc = bm.reshape(bsz, nc, L, ng, ns)
    cc = cm.reshape(bsz, nc, L, ng, ns)
    causal = jnp.tril(jnp.ones((L, L), dtype=bool))
    decay = jnp.exp(jnp.where(causal, ah[..., :, None] - ah[..., None, :], -jnp.inf))
    cb = jnp.einsum('bctgn,bcsgn->bcgts', cc, bc)
    y_intra = jnp.einsum('bcgts,bcgets,bcsgep->bctgep', cb, decay.astype(x.dtype), xw)

    w_end = jnp.exp(ah[..., -1:] - ah).astype(x.dtype)
    st_loc = jnp.einsum('bcges,bcsgn,bcsgep->bcgepn', w_end, bc, xw)
    g_chunk = jnp.exp(ah[..., -1])

    def step(st, inp):
        sl, gc = inp
        return gc[..., None, None] * st + sl, st

    _, s_start = lax.scan(step, jnp.zeros((bsz, ng, ne, hp, ns), jnp.float32),
                          (jnp.moveaxis(st_loc, 1, 0), jnp.moveaxis(g_chunk, 1, 0)))
    s_start = jnp.moveaxis(s_start, 0, 1)
    y_inter = (jnp.einsum('bctgn,bcgepn->bctgep', cc, s_start.astype(x.dtype))
               * jnp.exp(acs)[..., None].astype(x.dtype))
    return (y_intra + y_inter).reshape(bsz, s_len, nh, hp).astype(x.dtype)

def _dense(key, shape, fan_in):
    return jax.random.normal(key, shape, jnp.float32) * (fan_in ** -0.5)

def _gain(key, shape):
    return 1.0 + 0.02 * jax.random.normal(key, shape, jnp.float32)

def setup_inputs(seed: int = 0) -> dict:
    key = jax.random.key(seed)
    ks = jax.random.split(key, 32)
    nrm = jax.random.normal
    dt0 = jnp.exp(jax.random.uniform(ks[12], (DEPTH, S_HEADS), jnp.float32,
                                     minval=math.log(1e-3), maxval=math.log(1e-1)))
    return {
        "x": nrm(ks[0], (BATCH, SEQ, D_MODEL), jnp.float32),
        "p": nrm(ks[1], (DEPTH, BATCH, SEQ, PLE_DIM), jnp.float32),
        "g_ffn1": _gain(ks[2], (DEPTH, D_MODEL)),
        "w1_ffn1": _dense(ks[3], (DEPTH, D_MODEL, D_FF), D_MODEL),
        "w3_ffn1": _dense(ks[4], (DEPTH, D_MODEL, D_FF), D_MODEL),
        "w2_ffn1": _dense(ks[5], (DEPTH, D_FF, D_MODEL), D_FF),
        "g_mix": _gain(ks[6], (DEPTH, D_MODEL)),
        "w_in": _dense(ks[7], (DEPTH, D_MODEL, D_IN), D_MODEL),
        "b_igate": 0.1 * nrm(ks[8], (DEPTH, M_HEADS), jnp.float32),
        "b_fgate": jnp.linspace(3.0, 6.0, M_HEADS, dtype=jnp.float32)[None, :]
                   + 0.1 * nrm(ks[9], (DEPTH, M_HEADS), jnp.float32),
        "g_mlstm_head": _gain(ks[10], (DEPTH, M_HEADS, M_V)),
        "conv_w": _dense(ks[11], (DEPTH, S_CONV, S_CONV_DIM), S_CONV),
        "conv_b": 0.01 * nrm(ks[13], (DEPTH, S_CONV_DIM), jnp.float32),
        "dt_bias": dt0 + jnp.log(-jnp.expm1(-dt0)),
        "a_log": jnp.log(jax.random.uniform(ks[14], (DEPTH, S_HEADS), jnp.float32, minval=1.0, maxval=16.0)),
        "d_skip": 1.0 + 0.1 * nrm(ks[15], (DEPTH, S_HEADS), jnp.float32),
        "g_ssm_out": _gain(ks[16], (DEPTH, S_INNER)),
        "w_branch_a": _dense(ks[17], (DEPTH, M_INNER, D_MODEL), M_INNER),
        "w_branch_b": _dense(ks[18], (DEPTH, S_INNER, D_MODEL), S_INNER),
        "w_out": _dense(ks[19], (DEPTH, D_MODEL, D_MODEL), D_MODEL),
        "g_ffn2": _gain(ks[20], (DEPTH, D_MODEL)),
        "w1_ffn2": _dense(ks[21], (DEPTH, D_MODEL, D_FF), D_MODEL),
        "w3_ffn2": _dense(ks[22], (DEPTH, D_MODEL, D_FF), D_MODEL),
        "w2_ffn2": _dense(ks[23], (DEPTH, D_FF, D_MODEL), D_FF),
        "g_ple": _gain(ks[24], (DEPTH, D_MODEL)),
        "w_ple_gate": _dense(ks[25], (DEPTH, D_MODEL, D_MODEL), D_MODEL),
        "w_ple": _dense(ks[26], (DEPTH, PLE_DIM, D_MODEL), PLE_DIM),
        "g_final": _gain(ks[27], (D_MODEL,)),
    }

def reference(x, p, g_ffn1, w1_ffn1, w3_ffn1, w2_ffn1, g_mix, w_in, b_igate, b_fgate, g_mlstm_head,
              conv_w, conv_b, dt_bias, a_log, d_skip, g_ssm_out, w_branch_a, w_branch_b, w_out,
              g_ffn2, w1_ffn2, w3_ffn2, w2_ffn2, g_ple, w_ple_gate, w_ple, g_final):
    bsz, s_len, _ = x.shape
    split_at = [int(c) for c in np.cumsum(SPLIT_SIZES)[:-1]]
    h = x
    for i in range(DEPTH):
        h = h + 0.5 * swiglu(rmsnorm(h, g_ffn1[i]), w1_ffn1[i], w3_ffn1[i], w2_ffn1[i])

        u = rmsnorm(h, g_mix[i])
        proj = u @ w_in[i]
        q, k, v, o_pre, i_pre, f_pre, z, xbc, dt_raw, gate_pre = jnp.split(proj, split_at, axis=-1)

        ha = mlstm_chunkwise(q.reshape(bsz, s_len, M_HEADS, M_QK), k.reshape(bsz, s_len, M_HEADS, M_QK),
                             v.reshape(bsz, s_len, M_HEADS, M_V), i_pre + b_igate[i], f_pre + b_fgate[i])
        ha = rmsnorm(ha, g_mlstm_head[i]).reshape(bsz, s_len, M_INNER) * jax.nn.sigmoid(o_pre)

        xbc = jax.nn.silu(causal_dwconv(xbc, conv_w[i], conv_b[i]))
        xs, bm, cm = jnp.split(xbc, [S_INNER, S_INNER + S_GROUPS * S_STATE], axis=-1)
        xs = xs.reshape(bsz, s_len, S_HEADS, S_HEADDIM)
        dt = jax.nn.softplus(dt_raw.astype(jnp.float32) + dt_bias[i].astype(jnp.float32))
        a_neg = -jnp.exp(a_log[i].astype(jnp.float32))
        yb = ssd_chunked(xs, dt, a_neg, bm.reshape(bsz, s_len, S_GROUPS, S_STATE),
                         cm.reshape(bsz, s_len, S_GROUPS, S_STATE))
        yb = (yb + xs * d_skip[i][:, None]).reshape(bsz, s_len, S_INNER)
        yb = rmsnorm(yb * jax.nn.silu(z), g_ssm_out[i])

        g_a, g_b = jnp.split(jax.nn.sigmoid(gate_pre), N_BRANCH, axis=-1)
        merged = g_a * (ha @ w_branch_a[i]) + g_b * (yb @ w_branch_b[i])
        h = h + merged @ w_out[i]

        h = h + 0.5 * swiglu(rmsnorm(h, g_ffn2[i]), w1_ffn2[i], w3_ffn2[i], w2_ffn2[i])

        h = h + jax.nn.sigmoid(rmsnorm(h, g_ple[i]) @ w_ple_gate[i]) * (p[i] @ w_ple[i])
    return rmsnorm(h, g_final)


_drawn_inputs = setup_inputs


def setup_inputs(seed=0):
    import zlib

    import numpy as np

    out = dict(_drawn_inputs(seed))
    spreads = {}
    factors = {'g_ffn1': 4.279,
     'b_igate': 64.0,
     'g_mlstm_head': 38.907,
     'conv_b': 6.891,
     'g_ssm_out': 21.139,
     'g_ffn2': 6.36,
     'g_ple': 64.0,
     'g_final': 9.718}
    for name, (base, spread) in spreads.items():
        noise = np.random.default_rng([zlib.crc32(name.encode()), seed]).standard_normal(out[name].shape)
        drawn = base * np.exp(spread * noise) if base else spread * noise
        out[name] = __import__('jax').numpy.asarray(drawn.astype(out[name].dtype))
    for name, factor in factors.items():
        out[name] = (out[name] * factor).astype(out[name].dtype)
    return out
```

```python
from contextlib import ExitStack

import concourse.bass as bass
from concourse import mybir

F32 = mybir.dt.float32
F32R = mybir.dt.float32r
BF16 = mybir.dt.bfloat16
ALU = mybir.AluOpType
ACT = mybir.ActivationFunctionType
AX_X = mybir.AxisListType.X

P = 128
EPS = 1e-6
RING = 3


def trunk(nc, T, out):
    DEPTH, D, FF = T["w1_ffn1"].shape
    S = T["x"].shape[1]
    CH = 128
    NC = S // CH
    D_IN = T["w_in"].shape[2]
    MH = T["b_igate"].shape[1]
    MV = T["g_mlstm_head"].shape[2]
    MQK = 128
    SH = T["dt_bias"].shape[1]
    SI = T["g_ssm_out"].shape[1]
    HP = SI // SH
    SCONV, CDIM = T["conv_w"].shape[1:]
    NG = 4
    EH = SH // NG
    PLE = T["p"].shape[3]
    KD = D // P
    NP = 2 * P
    FT = FF // NP
    assert NC == 2 and MH == NG and MV == 2 * P and EH * HP == 4 * P and PLE == 2 * P and S == NP
    assert D_IN == 2 * MH * MQK + 2 * MH * MV + 2 * MH + SI + CDIM + SH + 2 * D

    C_Q, C_K = 0, MH * MQK
    C_V = 2 * MH * MQK
    C_O = C_V + MH * MV
    C_IF = C_O + MH * MV
    C_Z = C_IF + 2 * MH
    C_X = C_Z + SI
    C_B = C_X + SI
    C_C = C_B + NG * P
    C_DT = C_X + CDIM
    C_G = C_DT + SH

    U_FFN = 3 * FT
    GU = 9
    BC, QK, X01, X23, V, Z0, Z1, O, GA = range(GU)
    K_MIX = U_FFN
    K_GB = K_MIX + NG * GU
    K_MERGE = K_GB + 4
    K_OUT = K_MERGE + 12
    K_FFN2 = K_OUT + 4
    K_PLE = K_FFN2 + U_FFN
    NU = K_PLE + 4
    NE = NG * GU + 4
    assert NU % RING == 0 and GU % RING == 0

    ctx = ExitStack()
    with ctx:
        top = [nc.sbuf_base + 64 if isinstance(nc.sbuf_base, int) else 1024]
        top[0] = (top[0] + 63) // 64 * 64

        def at(name, shape, dt, off):
            n = 1
            for d in shape[1:]:
                n *= d
            n *= 2 if dt == BF16 else 4
            return nc.alloc_sbuf_tensor_at(name, shape, dt, offset=off), off + (n + 31) // 32 * 32

        def sb(name, shape, dt=F32):
            t, top[0] = at(name, shape, dt, top[0])
            return t

        raw = [sb(f"w_raw{i}", [P, KD, NP]) for i in range(RING)]
        whi = [sb(f"w_hi{i}", [P, KD, NP], F32R) for i in range(RING)]
        wlo = [sb(f"w_lo{i}", [P, KD, NP], F32R) for i in range(RING)]
        h = sb("h", [P, KD, S])
        u_hi = sb("u_hi", [P, KD, S], F32R)
        u_lo = sb("u_lo", [P, KD, S], F32R)
        gate_a = sb("gate_a", [P, KD, S])
        ha_hi = sb("ha_hi", [P, 2 * MH, S], F32R)
        ha_lo = sb("ha_lo", [P, 2 * MH, S], F32R)
        y_feat = sb("y_feat", [P, SI // P, S])
        w_ple = y_feat[:, 0:8, :].rearrange("p a b -> p (a b)").rearrange("p (k m) -> p k m", k=2)
        p_proj = y_feat[:, 8:16, :]
        p_tok = gate_a[:, 0:2, :]
        p_feat = gate_a[:, 2:4, :]

        ident = sb("ident", [P, P])
        tri_le = sb("tri_le", [P, P])
        tri_gt = sb("tri_gt", [P, P])
        ones = sb("ones", [P, P])
        zeros = sb("zeros", [P, P], BF16)
        m_half = sb("m_half", [P, 2])
        par_all = sb("par_all", [P, DEPTH, 176])
        par = sb("par", [P, 176])
        g_fin = sb("g_fin", [P, KD])
        row_all = sb("row_all", [P, DEPTH, 104])
        wsm = sb("wsm", [P, KD, 40])
        pre = sb("pre", [P, NC, 40])
        spx = sb("spx", [P, NC, 36])
        sp_a = sb("sp_a", [P, NC, 36])
        sp_b = sb("sp_b", [P, NC, 36])
        sp_c = sb("sp_c", [P, NC, 36])
        dA = sb("dA", [P, NC, SH])
        e_a = sb("e_a", [P, SH])
        eacs = sb("eacs", [P, SH])
        w_end = sb("w_end", [P, SH])
        tokc = sb("tokc", [P, 6, MH])
        M4 = sb("M4", [MH, MH, S])
        gcw = sb("gcw", [P, SCONV, 6])
        gcb = sb("gcb", [P, 6])
        gsn = sb("gsn", [P, 4])
        ghn = sb("ghn", [P, 2])
        gtk = sb("gtk", [P, 6])
        var = sb("var", [P, 2])
        rms = sb("rms", [P, 2])
        r_col = sb("r_col", [P, NC, P])
        rB_y = sb("rB_y", [P, S])
        y_ss = sb("y_ss", [P, NC, NG])
        den = sb("den", [P, 2])
        rden = sb("rden", [P, 2])
        nss = sb("nss", [P, 2])
        hvar = sb("hvar", [P, 2])
        hrms = sb("hrms", [P, 2])
        hsc = sb("hsc", [P, 2])

        base = top[0]
        a = base
        seg, a = at("seg", [P, NC, EH, P], F32, a)
        xcv, a = at("xcv", [P, 4, S], F32, a)
        bcv, a = at("bcv", [P, 2, S], F32, a)
        xw, a = at("xw", [P, NC, EH * HP], F32, a)
        xwe, a = at("xwe", [P, EH * HP], F32, a)
        R, a = at("R", [P, 2, 4, P], F32, a)
        y, a = at("y", [P, NC, EH * HP], F32, a)
        zs, a = at("zs", [P, NC, EH * HP], F32, a)
        st, a = at("st", [P, EH * HP], F32, a)
        xin, a = at("xin", [P, 2, 2, S + 3], F32, a)
        cth, a = at("cth", [P, 2, S], F32, a)
        zth, a = at("zth", [P, NC, NP], F32, a)
        qT, a = at("qT", [P, S], F32, a)
        kT, a = at("kT", [P, S], F32, a)
        pm, a = at("pm", [P, NC, P], F32, a)
        scT, a = at("scT", [P, NC, P], F32, a)
        vtok, a = at("vtok", [P, NC, 258], F32, a)
        ktok, a = at("ktok", [P, P], F32, a)
        cst, a = at("cst", [P, 258], F32, a)
        inter, a = at("inter", [P, 258], F32, a)
        num, a = at("num", [P, NC, 258], F32, a)
        osg, a = at("osg", [P, 2, S], F32, a)
        cbm, a = at("cbm", [P, NC, P], F32, a)
        btok, a = at("btok", [P, P], F32, a)
        a2 = base
        yb_hi, a2 = at("yb_hi", [P, SI // P, S], F32R, a2)
        yb_lo, a2 = at("yb_lo", [P, SI // P, S], F32R, a2)
        gate_b, a2 = at("gate_b", [P, KD, S], F32, a2)
        mtmp, a2 = at("mtmp", [P, 2, S], F32, a2)
        mrg, a2 = at("mrg", [P, 2, S], F32, a2)
        a3 = base
        u32, a3 = at("u32", [P, KD, S], F32, a3)
        sa, a3 = at("sa", [P, 2, S], F32, a3)
        h1f, a3 = at("h1f", [P, 2, S], F32, a3)
        h1_hi, a3 = at("h1_hi", [P, 2, S], F32R, a3)
        h1_lo, a3 = at("h1_lo", [P, 2, S], F32R, a3)
        x_tok, a3 = at("x_tok", [P, NC, D], F32, a3)
        a4 = base + 4 * KD * S
        par_rows, a4 = at("par_rows", [P, DEPTH, 2, P], F32, a4)
        row_one, a4 = at("row_one", [1, DEPTH, 104], F32, a4)
        gf_row, a4 = at("gf_row", [KD, P], F32, a4)
        a5 = base + 4 * KD * S
        r_i, a5 = at("r_i", [MH, S], F32, a5)
        r_f, a5 = at("r_f", [MH, S], F32, a5)
        r_b, a5 = at("r_b", [MH, S], F32, a5)
        r_w, a5 = at("r_w", [MH, S], F32, a5)
        r_m, a5 = at("r_m", [MH, S], F32, a5)
        r_x, a5 = at("r_x", [MH, 6, P], F32, a5)
        m_start = sb("m_start", [MH, 1])
        top_all = max(a, a2, a3, a4, a5)
        assert top_all <= nc.sbuf_usable_end

        bank = [ctx.enter_context(nc.psum_tensor(f"bank{i}", [P, 512], F32)) for i in range(8)]

        def two(b):
            return bank[b][:, :].rearrange("p (m s) -> p m s", m=2)

        names = """w_raw0 w_raw1 w_raw2 w_hi w_lo unit_done act_evac const_ready in_loaded par_loaded wsm_loaded
            p_loaded out_stored rows_done par_tr h_ready sq_ready ss_done var_ready rms_ready rcol_ready rB_done
            u32_ready u_hi_ready u_lo_ready silu_done prod_done h1_hi_ready h1_ready small_done x_abs sp_exp
            dA_ready ea_ready cum_done cum_exp row_tr row_ready row_back tok_ready r_built seg_done exp_done
            conv_done tanh_done cv_ready scores_done ktok_ready d_ready p_exp pm_ready sct_ready cb_done
            cbm_done btok_ready m_ready xtr_done xw_ready heads_done cst_ready num0_ready yi_done im_done
            st_ready inter_ready num1_ready nsq_ready hvar_ready hrms_ready hn_ready hnT_done yx_done y_ready
            zth_ready ha32_ready ha_hi_ready ha_ready yT_done yfeat_ready group_ready group_free ysq_ready
            yb_hi_ready yb_ready yvar_ready yrms_ready ycol_ready yB_done yB_ready merge_read mrg_ready
            m_hi_ready m_lo_ready ple_tanh pt_done pt_ready pp_done pp_ready xt_done fin_done row_bcast
            dve_chain pool_chain xtr_in""".split()
        sem = {n: ctx.enter_context(nc.semaphore(n)) for n in names}
        w_raw = [sem["w_raw0"], sem["w_raw1"], sem["w_raw2"]]
        block = ctx.enter_context(nc.Block())

        class Chain:

            def __init__(self, eng, s):
                self.eng, self.s, self.n = eng, s, 0

            def add(self, ins):
                ins.then_inc(self.s, 1)
                self.n += 1

            def wait(self):
                if self.n:
                    self.eng.wait_ge(self.s, self.n)

            def clear(self):
                if self.n:
                    self.eng.wait_ge(self.s, self.n)
                    self.eng.sem_clear(self.s)
                self.n = 0

        @block.sync
        def _(sp):
            def load(k, slot, src, dst, lay):
                sp.wait_ge(sem["w_lo"], lay * NU + k + 1)
                n = src.shape[1] // 2
                sp.dma_start(dst[:, 0:n], src[:, 0:n]).then_inc(w_raw[slot], 16)
                sp.dma_start(dst[:, n:], src[:, n:]).then_inc(w_raw[slot], 16)

            def cols(w, lay, c0, slot):
                src = w[lay].rearrange("(k p) m -> p k m", p=P)[:, :, c0:c0 + NP]
                return src, raw[slot][:, :, :]

            def dcols(w, lay, c0, slot):
                src = w[lay].rearrange("(k p) m -> p k m", p=P)[:, :, bass.ds(c0, NP)]
                return src, raw[slot][:, :, :]

            def rows2(w, lay, j, slot):
                src = w[lay, bass.ds(j * NP, NP), :].rearrange("(k p) m -> p k m", p=P)
                return src, raw[slot][:, :, :].rearrange("p a b -> p (a b)").rearrange("p (k m) -> p k m", k=2)

            def ffn(k0, w1, w3, w2, lay):
                s = k0 % RING
                load(k0, s, *cols(w1, lay, 0, s), lay)
                s = (k0 + 1) % RING
                load(k0 + 1, s, *cols(w3, lay, 0, s), lay)
                with nc.sync.Fori(0, FT - 1) as j:
                    a, b, c = [(k0 + 2 + r) % RING for r in range(3)]
                    load(k0 + 2 + j * 3, a, *dcols(w1, lay, (j + 1) * NP, a), lay)
                    load(k0 + 3 + j * 3, b, *rows2(w2, lay, j, b), lay)
                    load(k0 + 4 + j * 3, c, *dcols(w3, lay, (j + 1) * NP, c), lay)
                s = (k0 + U_FFN - 1) % RING
                load(k0 + U_FFN - 1, s, *rows2(w2, lay, FT - 1, s), lay)

            W = T["w_in"]
            with nc.sync.Fori(0, DEPTH) as lay:
                ffn(0, T["w1_ffn1"], T["w3_ffn1"], T["w2_ffn1"], lay)
                with nc.sync.Fori(0, NG) as g:
                    def two_cols(p, ca):
                        s = (K_MIX + p) % RING
                        wv = W[lay].rearrange("(k p) m -> p k m", p=P)
                        sp.wait_ge(sem["w_lo"], lay * NU + g * GU + (K_MIX + p + 1))
                        sp.dma_start(raw[s][:, :, 0:P], wv[:, :, bass.ds(ca, P)]).then_inc(w_raw[s], 16)
                        sp.dma_start(raw[s][:, :, P:NP], wv[:, :, bass.ds(ca + NG * P, P)]).then_inc(w_raw[s], 16)

                    def one(p, c):
                        s = (K_MIX + p) % RING
                        load(K_MIX + g * GU + p, s, *dcols(W, lay, c, s), lay)

                    two_cols(BC, g * P + C_B)
                    two_cols(QK, g * P + C_Q)
                    one(X01, g * (4 * P) + C_X)
                    one(X23, g * (4 * P) + C_X + NP)
                    one(V, g * NP + C_V)
                    one(Z0, g * (4 * P) + C_Z)
                    one(Z1, g * (4 * P) + C_Z + NP)
                    one(O, g * NP + C_O)
                    one(GA, g * NP + C_G)
                for i in range(4):
                    s = (K_GB + i) % RING
                    load(K_GB + i, s, *cols(W, lay, C_G + D + i * NP, s), lay)
                with nc.sync.Fori(0, 4) as m:
                    s = K_MERGE % RING
                    load(K_MERGE + m * 3, s, *dcols(T["w_branch_a"], lay, m * NP, s), lay)
                    for kh in range(2):
                        s = (K_MERGE + 1 + kh) % RING
                        src = T["w_branch_b"][lay, kh * D:(kh + 1) * D, :].rearrange("(k p) m -> p k m", p=P)
                        load(K_MERGE + 1 + kh + m * 3, s, src[:, :, bass.ds(m * NP, NP)], raw[s][:, :, :], lay)
                for i in range(4):
                    s = (K_OUT + i) % RING
                    load(K_OUT + i, s, *cols(T["w_out"], lay, i * NP, s), lay)
                ffn(K_FFN2, T["w1_ffn2"], T["w3_ffn2"], T["w2_ffn2"], lay)
                for i in range(4):
                    s = (K_PLE + i) % RING
                    load(K_PLE + i, s, *cols(T["w_ple_gate"], lay, i * NP, s), lay)
            sp.wait_ge(sem["fin_done"], 4)
            sp.dma_start(out[0].rearrange("(c t) d -> t c d", t=P), x_tok[:, :, :]).then_inc(sem["out_stored"], 16)
            sp.wait_ge(sem["out_stored"], 16)

        @block.gpsimd
        def _(pool):
            g_ = nc.gpsimd
            ch = Chain(pool, sem["pool_chain"])
            ch.add(g_.memset(ident[:, :], 0.0))
            ch.add(g_.memset(ones[:, :], 1.0))
            ch.add(g_.memset(m_half[:, :], -0.5))
            ch.wait()
            ch.add(g_.affine_select(out=ident[:, :], in_=ident[:, :], compare_op=ALU.not_equal, fill=1.0,
                                    base=0, pattern=[[-1, P]], channel_multiplier=1))
            ch.add(g_.affine_select(out=tri_le[:, :], in_=ones[:, :], compare_op=ALU.is_ge, fill=0.0,
                                    base=0, pattern=[[1, P]], channel_multiplier=-1))
            g_.affine_select(out=tri_gt[:, :], in_=ones[:, :], compare_op=ALU.is_gt, fill=0.0,
                             base=0, pattern=[[-1, P]], channel_multiplier=1).then_inc(sem["const_ready"], 1)
            pool.wait_ge(sem["rows_done"], 16 * 5)
            g_.partition_broadcast(row_all[:, :, :].rearrange("p a b -> p (a b)"),
                                   row_one[0:1, :, :].rearrange("p a b -> p (a b)")).then_inc(sem["row_bcast"], 1)
            ch.clear()

            def power(n, ready, src, done, dst):
                pool.wait_ge(sem[ready], n)
                g_.tensor_tensor(dst, src, m_half[:, :], ALU.pow).then_inc(sem[done], 1)

            with nc.gpsimd.Fori(0, DEPTH) as lay:
                power(lay * 4 + 1, "var_ready", var[:, :], "rms_ready", rms[:, :])
                power(lay * 4 + 2, "var_ready", var[:, :], "rms_ready", rms[:, :])
                with nc.gpsimd.Fori(0, NG) as g:
                    G = pool.snap(lay * NG + g)
                    pool.wait_ge(sem["group_free"], G + 1)
                    pool.wait_ge(sem["tok_ready"], lay * 2 + 2)
                    pool.wait_ge(sem["dA_ready"], lay + 1)
                    cw = par[:, 0:SCONV * 24].rearrange("p (j t) -> p j t", j=SCONV)
                    g_.tensor_copy(gcw[:, :, 2:6], cw[:, :, bass.ds(g * 4, 4)])
                    for b in range(2):
                        g_.tensor_copy(gcw[:, :, b:b + 1], cw[:, :, bass.ds(g + 16 + 4 * b, 1)])
                        g_.tensor_copy(gcb[:, b:b + 1], par[:, bass.ds(g + 96 + 16 + 4 * b, 1)])
                    g_.tensor_copy(gcb[:, 2:6], par[:, bass.ds(g * 4 + 96, 4)])
                    g_.tensor_copy(gsn[:, :], par[:, bass.ds(g * 4 + 120, 4)])
                    g_.tensor_copy(ghn[:, :], par[:, bass.ds(g * 2 + 136, 2)])
                    g_.tensor_copy(gtk[:, :].unsqueeze(2), tokc[:, :, bass.ds(g, 1)]).then_inc(sem["group_ready"], 1)
                    for c in range(NC):
                        for b in range(2):
                            pool.wait_ge(sem["seg_done"], G * 4 + (2 * c + b + 1))
                            g_.tensor_tensor(
                                R[:, b, :, :], tri_le[:, :].unsqueeze(1).broadcast_to([P, 4, P]),
                                dA[:, c, bass.ds(g * EH + 4 * b, 4)].unsqueeze(2).broadcast_to([P, 4, P]),
                                ALU.mult).then_inc(sem["r_built"], 1)
                    pool.wait_ge(sem["p_exp"], G + 1)
                    g_.tensor_tensor(pm[:, :, :], pm[:, :, :], tri_le[:, :].unsqueeze(1).broadcast_to([P, NC, P]),
                                     ALU.mult).then_inc(sem["pm_ready"], 1)
                    power(G + 1, "hvar_ready", hvar[:, :], "hrms_ready", hrms[:, :])
                power(lay + 1, "yvar_ready", var[:, :], "yrms_ready", rms[:, :])
                power(lay * 4 + 3, "var_ready", var[:, :], "rms_ready", rms[:, :])
                power(lay * 4 + 4, "var_ready", var[:, :], "rms_ready", rms[:, :])
            power(DEPTH * 4 + 1, "var_ready", var[:, :], "rms_ready", rms[:, :])

        @block.scalar
        def _(act):
            a_ = nc.scalar
            act.dma_start(x_tok[:, :, :], T["x"][0].rearrange("(c t) d -> t c d", t=P)).then_inc(sem["in_loaded"], 16)
            act.dma_start(par_rows[0:96, :, 0, :],
                          T["conv_w"].rearrange("l j (t c) -> (j t) l c", c=P)).then_inc(sem["par_loaded"], 16)
            r0 = 0
            for n, w in ((24, T["conv_b"]), (16, T["g_ssm_out"]), (8, T["g_mlstm_head"].rearrange("l h v -> l (h v)")),
                         (8, T["g_ffn1"]), (8, T["g_mix"]), (8, T["g_ffn2"]), (8, T["g_ple"])):
                act.dma_start(par_rows[r0:r0 + n, :, 1, :],
                              w.rearrange("l (t c) -> t l c", c=P)).then_inc(sem["par_loaded"], 16)
                r0 += n
            act.dma_start(gf_row[:, :], T["g_final"].rearrange("(t c) -> t c", c=P)).then_inc(sem["par_loaded"], 16)
            r0 = 0
            for w in (T["b_igate"], T["b_fgate"], T["dt_bias"], T["a_log"], T["d_skip"]):
                n = w.shape[1]
                act.dma_start(row_one[0:1, :, r0:r0 + n], w.unsqueeze(0)).then_inc(sem["rows_done"], 16)
                r0 += n

            def hi(lay, k, k3, slot):
                act.wait_ge(w_raw[slot], (lay * (NU // RING) + k3 + 1) * 32)
                act.wait_ge(sem["unit_done"], lay * NU + k + 1)
                a_.activation(whi[slot][:, :, :], raw[slot][:, :, :], ACT.Copy).then_inc(sem["w_hi"], 1)

            def shi(lay, k):
                if k < NU:
                    hi(lay, k, k // RING, k % RING)

            def done(lay, k):
                act.wait_ge(sem["unit_done"], lay * NU + k + (RING + 1))

            def norm(lay, n):
                N = lay * 4 + n
                for i in range(4):
                    act.wait_ge(sem["h_ready"], N * 4 + (i + 1))
                    a_.activation(u32[:, 2 * i:2 * i + 2, :], h[:, 2 * i:2 * i + 2, :],
                                  ACT.Square).then_inc(sem["sq_ready"], 1)

            def norm_hi(lay, n):
                N = lay * 4 + n
                for k in range(KD):
                    act.wait_ge(sem["u32_ready"], N * KD + (k + 1))
                    a_.activation(u_hi[:, k, :], u32[:, k, :], ACT.Copy).then_inc(sem["u_hi_ready"], 1)

            def ffn(lay, f, k0):
                F = lay * 2 + f
                shi(lay, k0 + 2)
                done(lay, k0)
                a_.activation(sa[:, :, :], two(4), ACT.Silu).then_inc(sem["silu_done"], 1)
                shi(lay, k0 + 3)
                b3 = (k0 + 2) // RING
                with nc.scalar.Fori(0, FT - 1) as j:
                    def sh(r):
                        k = k0 + 4 + r
                        hi(lay, k + j * 3, k // RING + j, k % RING)
                    act.wait_ge(sem["prod_done"], F * FT + j + 1)
                    a_.activation(h1_hi[:, :, :], h1f[:, :, :], ACT.Copy).then_inc(sem["h1_hi_ready"], 1)
                    sh(0)
                    act.wait_ge(sem["unit_done"], lay * NU + j * 3 + (k0 + 2 + RING + 1))
                    a_.activation(sa[:, :, :], two(4), ACT.Silu).then_inc(sem["silu_done"], 1)
                    sh(1)
                    sh(2)
                act.wait_ge(sem["prod_done"], (F + 1) * FT)
                a_.activation(h1_hi[:, :, :], h1f[:, :, :], ACT.Copy).then_inc(sem["h1_hi_ready"], 1)
                shi(lay, k0 + U_FFN + 1)

            def small(lay):
                act.wait_ge(sem["x_abs"], lay + 1)
                a_.activation(sp_b[:, :, :], sp_a[:, :, :], ACT.Exp, scale=-1.0).then_inc(sem["sp_exp"], 1)
                act.wait_ge(sem["row_bcast"], 1)
                a_.activation(e_a[:, :], row_all[:, lay, 40:72], ACT.Exp).then_inc(sem["ea_ready"], 1)
                act.wait_ge(sem["cum_done"], lay + 1)
                a_.activation(eacs[:, :], bank[7][:, 0:SH], ACT.Exp)
                a_.activation(w_end[:, :], bank[7][:, SH:2 * SH], ACT.Exp).then_inc(sem["cum_exp"], 1)
                act.wait_ge(sem["row_back"], lay + 1)
                tk = bank[6][:, 0:24].rearrange("p (a h) -> p a h", a=6)
                a_.activation(tokc[:, 0:2, :], tk[:, 0:2, :], ACT.Copy).then_inc(sem["tok_ready"], 1)
                a_.activation(tokc[:, 2:6, :], tk[:, 2:6, :], ACT.Exp).then_inc(sem["tok_ready"], 1)

            def groups(lay):
                with nc.scalar.Fori(0, NG) as g:
                    G = act.snap(lay * NG + g)

                    def step(p):
                        k = K_MIX + p + 2
                        hi(lay, g * GU + k, g * (GU // RING) + k // RING, k % RING)

                    def gdone(p):
                        act.wait_ge(sem["unit_done"], lay * NU + g * GU + (K_MIX + p + RING + 1))

                    def tanh_conv(i, dst):
                        act.wait_ge(sem["conv_done"], G * 3 + (i + 1))
                        a_.activation(cth[:, :, :], dst, ACT.Tanh).then_inc(sem["tanh_done"], 1)

                    def decay(c):
                        for b in range(2):
                            act.wait_ge(sem["seg_done"], G * 4 + (2 * c + b + 3))
                            a_.activation(seg[:, c, 4 * b:4 * b + 4, :],
                                          bank[4 + 2 * c + b][:, :].rearrange("p (e t) -> p e t", e=4),
                                          ACT.Exp).then_inc(sem["exp_done"], 1)

                    step(0)
                    gdone(BC)
                    a_.activation(xin[:, 0, :, 3:], two(0), ACT.Copy).then_inc(sem["act_evac"], 1)
                    step(1)
                    tanh_conv(0, bcv[:, :, :])
                    gdone(QK)
                    a_.activation(qT[:, :], bank[1][:, 0:S], ACT.Copy, scale=MQK ** -0.5)
                    a_.activation(kT[:, :], bank[1][:, S:2 * S], ACT.Copy).then_inc(sem["act_evac"], 1)
                    step(2)
                    decay(0)
                    gdone(X01)
                    a_.activation(xin[:, 1, :, 3:], two(2), ACT.Copy).then_inc(sem["act_evac"], 1)
                    step(3)
                    decay(1)
                    act.wait_ge(sem["scores_done"], G + 1)
                    act.wait_ge(sem["group_ready"], G + 1)
                    a_.activation(ktok[:, :], bank[3][:, 256:384], ACT.Copy, scale=gtk[:, 5:6]).then_inc(sem["ktok_ready"], 1)
                    tanh_conv(1, xcv[:, 0:2, :])
                    act.wait_ge(sem["d_ready"], G + 1)
                    a_.activation(pm[:, :, :], pm[:, :, :], ACT.Exp, scale=-1.0).then_inc(sem["p_exp"], 1)
                    gdone(X23)
                    a_.activation(xin[:, 0, :, 3:], two(0), ACT.Copy).then_inc(sem["act_evac"], 1)
                    step(4)
                    tanh_conv(2, xcv[:, 2:4, :])
                    act.wait_ge(sem["cbm_done"], G + 1)
                    a_.activation(btok[:, :], bank[5][:, 256:384], ACT.Copy).then_inc(sem["btok_ready"], 1)
                    gdone(V)
                    a_.activation(vtok[:, :, 0:MV], two(1), ACT.Copy).then_inc(sem["act_evac"], 1)
                    step(5)
                    gdone(Z0)
                    a_.activation(zth[:, :, :], two(2), ACT.Tanh, scale=0.5).then_inc(sem["act_evac"], 1)
                    step(6)
                    act.wait_ge(sem["heads_done"], G + 1)
                    a_.activation(cst[:, 0:257], bank[3][:, 0:257], ACT.Copy).then_inc(sem["cst_ready"], 1)
                    a_.activation(num[:, 0, 0:257], bank[4][:, 0:257], ACT.Copy).then_inc(sem["num0_ready"], 1)
                    gdone(Z1)
                    act.wait_ge(sem["zth_ready"], G + 1)
                    a_.activation(zth[:, :, :], two(0), ACT.Tanh, scale=0.5).then_inc(sem["act_evac"], 1)
                    step(7)
                    act.wait_ge(sem["im_done"], G + 1)
                    a_.activation(inter[:, 0:257], bank[3][:, 0:257], ACT.Copy, scale=gtk[:, 4:5]).then_inc(sem["inter_ready"], 1)
                    act.wait_ge(sem["yi_done"], G + 1)
                    a_.activation(st[:, :], bank[4][:, :], ACT.Copy).then_inc(sem["st_ready"], 1)
                    act.wait_ge(sem["num1_ready"], G + 1)
                    for c in range(NC):
                        squares = (pm, scT)[c][:, :, :].rearrange("p a b -> p (a b)")
                        i = a_.activation(squares, num[:, c, 0:MV], ACT.Square, accum_out=nss[:, c:c + 1])
                    i.then_inc(sem["nsq_ready"], 1)
                    gdone(O)
                    a_.activation(osg[:, :, :], two(1), ACT.Tanh, scale=0.5).then_inc(sem["act_evac"], 1)
                    step(8)
                    act.wait_ge(sem["ha32_ready"], G + 1)
                    a_.activation(ha_hi[:, bass.ds(g * 2, 2), :], osg[:, :, :], ACT.Copy).then_inc(sem["ha_hi_ready"], 1)
                    act.wait_ge(sem["y_ready"], G + 1)
                    for c in range(NC):
                        i = a_.activation((st, xwe)[c][:, :], y[:, c, :], ACT.Square, accum_out=y_ss[:, c, bass.ds(g, 1)])
                    i.then_inc(sem["ysq_ready"], 1)
                    gdone(GA)
                    a_.activation(gate_a[:, bass.ds(g * 2, 2), :], two(2), ACT.Tanh, scale=0.5).then_inc(sem["act_evac"], 1)
                    act.wait_ge(sem["yT_done"], G + 1)
                    for c in range(NC):
                        for t in range(4):
                            i = a_.activation(y_feat[:, bass.ds(g * 4 + t, 1), c * P:(c + 1) * P],
                                              bank[6 + c][:, t * P:(t + 1) * P].unsqueeze(1), ACT.Copy, scale=gsn[:, t:t + 1])
                    i.then_inc(sem["yfeat_ready"], 1)

            with nc.scalar.Fori(0, DEPTH) as lay:
                act.dma_start(wsm[:, :, 0:8], T["w_in"][lay].rearrange("(k p) m -> p k m", p=P)[:, :, C_IF:C_IF + 8],
                              ).then_inc(sem["wsm_loaded"], 16)
                act.dma_start(wsm[:, :, 8:40], T["w_in"][lay].rearrange("(k p) m -> p k m", p=P)[:, :, C_DT:C_DT + SH],
                              ).then_inc(sem["wsm_loaded"], 16)
                shi(lay, 0)
                shi(lay, 1)
                norm(lay, 0)
                norm_hi(lay, 0)
                ffn(lay, 0, 0)
                norm(lay, 1)
                norm_hi(lay, 1)
                small(lay)
                groups(lay)
                act.wait_ge(sem["group_free"], lay * NG + NG + 1)
                for q in range(4):
                    shi(lay, K_GB + q + 2)
                    a_.activation(yb_hi[:, 4 * q:4 * q + 4, :], y_feat[:, 4 * q:4 * q + 4, :], ACT.Copy)\
                        .then_inc(sem["yb_hi_ready"], 1)
                    done(lay, K_GB + q)
                    a_.activation(gate_b[:, 2 * q:2 * q + 2, :], two(q % 3), ACT.Tanh, scale=0.5)\
                        .then_inc(sem["act_evac"], 1)
                act.wait_ge(sem["yB_done"], lay + 1)
                a_.activation(rB_y[:, :], bank[7][:, 0:S], ACT.Copy).then_inc(sem["yB_ready"], 1)
                with nc.scalar.Fori(0, 4) as m:
                    for r in range(3):
                        k = K_MERGE + r + 2
                        hi(lay, m * 3 + k, m + k // RING, k % RING)
                    act.wait_ge(sem["mrg_ready"], lay * 4 + m + 1)
                    a_.activation(u_hi[:, bass.ds(m * 2, 2), :], mrg[:, :, :], ACT.Copy).then_inc(sem["m_hi_ready"], 1)
                act.wait_ge(sem["m_lo_ready"], lay * 4 + 4)
                act.dma_start(w_ple, T["w_ple"][lay].rearrange("(k p) m -> p k m", p=P)).then_inc(sem["p_loaded"], 16)
                act.dma_start(p_tok, T["p"][lay, 0].rearrange("(c t) d -> t c d", t=P)).then_inc(sem["p_loaded"], 16)
                for q in range(4):
                    shi(lay, K_OUT + q + 2)
                act.wait_ge(sem["pt_done"], lay + 1)
                a_.activation(p_feat, two(3), ACT.Copy).then_inc(sem["pt_ready"], 1)
                norm(lay, 2)
                for q in range(4):
                    act.wait_ge(sem["pp_done"], lay * 4 + q + 1)
                    a_.activation(p_proj[:, 2 * q:2 * q + 2, :], two(4 + q % 2), ACT.Copy).then_inc(sem["pp_ready"], 1)
                norm_hi(lay, 2)
                ffn(lay, 1, K_FFN2)
                norm(lay, 3)
                norm_hi(lay, 3)
                for q in range(4):
                    shi(lay, K_PLE + q + 2)
                    done(lay, K_PLE + q)
                    if q >= 2:
                        act.wait_ge(sem["h_ready"], lay * 16 + 16 + (q - 1))
                    a_.activation(sa[:, :, :] if q % 2 == 0 else h1f[:, :, :], two(q % 3), ACT.Tanh,
                                  scale=0.5).then_inc(sem["ple_tanh"], 1)
            norm(DEPTH, 0)

        @block.vector
        def _(dve):
            v_ = nc.vector
            ch = Chain(dve, sem["dve_chain"])
            dve.sem_inc(sem["w_lo"], RING)
            dve.sem_inc(sem["unit_done"], RING)
            dve.sem_inc(sem["act_evac"], RING)
            dve.sem_inc(sem["seg_done"], 2)
            dve.sem_inc(sem["group_free"], 1)
            dve.sem_inc(sem["merge_read"], 2)
            v_.memset(zeros[:, :], 0.0).then_inc(sem["const_ready"], 1)

            def lo(lay, k, slot):
                dve.wait_ge(sem["w_hi"], lay * NU + k + 1)
                v_.tensor_tensor(wlo[slot][:, :, :], raw[slot][:, :, :], whi[slot][:, :, :].bitcast(F32),
                                 ALU.subtract).then_inc(sem["w_lo"], 1)

            def slo(lay, k):
                if k < NU:
                    lo(lay, k, k % RING)

            def done(lay, k):
                dve.wait_ge(sem["unit_done"], lay * NU + k + (RING + 1))

            def norm(lay, n, final=False):
                N = lay * 4 + n
                dve.wait_ge(sem["ss_done"], N + 1)
                v_.tensor_scalar(var[:, 0:1], bank[6][:, 0:1], 1.0 / D, EPS, ALU.mult, ALU.add)
                v_.tensor_scalar(var[:, 1:2], bank[7][:, 0:1], 1.0 / D, EPS, ALU.mult, ALU.add)\
                    .then_inc(sem["var_ready"], 1)
                dve.wait_ge(sem["rms_ready"], N + 1)
                v_.tensor_scalar(r_col[:, 0, :], ones[:, :], rms[:, 0:1], None, ALU.mult)
                v_.tensor_scalar(r_col[:, 1, :], ones[:, :], rms[:, 1:2], None, ALU.mult).then_inc(sem["rcol_ready"], 1)
                dve.wait_ge(sem["rB_done"], N + 1)
                for k in range(KD):
                    gk = g_fin[:, k:k + 1] if final else par[:, 144 + 8 * n + k:145 + 8 * n + k]
                    v_.scalar_tensor_tensor(out=u32[:, k, :], in0=h[:, k, :], scalar=gk, in1=bank[6][:, S:2 * S],
                                            op0=ALU.mult, op1=ALU.mult).then_inc(sem["u32_ready"], 1)
                if not final:
                    for k in range(KD):
                        dve.wait_ge(sem["u_hi_ready"], N * KD + (k + 1))
                        v_.tensor_tensor(u_lo[:, k, :], u32[:, k, :], u_hi[:, k, :].bitcast(F32),
                                         ALU.subtract).then_inc(sem["u_lo_ready"], 1)

            def ffn(lay, f, k0):
                F = lay * 2 + f

                def product(done_value, silu_value):
                    dve.wait_ge(sem["unit_done"], done_value)
                    dve.wait_ge(sem["silu_done"], silu_value)
                    v_.tensor_tensor(h1f[:, :, :], sa[:, :, :], two(5), ALU.mult).then_inc(sem["prod_done"], 1)

                def h1_low(n):
                    dve.wait_ge(sem["h1_hi_ready"], n)
                    v_.tensor_tensor(h1_lo[:, :, :], h1f[:, :, :], h1_hi[:, :, :].bitcast(F32),
                                     ALU.subtract).then_inc(sem["h1_ready"], 1)

                slo(lay, k0 + 2)
                slo(lay, k0 + 3)
                product(lay * NU + (k0 + 1 + RING + 1), F * FT + 1)
                with nc.vector.Fori(0, FT - 1) as j:
                    h1_low(F * FT + j + 1)
                    for r in range(3):
                        k = k0 + 4 + r
                        lo(lay, j * 3 + k, k % RING)
                    product(lay * NU + j * 3 + (k0 + 4 + RING + 1), F * FT + j + 2)
                h1_low((F + 1) * FT)
                slo(lay, k0 + U_FFN + 1)
                done(lay, k0 + U_FFN - 1)
                for i in range(4):
                    v_.scalar_tensor_tensor(out=h[:, 2 * i:2 * i + 2, :], in0=two(i), scalar=0.5,
                                            in1=h[:, 2 * i:2 * i + 2, :], op0=ALU.mult, op1=ALU.add)\
                        .then_inc(sem["h_ready"], 1)

            def small(lay):
                dve.wait_ge(sem["small_done"], lay + 1)
                ps = bank[7][:, 0:80].rearrange("p (c n) -> p c n", c=NC)
                dve.wait_ge(sem["row_bcast"], 1)
                ch.add(v_.tensor_tensor(pre[:, :, :], ps,
                                        row_all[:, lay, 0:40].unsqueeze(1).broadcast_to([P, NC, 40]), ALU.add))
                ch.wait()
                ch.add(v_.tensor_scalar(spx[:, :, 0:4], pre[:, :, 4:8], -1.0, None, ALU.mult))
                ch.add(v_.tensor_copy(spx[:, :, 4:36], pre[:, :, 8:40]))
                ch.wait()
                v_.scalar_tensor_tensor(out=sp_a[:, :, :], in0=spx[:, :, :], scalar=-1.0, in1=spx[:, :, :],
                                        op0=ALU.mult, op1=ALU.max).then_inc(sem["x_abs"], 1)
                ch.add(v_.tensor_scalar(spx[:, :, :], spx[:, :, :], 0.0, None, ALU.max))
                dve.wait_ge(sem["sp_exp"], lay + 1)
                ch.add(v_.tensor_scalar(sp_a[:, :, :], sp_b[:, :, :], 2.0, None, ALU.add))
                ch.wait()
                ch.add(v_.reciprocal(sp_c[:, :, :], sp_a[:, :, :]))
                ch.wait()
                ch.add(v_.tensor_tensor(sp_a[:, :, :], sp_b[:, :, :], sp_c[:, :, :], ALU.mult))
                ch.wait()
                ch.add(v_.tensor_tensor(sp_b[:, :, :], sp_a[:, :, :], sp_a[:, :, :], ALU.mult))
                ch.wait()
                ch.add(v_.tensor_scalar(sp_c[:, :, :], sp_b[:, :, :], 1.0 / 17, None, ALU.mult))
                for n in (15, 13, 11, 9, 7, 5, 3):
                    ch.wait()
                    ch.add(v_.scalar_tensor_tensor(out=sp_c[:, :, :], in0=sp_c[:, :, :], scalar=1.0 / n,
                                                   in1=sp_b[:, :, :], op0=ALU.add, op1=ALU.mult))
                ch.wait()
                ch.add(v_.scalar_tensor_tensor(out=sp_c[:, :, :], in0=sp_c[:, :, :], scalar=1.0,
                                               in1=sp_a[:, :, :], op0=ALU.add, op1=ALU.mult))
                ch.wait()
                ch.add(v_.scalar_tensor_tensor(out=spx[:, :, :], in0=sp_c[:, :, :], scalar=2.0,
                                               in1=spx[:, :, :], op0=ALU.mult, op1=ALU.add))
                ch.wait()
                dve.wait_ge(sem["ea_ready"], lay + 1)
                v_.scalar_tensor_tensor(out=dA[:, :, :], in0=spx[:, :, 4:36], scalar=-1.0,
                                        in1=e_a[:, :].unsqueeze(1).broadcast_to([P, NC, SH]),
                                        op0=ALU.mult, op1=ALU.mult).then_inc(sem["dA_ready"], 1)
                dve.wait_ge(sem["row_tr"], lay + 1)
                ch.add(v_.tensor_copy(r_i[:, :], bank[6][0:MH, 0:S]))
                ch.add(v_.tensor_copy(r_f[:, :], bank[6][0:MH, S:2 * S]))
                ch.wait()
                for c in range(NC):
                    s = slice(c * P, (c + 1) * P)
                    ch.add(v_.tensor_tensor_scan(r_b[:, s], ones[0:MH, :], r_f[:, s], 0.0, ALU.mult, ALU.subtract))
                ch.wait()
                ch.add(v_.tensor_tensor(r_w[:, :], r_i[:, :], r_b[:, :], ALU.subtract))
                ch.wait()
                ch.add(v_.tensor_tensor_scan(r_m[:, 0:P], r_w[:, 0:P], r_w[:, 0:P], 0.0, ALU.max, ALU.max))
                ch.wait()
                ch.add(v_.tensor_tensor(m_start[:, :], r_b[:, P - 1:P], r_m[:, P - 1:P], ALU.add))
                ch.wait()
                ch.add(v_.tensor_tensor_scan(r_m[:, P:], r_w[:, P:], r_w[:, P:], m_start[:, :], ALU.max, ALU.max))
                ch.wait()
                ch.add(v_.tensor_copy(r_x[:, 0:2, :], r_w[:, :].rearrange("p (c t) -> p c t", c=NC)))
                ch.add(v_.scalar_tensor_tensor(out=r_x[:, 2:4, :], in0=r_b[:, :].rearrange("p (c t) -> p c t", c=NC),
                                               scalar=-1.0, in1=r_m[:, :].rearrange("p (c t) -> p c t", c=NC),
                                               op0=ALU.mult, op1=ALU.subtract))
                ch.add(v_.tensor_scalar(r_x[:, 4, :], r_m[:, P:], m_start[:, :], -1.0, ALU.subtract, ALU.mult))
                ch.add(v_.tensor_scalar(r_x[:, 5, :], r_w[:, 0:P], r_m[:, P - 1:P], None, ALU.subtract))
                v_.tensor_tensor(M4[:, :, :], r_m[:, :].unsqueeze(1).broadcast_to([MH, MH, S]),
                                 ident[0:MH, 0:MH].unsqueeze(2).broadcast_to([MH, MH, S]),
                                 ALU.mult).then_inc(sem["row_ready"], 1)
                v_.memset(xin[:, :, :, 0:3], 0.0)
                ch.add(v_.memset(vtok[:, :, MV:MV + 1], 1.0))
                ch.clear()

            def groups(lay):
                with nc.vector.Fori(0, NG) as g:
                    G = dve.snap(lay * NG + g)

                    def step(p):
                        k = K_MIX + p + 2
                        lo(lay, g * GU + k, k % RING)

                    def taken(p):
                        dve.wait_ge(sem["act_evac"], lay * NE + g * GU + (p + RING + 1))

                    def conv(i, buf, tiles, dst):
                        for j in range(SCONV):
                            for q, t in enumerate(tiles):
                                src = xin[:, buf, q, j:j + S]
                                if j == 0:
                                    ins = v_.tensor_scalar(dst[:, q, :], src, gcw[:, 0, t:t + 1], gcb[:, t:t + 1],
                                                           ALU.mult, ALU.add)
                                else:
                                    ins = v_.scalar_tensor_tensor(out=dst[:, q, :], in0=src, scalar=gcw[:, j, t:t + 1],
                                                                  in1=dst[:, q, :], op0=ALU.mult, op1=ALU.add)
                                if j < SCONV - 1 or q == 0:
                                    ch.add(ins)
                                else:
                                    ins.then_inc(sem["conv_done"], 1)
                            if j < SCONV - 1:
                                ch.wait()

                    def silu(i, dst):
                        dve.wait_ge(sem["tanh_done"], G * 3 + (i + 1))
                        v_.scalar_tensor_tensor(out=dst, in0=cth[:, :, :], scalar=1.0, in1=dst,
                                                op0=ALU.add, op1=ALU.mult).then_inc(sem["cv_ready"], 1)

                    heads = bass.ds(g * EH, EH)

                    def per_head(col):
                        return col.unsqueeze(2).broadcast_to([P, EH, HP])

                    def split_heads(x):
                        return x.rearrange("p (e d) -> p e d", e=EH)

                    step(0)
                    step(1)
                    dve.wait_ge(sem["group_ready"], G + 1)
                    taken(BC)
                    conv(0, 0, (0, 1), bcv[:, :, :])
                    silu(0, bcv[:, :, :])
                    step(2)
                    dve.wait_ge(sem["scores_done"], G + 1)
                    for c in range(NC):
                        i = v_.tensor_scalar(pm[:, c, :], bank[4][:, c * P:(c + 1) * P], gtk[:, c:c + 1], 0.0,
                                             ALU.subtract, ALU.max)
                    i.then_inc(sem["d_ready"], 1)
                    step(3)
                    taken(X01)
                    conv(1, 1, (2, 3), xcv[:, 0:2, :])
                    silu(1, xcv[:, 0:2, :])
                    dve.wait_ge(sem["pm_ready"], G + 1)
                    dve.wait_ge(sem["ktok_ready"], G + 1)
                    v_.tensor_tensor(scT[:, :, :], pm[:, :, :], bank[3][:, 0:S].rearrange("p (c t) -> p c t", c=NC),
                                     ALU.mult).then_inc(sem["sct_ready"], 1)
                    step(4)
                    taken(X23)
                    conv(2, 0, (4, 5), xcv[:, 2:4, :])
                    silu(2, xcv[:, 2:4, :])
                    dve.wait_ge(sem["cb_done"], G + 1)
                    v_.tensor_tensor(cbm[:, :, :], bank[5][:, 0:S].rearrange("p (c t) -> p c t", c=NC),
                                     tri_le[:, :].unsqueeze(1).broadcast_to([P, NC, P]), ALU.mult)\
                        .then_inc(sem["cbm_done"], 1)
                    step(5)
                    dve.wait_ge(sem["exp_done"], G * 4 + 4)
                    dve.wait_ge(sem["cbm_done"], G + 1)
                    for c in range(NC):
                        v_.tensor_tensor(seg[:, c, :, :], seg[:, c, :, :],
                                         cbm[:, c, :].unsqueeze(1).broadcast_to([P, EH, P]), ALU.mult)\
                            .then_inc(sem["m_ready"], 1)
                    step(6)
                    taken(Z0)
                    v_.scalar_tensor_tensor(out=zs[:, :, 0:NP], in0=zth[:, :, :], scalar=1.0, in1=two(2),
                                            op0=ALU.add, op1=ALU.mult).then_inc(sem["zth_ready"], 1)
                    dve.wait_ge(sem["xtr_done"], G + 1)
                    for c in range(NC):
                        ch.add(v_.tensor_tensor(split_heads(xw[:, c, :]), split_heads(bank[6 + c][:, :]),
                                                per_head(spx[:, c, bass.ds(g * EH + 4, EH)]), ALU.mult))
                        ch.add(v_.tensor_tensor(split_heads(y[:, c, :]), split_heads(bank[6 + c][:, :]),
                                                per_head(row_all[:, lay, bass.ds(g * EH + 72, EH)]), ALU.mult))
                    ch.wait()
                    dve.wait_ge(sem["cum_exp"], lay + 1)
                    v_.tensor_tensor(split_heads(xwe[:, :]), split_heads(xw[:, 0, :]), per_head(w_end[:, heads]),
                                     ALU.mult).then_inc(sem["xw_ready"], 1)
                    step(7)
                    dve.wait_ge(sem["inter_ready"], G + 1)
                    v_.tensor_tensor(num[:, 1, 0:257], bank[5][:, 0:257], inter[:, 0:257], ALU.add)\
                        .then_inc(sem["num1_ready"], 1)
                    dve.wait_ge(sem["num1_ready"], G + 1)
                    ch.add(v_.scalar_tensor_tensor(out=den[:, :].unsqueeze(2), in0=num[:, :, MV:MV + 1], scalar=-1.0,
                                                   in1=num[:, :, MV:MV + 1], op0=ALU.mult, op1=ALU.max))
                    ch.wait()
                    ch.add(v_.tensor_tensor(den[:, :], den[:, :], gtk[:, 2:4], ALU.max))
                    ch.wait()
                    ch.add(v_.reciprocal(rden[:, :], den[:, :]))
                    dve.wait_ge(sem["nsq_ready"], G + 1)
                    ch.wait()
                    ch.add(v_.tensor_tensor(hvar[:, :], nss[:, :], rden[:, :], ALU.mult))
                    ch.wait()
                    ch.add(v_.tensor_tensor(hvar[:, :], hvar[:, :], rden[:, :], ALU.mult))
                    ch.wait()
                    v_.tensor_scalar(hvar[:, :], hvar[:, :], 1.0 / MV, EPS, ALU.mult, ALU.add).then_inc(sem["hvar_ready"], 1)
                    dve.wait_ge(sem["yi_done"], G + 1)
                    for c in range(NC):
                        ch.add(v_.tensor_tensor(y[:, c, :], y[:, c, :], bank[6 + c][:, :], ALU.add))
                    dve.wait_ge(sem["hrms_ready"], G + 1)
                    ch.add(v_.tensor_tensor(hsc[:, :], hrms[:, :], rden[:, :], ALU.mult))
                    ch.wait()
                    for c in range(NC):
                        i = v_.tensor_scalar(num[:, c, 0:MV], num[:, c, 0:MV], hsc[:, c:c + 1], None, ALU.mult)
                    i.then_inc(sem["hn_ready"], 1)
                    taken(Z1)
                    ch.add(v_.scalar_tensor_tensor(out=zs[:, :, NP:2 * NP], in0=zth[:, :, :], scalar=1.0, in1=two(0),
                                                   op0=ALU.add, op1=ALU.mult))
                    step(8)
                    dve.wait_ge(sem["yx_done"], G + 1)
                    ch.add(v_.tensor_tensor(split_heads(xwe[:, :]), split_heads(bank[4][:, :]),
                                            per_head(eacs[:, heads]), ALU.mult))
                    ch.wait()
                    ch.add(v_.tensor_tensor(y[:, 1, :], y[:, 1, :], xwe[:, :], ALU.add))
                    ch.wait()
                    v_.scalar_tensor_tensor(out=y[:, :, :], in0=y[:, :, :], scalar=0.5, in1=zs[:, :, :],
                                            op0=ALU.mult, op1=ALU.mult).then_inc(sem["y_ready"], 1)
                    taken(O)
                    for t in range(2):
                        ch.add(v_.tensor_scalar(osg[:, t, :], osg[:, t, :], 1.0, ghn[:, t:t + 1], ALU.add, ALU.mult))
                    ch.wait()
                    dve.wait_ge(sem["hnT_done"], G + 1)
                    v_.tensor_tensor(osg[:, :, :], osg[:, :, :], two(3), ALU.mult).then_inc(sem["ha32_ready"], 1)
                    dve.wait_ge(sem["ha_hi_ready"], G + 1)
                    v_.tensor_tensor(ha_lo[:, bass.ds(g * 2, 2), :], osg[:, :, :],
                                     ha_hi[:, bass.ds(g * 2, 2), :].bitcast(F32), ALU.subtract).then_inc(sem["ha_ready"], 1)
                    dve.wait_ge(sem["yfeat_ready"], G + 1)
                    dve.sem_inc(sem["group_free"], 1)
                    ch.clear()

            dve.wait_ge(sem["par_tr"], 1)
            for l in range(DEPTH):
                ch.add(v_.tensor_copy(par_all[:, l, 0:96], bank[4 + l][:, 0:96]))
                ch.add(v_.tensor_copy(par_all[:, l, 96:176], bank[4 + l][:, 128:208]))
            ch.add(v_.tensor_copy(g_fin[:, :], bank[4][:, 256:264]))
            ch.wait()
            for i in range(4):
                dve.wait_ge(sem["xtr_in"], i + 1)
                v_.tensor_copy(h[:, 2 * i:2 * i + 2, :], two(i)).then_inc(sem["h_ready"], 1)
            ch.clear()

            with nc.vector.Fori(0, DEPTH) as lay:
                ch.add(v_.tensor_scalar(par[:, 0:120], par_all[:, lay, 0:120], 0.5, None, ALU.mult))
                ch.add(v_.tensor_copy(par[:, 120:136], par_all[:, lay, 120:136]))
                ch.add(v_.tensor_scalar(par[:, 136:144], par_all[:, lay, 136:144], 0.5, None, ALU.mult))
                ch.add(v_.tensor_copy(par[:, 144:176], par_all[:, lay, 144:176]))
                ch.wait()
                slo(lay, 0)
                slo(lay, 1)
                norm(lay, 0)
                ffn(lay, 0, 0)
                norm(lay, 1)
                small(lay)
                groups(lay)
                for q in range(4):
                    slo(lay, K_GB + q + 2)
                    dve.wait_ge(sem["yb_hi_ready"], lay * 4 + q + 1)
                    v_.tensor_tensor(yb_lo[:, 4 * q:4 * q + 4, :], y_feat[:, 4 * q:4 * q + 4, :],
                                     yb_hi[:, 4 * q:4 * q + 4, :].bitcast(F32), ALU.subtract).then_inc(sem["yb_ready"], 1)
                    if q == 0:
                        dve.wait_ge(sem["ysq_ready"], lay * NG + NG)
                        ch.add(v_.tensor_reduce(var[:, :], y_ss[:, :, :], AX_X, ALU.add))
                        ch.wait()
                        v_.tensor_scalar(var[:, :], var[:, :], 1.0 / SI, EPS, ALU.mult, ALU.add).then_inc(sem["yvar_ready"], 1)
                    if q == 1:
                        dve.wait_ge(sem["yrms_ready"], lay + 1)
                        v_.tensor_scalar(r_col[:, 0, :], ones[:, :], rms[:, 0:1], None, ALU.mult)
                        v_.tensor_scalar(r_col[:, 1, :], ones[:, :], rms[:, 1:2], None, ALU.mult).then_inc(sem["ycol_ready"], 1)
                ch.clear()
                with nc.vector.Fori(0, 4) as m:
                    for r in range(2):
                        k = K_MERGE + r + 2
                        lo(lay, m * 3 + k, k % RING)
                    dve.wait_ge(sem["unit_done"], lay * NU + m * 3 + (K_MERGE + RING + 1))
                    v_.scalar_tensor_tensor(out=mtmp[:, :, :], in0=gate_a[:, bass.ds(m * 2, 2), :], scalar=1.0,
                                            in1=two(0), op0=ALU.add, op1=ALU.mult).then_inc(sem["merge_read"], 1)
                    k = K_MERGE + 4
                    lo(lay, m * 3 + k, k % RING)
                    dve.wait_ge(sem["unit_done"], lay * NU + m * 3 + (K_MERGE + 2 + RING + 1))
                    v_.scalar_tensor_tensor(out=mrg[:, :, :], in0=gate_b[:, bass.ds(m * 2, 2), :], scalar=1.0,
                                            in1=two(1), op0=ALU.add, op1=ALU.mult).then_inc(sem["merge_read"], 1)
                    dve.wait_ge(sem["merge_read"], lay * 8 + m * 2 + 4)
                    dve.wait_ge(sem["yB_ready"], lay + 1)
                    ch.add(v_.tensor_tensor(mrg[:, :, :], mrg[:, :, :],
                                            rB_y[:, :].unsqueeze(1).broadcast_to([P, 2, S]), ALU.mult))
                    ch.wait()
                    v_.tensor_tensor(mrg[:, :, :], mrg[:, :, :], mtmp[:, :, :], ALU.add).then_inc(sem["mrg_ready"], 1)
                    dve.wait_ge(sem["m_hi_ready"], lay * 4 + m + 1)
                    v_.tensor_tensor(u_lo[:, bass.ds(m * 2, 2), :], mrg[:, :, :],
                                     u_hi[:, bass.ds(m * 2, 2), :].bitcast(F32), ALU.subtract).then_inc(sem["m_lo_ready"], 1)
                    ch.clear()
                for q in range(4):
                    slo(lay, K_OUT + q + 2)
                    done(lay, K_OUT + q)
                    v_.scalar_tensor_tensor(out=h[:, 2 * q:2 * q + 2, :], in0=two(q % 3), scalar=0.5,
                                            in1=h[:, 2 * q:2 * q + 2, :], op0=ALU.mult, op1=ALU.add)\
                        .then_inc(sem["h_ready"], 1)
                norm(lay, 2)
                ffn(lay, 1, K_FFN2)
                norm(lay, 3)
                for q in range(4):
                    slo(lay, K_PLE + q + 2)
                    dve.wait_ge(sem["pp_ready"], lay * 4 + 4)
                    dve.wait_ge(sem["ple_tanh"], lay * 4 + q + 1)
                    t = sa if q % 2 == 0 else h1f
                    ch.add(v_.scalar_tensor_tensor(out=t[:, :, :], in0=t[:, :, :], scalar=1.0,
                                                   in1=p_proj[:, 2 * q:2 * q + 2, :], op0=ALU.add, op1=ALU.mult))
                    ch.wait()
                    v_.scalar_tensor_tensor(out=h[:, 2 * q:2 * q + 2, :], in0=t[:, :, :], scalar=0.5,
                                            in1=h[:, 2 * q:2 * q + 2, :], op0=ALU.mult, op1=ALU.add)\
                        .then_inc(sem["h_ready"], 1)
                ch.clear()
            norm(DEPTH, 0, final=True)
            for q in range(4):
                dve.wait_ge(sem["xt_done"], q + 1)
                c = q // 2
                v_.tensor_copy(x_tok[:, c, (q % 2) * 512:(q % 2) * 512 + 512], bank[q][:, :]).then_inc(sem["fin_done"], 1)

        @block.tensor
        def _(pe):
            mm = nc.tensor.matmul

            def weights(lay, k):
                pe.wait_ge(sem["w_lo"], lay * NU + k + (RING + 1))

            def zero_bank(b):
                mm(bank[b][:, :], zeros[:, :], zeros[:, :].unsqueeze(1).broadcast_to([P, 4, P]), start=True,
                   stop=False, skip_group_check=True)

            def feat(slot, b, xh, xl, seeded=False):
                for m in range(2):
                    o = bank[b][:, m * S:(m + 1) * S]
                    cs = slice(m * P, (m + 1) * P)
                    for k in range(KD):
                        for q, (w, x) in enumerate(((whi, xh), (whi, xl), (wlo, xh))):
                            i = mm(o, w[slot][:, k, cs], x[:, k, :], start=(k + q == 0 and not seeded),
                                   stop=(k == KD - 1 and q == 2 and not seeded), skip_group_check=seeded)
                i.then_inc(sem["unit_done"], 1)

            def tok(slot, b, xh, xl):
                for c in range(NC):
                    o = bank[b][:, c * NP:(c + 1) * NP]
                    cs = slice(c * P, (c + 1) * P)
                    for k in range(KD):
                        mm(o, xh[:, k, cs], whi[slot][:, k, :], start=(k == 0), stop=False)
                        mm(o, xh[:, k, cs], wlo[slot][:, k, :], start=False, stop=False)
                        i = mm(o, xl[:, k, cs], whi[slot][:, k, :], start=False, stop=(k == KD - 1))
                i.then_inc(sem["unit_done"], 1)

            def norm(lay, n):
                N = lay * 4 + n
                for i in range(4):
                    pe.wait_ge(sem["sq_ready"], N * 4 + (i + 1))
                    for k in (2 * i, 2 * i + 1):
                        for c in range(NC):
                            ins = mm(bank[6 + c][:, 0:1], u32[:, k, c * P:(c + 1) * P], ones[:, 0:1],
                                     start=(k == 0), stop=(k == KD - 1))
                ins.then_inc(sem["ss_done"], 1)

            def norm_rows(lay, n):
                N = lay * 4 + n
                pe.wait_ge(sem["rcol_ready"], N + 1)
                for c in range(NC):
                    ins = mm(bank[6][:, S + c * P:S + (c + 1) * P], r_col[:, c, :], ident[:, :], start=True, stop=True)
                ins.then_inc(sem["rB_done"], 1)

            def ffn(lay, f, k0):
                F = lay * 2 + f
                s = [(k0 + r) % RING for r in range(3)]
                for b in range(4):
                    zero_bank(b)

                def down(slot):
                    w = [x[slot][:, :, :].rearrange("p a b -> p (a b)").rearrange("p (k m) -> p k m", k=2)
                         for x in (whi, wlo)]
                    for m in range(KD):
                        o = bank[m // 2][:, (m % 2) * S:(m % 2 + 1) * S]
                        cs = slice(m * P, (m + 1) * P)
                        for kk in range(2):
                            for ww, xx in ((w[0], h1_hi), (w[0], h1_lo), (w[1], h1_hi)):
                                i = mm(o, ww[:, kk, cs], xx[:, kk, :], start=False, stop=False, skip_group_check=True)
                    i.then_inc(sem["unit_done"], 1)

                pe.wait_ge(sem["u_lo_ready"], (lay * 4 + 2 * f + 1) * KD)
                weights(lay, k0)
                feat(s[0], 4, u_hi, u_lo)
                weights(lay, k0 + 1)
                feat(s[1], 5, u_hi, u_lo)
                with nc.tensor.Fori(0, FT - 1) as j:
                    weights(lay, j * 3 + (k0 + 2))
                    pe.wait_ge(sem["silu_done"], F * FT + j + 1)
                    feat(s[2], 4, u_hi, u_lo)
                    weights(lay, j * 3 + (k0 + 3))
                    pe.wait_ge(sem["h1_ready"], F * FT + j + 1)
                    down(s[0])
                    weights(lay, j * 3 + (k0 + 4))
                    feat(s[1], 5, u_hi, u_lo)
                weights(lay, k0 + U_FFN - 1)
                pe.wait_ge(sem["h1_ready"], (F + 1) * FT)
                down(s[2])

            def small(lay):
                pe.wait_ge(sem["u_lo_ready"], (lay * 4 + 2) * KD)
                pe.wait_ge(sem["wsm_loaded"], lay * 32 + 32)
                for c in range(NC):
                    for k in range(KD):
                        for q, xx in enumerate((u_hi, u_lo)):
                            i = mm(bank[7][:, c * 40:(c + 1) * 40], xx[:, k, c * P:(c + 1) * P].bitcast(F32),
                                   wsm[:, k, :], start=(k == 0 and q == 0), stop=(k == KD - 1 and q == 1))
                i.then_inc(sem["small_done"], 1)

            def gates(lay):
                pe.wait_ge(sem["dA_ready"], lay + 1)
                mm(bank[7][:, 0:SH], tri_le[:, :], dA[:, 1, :], start=True, stop=True)
                mm(bank[7][:, SH:2 * SH], tri_gt[:, :], dA[:, 0, :], start=True, stop=True).then_inc(sem["cum_done"], 1)
                for c in range(NC):
                    nc.tensor.transpose(bank[6][0:MH, c * P:(c + 1) * P], pre[:, c, 0:MH], ident[:, :])
                    i = nc.tensor.transpose(bank[6][0:MH, S + c * P:S + (c + 1) * P], spx[:, c, 0:MH], ident[:, :])
                i.then_inc(sem["row_tr"], 1)

            def gates_back(lay):
                pe.wait_ge(sem["row_ready"], lay + 1)
                for r in range(6):
                    i = mm(bank[6][:, r * MH:(r + 1) * MH], r_x[:, r, :], ident[0:MH, 0:MH], start=True, stop=True)
                i.then_inc(sem["row_back"], 1)

            def groups(lay):
                with nc.tensor.Fori(0, NG) as g:
                    G = pe.snap(lay * NG + g)

                    def unit(p, kind):
                        weights(lay, g * GU + (K_MIX + p))
                        pe.wait_ge(sem["act_evac"], lay * NE + g * GU + (p + 1))
                        kind((K_MIX + p) % RING, p % 3, u_hi, u_lo)

                    def evac(p):
                        pe.wait_ge(sem["act_evac"], lay * NE + g * GU + (p + RING + 1))

                    def segments(c):
                        for b in range(2):
                            pe.wait_ge(sem["r_built"], G * 4 + (2 * c + b + 1))
                            mm(bank[4 + 2 * c + b][:, :], tri_gt[:, :], R[:, b, :, :], start=True, stop=True)\
                                .then_inc(sem["seg_done"], 1)

                    unit(BC, feat)
                    unit(QK, feat)
                    segments(0)
                    unit(X01, feat)
                    segments(1)
                    evac(QK)
                    pe.wait_ge(sem["exp_done"], G * 4 + 2)
                    for c in range(NC):
                        cs = slice(c * P, (c + 1) * P)
                        mm(bank[3][:, cs], kT[:, cs], qT[:, cs], start=True, stop=True)
                    nc.tensor.transpose(bank[3][:, 256:384], kT[:, 0:P], ident[:, :])
                    mm(bank[4][:, 0:S], ones[0:MH, :], M4[:, bass.ds(g, 1), :].rearrange("p a b -> p (a b)"),
                       start=True, stop=True).then_inc(sem["scores_done"], 1)
                    unit(X23, feat)
                    pe.wait_ge(sem["cv_ready"], G * 3 + 1)
                    for c in range(NC):
                        cs = slice(c * P, (c + 1) * P)
                        mm(bank[5][:, cs], bcv[:, 0, cs], bcv[:, 1, cs], start=True, stop=True)
                    nc.tensor.transpose(bank[5][:, 256:384], bcv[:, 0, 0:P], ident[:, :]).then_inc(sem["cb_done"], 1)
                    unit(V, tok)
                    unit(Z0, tok)
                    pe.wait_ge(sem["sct_ready"], G + 1)
                    evac(V)
                    mm(bank[3][:, 0:257], ktok[:, :], vtok[:, 0, 0:257], start=True, stop=True)
                    mm(bank[4][:, 0:257], scT[:, 0, :], vtok[:, 0, 0:257], start=True, stop=True)
                    pe.wait_ge(sem["btok_ready"], G + 1)
                    mm(bank[5][:, 0:257], scT[:, 1, :], vtok[:, 1, 0:257], start=True, stop=True)\
                        .then_inc(sem["heads_done"], 1)
                    pe.wait_ge(sem["cv_ready"], G * 3 + 3)
                    pe.wait_ge(sem["exp_done"], G * 4 + 4)
                    for c in range(NC):
                        for t in range(4):
                            i = nc.tensor.transpose(bank[6 + c][:, t * P:(t + 1) * P], xcv[:, t, c * P:(c + 1) * P],
                                                    ident[:, :])
                    i.then_inc(sem["xtr_done"], 1)
                    unit(Z1, tok)
                    pe.wait_ge(sem["cst_ready"], G + 1)
                    mm(bank[3][:, 0:257], qT[:, P:2 * P], cst[:, 0:257], start=True, stop=True).then_inc(sem["im_done"], 1)
                    pe.wait_ge(sem["m_ready"], G * 2 + 2)
                    pe.wait_ge(sem["xw_ready"], G + 1)
                    pe.wait_ge(sem["num0_ready"], G + 1)
                    for c in range(NC):
                        for e in range(EH):
                            es = slice(e * HP, (e + 1) * HP)
                            mm(bank[6 + c][:, es], seg[:, c, e, :], xw[:, c, es], start=True, stop=True)
                    mm(bank[4][:, :], btok[:, :], xwe[:, :], start=True, stop=True).then_inc(sem["yi_done"], 1)
                    unit(O, feat)
                    pe.wait_ge(sem["st_ready"], G + 1)
                    mm(bank[4][:, :], bcv[:, 1, P:2 * P], st[:, :], start=True, stop=True).then_inc(sem["yx_done"], 1)
                    pe.wait_ge(sem["hn_ready"], G + 1)
                    for t in range(2):
                        for c in range(NC):
                            i = nc.tensor.transpose(bank[3][:, t * S + c * P:t * S + (c + 1) * P],
                                                    num[:, c, t * P:(t + 1) * P], ident[:, :])
                    i.then_inc(sem["hnT_done"], 1)
                    unit(GA, feat)
                    pe.wait_ge(sem["y_ready"], G + 1)
                    for c in range(NC):
                        for t in range(4):
                            i = nc.tensor.transpose(bank[6 + c][:, t * P:(t + 1) * P], y[:, c, t * P:(t + 1) * P],
                                                    ident[:, :])
                    i.then_inc(sem["yT_done"], 1)

            pe.wait_ge(sem["const_ready"], 2)
            pe.wait_ge(sem["par_loaded"], 16 * 9)
            for l in range(DEPTH):
                nc.tensor.transpose(bank[4 + l][:, 0:96], par_rows[0:96, l, 0, :], ident[0:96, 0:96])
                nc.tensor.transpose(bank[4 + l][:, 128:208], par_rows[0:80, l, 1, :], ident[0:80, 0:80])
            nc.tensor.transpose(bank[4][:, 256:264], gf_row[:, :], ident[0:KD, 0:KD]).then_inc(sem["par_tr"], 1)
            pe.wait_ge(sem["in_loaded"], 16)
            for i in range(4):
                for q in range(2):
                    for c in range(NC):
                        ins = nc.tensor.transpose(bank[i][:, q * S + c * P:q * S + (c + 1) * P],
                                                  x_tok[:, c, (2 * i + q) * P:(2 * i + q + 1) * P], ident[:, :])
                ins.then_inc(sem["xtr_in"], 1)

            with nc.tensor.Fori(0, DEPTH) as lay:
                norm(lay, 0)
                norm_rows(lay, 0)
                ffn(lay, 0, 0)
                norm(lay, 1)
                norm_rows(lay, 1)
                small(lay)
                gates(lay)
                gates_back(lay)
                groups(lay)
                for q in range(4):
                    weights(lay, K_GB + q)
                    pe.wait_ge(sem["act_evac"], lay * NE + (NG * GU + q + 1))
                    feat((K_GB + q) % RING, q % 3, u_hi, u_lo)
                pe.wait_ge(sem["ycol_ready"], lay + 1)
                for c in range(NC):
                    i = mm(bank[7][:, c * P:(c + 1) * P], r_col[:, c, :], ident[:, :], start=True, stop=True)
                i.then_inc(sem["yB_done"], 1)
                with nc.tensor.Fori(0, 4) as m:
                    pe.wait_ge(sem["ha_ready"], lay * NG + NG)
                    pe.wait_ge(sem["yB_ready"], lay + 1)
                    weights(lay, m * 3 + K_MERGE)
                    pe.wait_ge(sem["merge_read"], lay * 8 + m * 2 + 1)
                    feat(K_MERGE % RING, 0, ha_hi, ha_lo)
                    pe.wait_ge(sem["yb_ready"], lay * 4 + 4)
                    pe.wait_ge(sem["merge_read"], lay * 8 + m * 2 + 2)
                    zero_bank(1)
                    for kh in range(2):
                        weights(lay, m * 3 + (K_MERGE + 1 + kh))
                        feat((K_MERGE + 1 + kh) % RING, 1, yb_hi[:, kh * KD:(kh + 1) * KD, :],
                             yb_lo[:, kh * KD:(kh + 1) * KD, :], seeded=True)
                for q in range(4):
                    weights(lay, K_OUT + q)
                    if q == 0:
                        pe.wait_ge(sem["m_lo_ready"], lay * 4 + 4)
                    if q == 3:
                        pe.wait_ge(sem["h_ready"], lay * 16 + 9)
                    feat((K_OUT + q) % RING, q % 3, u_hi, u_lo)
                pe.wait_ge(sem["p_loaded"], lay * 32 + 32)
                for k in range(2):
                    for c in range(NC):
                        i = nc.tensor.transpose(bank[3][:, k * S + c * P:k * S + (c + 1) * P],
                                                p_tok[:, c, k * P:(k + 1) * P], ident[:, :])
                i.then_inc(sem["pt_done"], 1)

                def p_project(q):
                    for m in (2 * q, 2 * q + 1):
                        for k in range(2):
                            i = mm(bank[4 + q % 2][:, (m % 2) * S:(m % 2 + 1) * S], w_ple[:, k, m * P:(m + 1) * P],
                                   p_feat[:, k, :], start=(k == 0), stop=(k == 1))
                    i.then_inc(sem["pp_done"], 1)

                pe.wait_ge(sem["pt_ready"], lay + 1)
                p_project(0)
                p_project(1)
                norm(lay, 2)
                for q in (2, 3):
                    pe.wait_ge(sem["pp_ready"], lay * 4 + q - 1)
                    p_project(q)
                norm_rows(lay, 2)
                ffn(lay, 1, K_FFN2)
                norm(lay, 3)
                norm_rows(lay, 3)
                pe.wait_ge(sem["u_lo_ready"], (lay * 4 + 4) * KD)
                for q in range(4):
                    weights(lay, K_PLE + q)
                    if q == 3:
                        pe.wait_ge(sem["ple_tanh"], lay * 4 + 1)
                    feat((K_PLE + q) % RING, q % 3, u_hi, u_lo)
            norm(DEPTH, 0)
            norm_rows(DEPTH, 0)
            pe.wait_ge(sem["u32_ready"], (DEPTH * 4 + 1) * KD)
            for q in range(4):
                c = q // 2
                for t in range(4):
                    k = (q % 2) * 4 + t
                    i = nc.tensor.transpose(bank[q][:, t * P:(t + 1) * P], u32[:, k, c * P:(c + 1) * P], ident[:, :])
                i.then_inc(sem["xt_done"], 1)


_INS = ["x", "p", "g_ffn1", "w1_ffn1", "w3_ffn1", "w2_ffn1", "g_mix", "w_in", "b_igate", "b_fgate", "g_mlstm_head",
        "conv_w", "conv_b", "dt_bias", "a_log", "d_skip", "g_ssm_out", "w_branch_a", "w_branch_b", "w_out", "g_ffn2",
        "w1_ffn2", "w3_ffn2", "w2_ffn2", "g_ple", "w_ple_gate", "w_ple", "g_final"]


def kernel(**inputs):
    import numpy as _np
    import concourse.bacc as _bacc
    from concourse import mybir as _mybir
    from concourse.bass_utils import run_bass_kernel_spmd as _run

    nc = _bacc.Bacc("TRN2", target_bir_lowering=False, num_devices=1)
    arrays, tensors = {}, {}
    for name in _INS:
        a = _np.ascontiguousarray(inputs[name])
        arrays[f"in_{name}_dram"] = a
        tensors[name] = nc.dram_tensor(f"in_{name}_dram", a.shape, _mybir.dt.from_np(a.dtype),
                                       kind="ExternalInput").ap()
    out = nc.dram_tensor("out_0_dram", inputs["x"].shape, _mybir.dt.float32, kind="ExternalOutput").ap()
    trunk(nc, tensors, out)
    r = _run(nc, [arrays], core_ids=[0])
    return r.results[0]["out_0_dram"]
```

```python
from contextlib import ExitStack

import concourse.bass as bass
from concourse import mybir

F32 = mybir.dt.float32
F32R = mybir.dt.float32r
BF16 = mybir.dt.bfloat16
ALU = mybir.AluOpType
ACT = mybir.ActivationFunctionType
AX_X = mybir.AxisListType.X

P = 128
EPS = 1e-6
RING = 3


def trunk(nc, T, out):
    DEPTH, D, FF = T["w1_ffn1"].shape
    S = T["x"].shape[1]
    CH = 128
    NC = S // CH
    D_IN = T["w_in"].shape[2]
    MH = T["b_igate"].shape[1]
    MV = T["g_mlstm_head"].shape[2]
    MQK = 128
    SH = T["dt_bias"].shape[1]
    SI = T["g_ssm_out"].shape[1]
    HP = SI // SH
    SCONV, CDIM = T["conv_w"].shape[1:]
    NG = 4
    EH = SH // NG
    PLE = T["p"].shape[3]
    KD = D // P
    NP = 2 * P
    FT = FF // NP
    assert NC == 2 and MH == NG and MV == 2 * P and EH * HP == 4 * P and PLE == 2 * P and S == NP
    assert D_IN == 2 * MH * MQK + 2 * MH * MV + 2 * MH + SI + CDIM + SH + 2 * D

    C_Q, C_K = 0, MH * MQK
    C_V = 2 * MH * MQK
    C_O = C_V + MH * MV
    C_IF = C_O + MH * MV
    C_Z = C_IF + 2 * MH
    C_X = C_Z + SI
    C_B = C_X + SI
    C_C = C_B + NG * P
    C_DT = C_X + CDIM
    C_G = C_DT + SH

    U_FFN = 3 * FT
    GU = 9
    BC, QK, X01, X23, V, Z0, Z1, O, GA = range(GU)
    K_MIX = U_FFN
    K_GB = K_MIX + NG * GU
    K_MERGE = K_GB + 4
    K_OUT = K_MERGE + 12
    K_FFN2 = K_OUT + 4
    K_PLE = K_FFN2 + U_FFN
    NU = K_PLE + 4
    NE = NG * GU + 4
    assert NU % RING == 0 and GU % RING == 0

    ctx = ExitStack()
    with ctx:
        top = [nc.sbuf_base + 64 if isinstance(nc.sbuf_base, int) else 1024]
        top[0] = (top[0] + 63) // 64 * 64

        def at(name, shape, dt, off):
            n = 1
            for d in shape[1:]:
                n *= d
            n *= 2 if dt == BF16 else 4
            return nc.alloc_sbuf_tensor_at(name, shape, dt, offset=off), off + (n + 31) // 32 * 32

        def sb(name, shape, dt=F32):
            t, top[0] = at(name, shape, dt, top[0])
            return t

        raw = [sb(f"w_raw{i}", [P, KD, NP]) for i in range(RING)]
        whi = [sb(f"w_hi{i}", [P, KD, NP], F32R) for i in range(RING)]
        wlo = [sb(f"w_lo{i}", [P, KD, NP], F32R) for i in range(RING)]
        h = sb("h", [P, KD, S])
        u_hi = sb("u_hi", [P, KD, S], F32R)
        u_lo = sb("u_lo", [P, KD, S], F32R)
        gate_a = sb("gate_a", [P, KD, S])
        ha_hi = sb("ha_hi", [P, 2 * MH, S], F32R)
        ha_lo = sb("ha_lo", [P, 2 * MH, S], F32R)
        y_feat = sb("y_feat", [P, SI // P, S])
        w_ple = y_feat[:, 0:8, :].rearrange("p a b -> p (a b)").rearrange("p (k m) -> p k m", k=2)
        p_proj = y_feat[:, 8:16, :]
        p_tok = gate_a[:, 0:2, :]
        p_feat = gate_a[:, 2:4, :]

        ident = sb("ident", [P, P])
        tri_le = sb("tri_le", [P, P])
        tri_gt = sb("tri_gt", [P, P])
        ones = sb("ones", [P, P])
        zeros = sb("zeros", [P, P], BF16)
        m_half = sb("m_half", [P, 1])
        par_all = sb("par_all", [P, DEPTH, 176])
        par = sb("par", [P, 176])
        g_fin = sb("g_fin", [P, KD])
        row_all = sb("row_all", [P, DEPTH, 104])
        wsm = sb("wsm", [P, KD, 40])
        pre = sb("pre", [P, NC, 40])
        spx = sb("spx", [P, NC, 36])
        sp_a = sb("sp_a", [P, NC, 36])
        sp_b = sb("sp_b", [P, NC, 36])
        sp_c = sb("sp_c", [P, NC, 36])
        dA = sb("dA", [P, NC, SH])
        e_a = sb("e_a", [P, SH])
        dcol = sb("dcol", [P, DEPTH, SI // P])
        w_end = sb("w_end", [P, SH])
        tokc = sb("tokc", [P, 6, MH])
        M4 = sb("M4", [MH, MH, S])
        gcw = sb("gcw", [P, SCONV, 6])
        gcb = sb("gcb", [P, 6])
        gdk = sb("gdk", [P, 4])
        ghn = sb("ghn", [P, 2])
        gtk = sb("gtk", [P, 6])
        var = sb("var", [P, NC])
        rms = sb("rms", [P, NC])
        mdiag = sb("mdiag", [P, NC, P])
        rdiag = sb("rdiag", [P, NC, P])
        rB_y = sb("rB_y", [P, S])
        den = sb("den", [P, 2])
        rden = sb("rden", [P, 2])
        nss = sb("nss", [P, 2])
        hvar = sb("hvar", [P, 2])
        hrms = sb("hrms", [P, 2])
        hsc = sb("hsc", [P, 2])

        base = top[0]
        a = base
        seg, a = at("seg", [P, NC, EH, P], F32, a)
        xcv, a = at("xcv", [P, 4, S], F32, a)
        bcv, a = at("bcv", [P, 2, S], F32, a)
        R, _ = at("R", [P, 2, 4, P], F32, a)
        cs, a = at("cs", [P, EH, P], F32, a)
        qT, a = at("qT", [P, S], F32, a)
        kT, a = at("kT", [P, S], F32, a)
        pm, a = at("pm", [P, NC, P], F32, a)
        scT, a = at("scT", [P, NC, P], F32, a)
        cth, a = at("cth", [P, 2, S], F32, a)
        late = a
        xw, a = at("xw", [P, NC, EH * HP], F32, a)
        xwe, a = at("xwe", [P, EH * HP], F32, a)
        zs, a = at("zs", [P, 4, S], F32, a)
        num, a = at("num", [P, NC, 258], F32, a)
        osg, a = at("osg", [P, 2, S], F32, a)
        late_end = a
        st, a = at("st", [P, EH * HP], F32, a)
        xin, a = at("xin", [P, 2, 2, S + 3], F32, a)
        zth, a = at("zth", [P, 2, S], F32, a)
        vtok, a = at("vtok", [P, NC, 258], F32, a)
        ktok, a = at("ktok", [P, P], F32, a)
        cst, a = at("cst", [P, 258], F32, a)
        inter = cst
        cbm, a = at("cbm", [P, NC, P], F32, a)
        btok, a = at("btok", [P, P], F32, a)
        ysum, a = at("ysum", [P, 4, S], F32, a)
        a2 = base
        yb_hi, a2 = at("yb_hi", [P, SI // P, S], F32R, a2)
        yb_lo, a2 = at("yb_lo", [P, SI // P, S], F32R, a2)
        gate_b, a2 = at("gate_b", [P, KD, S], F32, a2)
        mtmp, a2 = at("mtmp", [P, 2, S], F32, a2)
        mrg, a2 = at("mrg", [P, 2, S], F32, a2)
        a3 = base
        u32, a3 = at("u32", [P, KD, S], F32, a3)
        sa, a3 = at("sa", [P, 2, S], F32, a3)
        h1f, a3 = at("h1f", [P, 2, S], F32, a3)
        h1_hi, a3 = at("h1_hi", [P, 2, S], F32R, a3)
        h1_lo, a3 = at("h1_lo", [P, 2, S], F32R, a3)
        x_tok, a3 = at("x_tok", [P, NC, D], F32, a3)
        a4 = base + 4 * KD * S
        par_rows, a4 = at("par_rows", [P, DEPTH, 2, P], F32, a4)
        row_one, a4 = at("row_one", [1, DEPTH, 104], F32, a4)
        gf_row, a4 = at("gf_row", [KD, P], F32, a4)
        a5 = late
        wsm_hi, a5 = at("wsm_hi", [P, KD, 40], F32R, a5)
        wsm_lo, a5 = at("wsm_lo", [P, KD, 40], F32R, a5)
        pre_row, a5 = at("pre_row", [40, S], F32, a5)
        r_i, a5 = at("r_i", [MH, S], F32, a5)
        r_f, a5 = at("r_f", [MH, S], F32, a5)
        r_b, a5 = at("r_b", [MH, S], F32, a5)
        r_w, a5 = at("r_w", [MH, S], F32, a5)
        r_m, a5 = at("r_m", [MH, S], F32, a5)
        r_x, a5 = at("r_x", [MH, 6, P], F32, a5)
        assert a5 <= late_end
        m_start = sb("m_start", [MH, 1])
        top_all = max(a, a2, a3, a4, a5)
        assert top_all <= nc.sbuf_usable_end

        bank = [ctx.enter_context(nc.psum_tensor(f"bank{i}", [P, 512], F32)) for i in range(8)]

        def two(b):
            return bank[b][:, :].rearrange("p (m s) -> p m s", m=2)

        names = """rdiag_ready rB_done ydiag_ready yB_done yB_ready wsm_hi_ready wsm_ready pre_row_ready pre_ready down_done acs_done acs_exp cs_ready y_done ysum_ready
            gtk_ready w_raw0 w_raw1 w_raw2 w_hi w_lo unit_done act_evac const_ready in_loaded par_loaded
            wsm_loaded p_loaded out_stored rows_done par_tr h_ready sq_ready ss_done var_ready rms_ready
            u32_ready u_hi_ready u_lo_ready silu_done prod_done h1_hi_ready h1_ready small_done x_abs sp_exp
            dA_ready ea_ready cum_done cum_exp row_tr row_ready row_back tok_ready r_built seg_done exp_done
            conv_done tanh_done cv_ready scores_done d_ready p_exp pm_ready sct_ready cb_done cbm_done
            btok_ready m_ready xtr_done xw_ready heads_done cst_ready num0_ready yi_done im_done st_ready
            inter_ready num1_ready nsq_ready hvar_ready hrms_ready hn_ready hnT_done y_ready zth_ready
            ha32_ready ha_hi_ready ha_ready group_ready group_free ysq_ready yb_hi_ready yb_ready yss_done
            yvar_ready yrms_ready merge_read mrg_ready m_hi_ready m_lo_ready ple_tanh pt_done pt_ready pp_done
            pp_ready xt_done fin_done row_bcast dve_chain pool_chain xtr_in""".split()
        sem = {n: ctx.enter_context(nc.semaphore(n)) for n in names}
        w_raw = [sem["w_raw0"], sem["w_raw1"], sem["w_raw2"]]
        block = ctx.enter_context(nc.Block())

        class Chain:

            def __init__(self, eng, s):
                self.eng, self.s, self.n = eng, s, 0

            def add(self, ins):
                ins.then_inc(self.s, 1)
                self.n += 1

            def wait(self):
                if self.n:
                    self.eng.wait_ge(self.s, self.n)

            def clear(self):
                if self.n:
                    self.eng.wait_ge(self.s, self.n)
                    self.eng.sem_clear(self.s)
                self.n = 0

        @block.sync
        def _(sp):
            def load(k, slot, src, dst, lay):
                sp.wait_ge(sem["w_lo"], lay * NU + k + 1)
                n = src.shape[1] // 2
                sp.dma_start(dst[:, 0:n], src[:, 0:n]).then_inc(w_raw[slot], 16)
                sp.dma_start(dst[:, n:], src[:, n:]).then_inc(w_raw[slot], 16)

            def cols(w, lay, c0, slot):
                src = w[lay].rearrange("(k p) m -> p k m", p=P)[:, :, c0:c0 + NP]
                return src, raw[slot][:, :, :]

            def dcols(w, lay, c0, slot):
                src = w[lay].rearrange("(k p) m -> p k m", p=P)[:, :, bass.ds(c0, NP)]
                return src, raw[slot][:, :, :]

            def rows2(w, lay, j, slot):
                src = w[lay, bass.ds(j * NP, NP), :].rearrange("(k p) m -> p k m", p=P)
                return src, raw[slot][:, :, :].rearrange("p a b -> p (a b)").rearrange("p (k m) -> p k m", k=2)

            def ffn(k0, w1, w3, w2, lay):
                s = k0 % RING
                load(k0, s, *cols(w1, lay, 0, s), lay)
                s = (k0 + 1) % RING
                load(k0 + 1, s, *cols(w3, lay, 0, s), lay)
                with nc.sync.Fori(0, FT - 1) as j:
                    a, b, c = [(k0 + 2 + r) % RING for r in range(3)]
                    load(k0 + 2 + j * 3, a, *dcols(w1, lay, (j + 1) * NP, a), lay)
                    load(k0 + 3 + j * 3, b, *rows2(w2, lay, j, b), lay)
                    load(k0 + 4 + j * 3, c, *dcols(w3, lay, (j + 1) * NP, c), lay)
                s = (k0 + U_FFN - 1) % RING
                load(k0 + U_FFN - 1, s, *rows2(w2, lay, FT - 1, s), lay)

            W = T["w_in"]
            with nc.sync.Fori(0, DEPTH) as lay:
                ffn(0, T["w1_ffn1"], T["w3_ffn1"], T["w2_ffn1"], lay)
                with nc.sync.Fori(0, NG) as g:
                    def two_cols(p, ca):
                        s = (K_MIX + p) % RING
                        wv = W[lay].rearrange("(k p) m -> p k m", p=P)
                        sp.wait_ge(sem["w_lo"], lay * NU + g * GU + (K_MIX + p + 1))
                        sp.dma_start(raw[s][:, :, 0:P], wv[:, :, bass.ds(ca, P)]).then_inc(w_raw[s], 16)
                        sp.dma_start(raw[s][:, :, P:NP], wv[:, :, bass.ds(ca + NG * P, P)]).then_inc(w_raw[s], 16)

                    def one(p, c):
                        s = (K_MIX + p) % RING
                        load(K_MIX + g * GU + p, s, *dcols(W, lay, c, s), lay)

                    two_cols(BC, g * P + C_B)
                    two_cols(QK, g * P + C_Q)
                    one(X01, g * (4 * P) + C_X)
                    one(X23, g * (4 * P) + C_X + NP)
                    one(V, g * NP + C_V)
                    one(Z0, g * (4 * P) + C_Z)
                    one(Z1, g * (4 * P) + C_Z + NP)
                    one(O, g * NP + C_O)
                    one(GA, g * NP + C_G)
                for i in range(4):
                    s = (K_GB + i) % RING
                    load(K_GB + i, s, *cols(W, lay, C_G + D + i * NP, s), lay)
                with nc.sync.Fori(0, 4) as m:
                    s = K_MERGE % RING
                    load(K_MERGE + m * 3, s, *dcols(T["w_branch_a"], lay, m * NP, s), lay)
                    for kh in range(2):
                        s = (K_MERGE + 1 + kh) % RING
                        src = T["w_branch_b"][lay, kh * D:(kh + 1) * D, :].rearrange("(k p) m -> p k m", p=P)
                        load(K_MERGE + 1 + kh + m * 3, s, src[:, :, bass.ds(m * NP, NP)], raw[s][:, :, :], lay)
                for i in range(4):
                    s = (K_OUT + i) % RING
                    load(K_OUT + i, s, *cols(T["w_out"], lay, i * NP, s), lay)
                ffn(K_FFN2, T["w1_ffn2"], T["w3_ffn2"], T["w2_ffn2"], lay)
                for i in range(4):
                    s = (K_PLE + i) % RING
                    load(K_PLE + i, s, *cols(T["w_ple_gate"], lay, i * NP, s), lay)
            sp.wait_ge(sem["fin_done"], 4)
            sp.dma_start(out[0].rearrange("(c t) d -> t c d", t=P), x_tok[:, :, :]).then_inc(sem["out_stored"], 16)
            sp.wait_ge(sem["out_stored"], 16)

        @block.gpsimd
        def _(pool):
            g_ = nc.gpsimd
            ch = Chain(pool, sem["pool_chain"])
            ch.add(g_.memset(ident[:, :], 0.0))
            ch.add(g_.memset(ones[:, :], 1.0))
            ch.add(g_.memset(m_half[:, :], -0.5))
            ch.wait()
            ch.add(g_.affine_select(out=ident[:, :], in_=ident[:, :], compare_op=ALU.not_equal, fill=1.0,
                                    base=0, pattern=[[-1, P]], channel_multiplier=1))
            ch.add(g_.affine_select(out=tri_le[:, :], in_=ones[:, :], compare_op=ALU.is_ge, fill=0.0,
                                    base=0, pattern=[[1, P]], channel_multiplier=-1))
            g_.affine_select(out=tri_gt[:, :], in_=ones[:, :], compare_op=ALU.is_gt, fill=0.0,
                             base=0, pattern=[[-1, P]], channel_multiplier=1).then_inc(sem["const_ready"], 1)
            pool.wait_ge(sem["rows_done"], 16 * 5)
            g_.partition_broadcast(row_all[:, :, :].rearrange("p a b -> p (a b)"),
                                   row_one[0:1, :, :].rearrange("p a b -> p (a b)")).then_inc(sem["row_bcast"], 1)
            ch.add(g_.memset(ysum[:, :, :], 0.0))
            ch.clear()

            def power(n, ready, src, done, dst):
                pool.wait_ge(sem[ready], n)
                g_.tensor_tensor(dst, src, m_half[:, :].broadcast_to([P, dst.shape[1]]), ALU.pow).then_inc(sem[done], 1)

            def row_norm(n):
                power(n, "var_ready", var[:, :], "rms_ready", rms[:, :])

            with nc.gpsimd.Fori(0, DEPTH) as lay:
                row_norm(lay * 4 + 1)
                row_norm(lay * 4 + 2)
                with nc.gpsimd.Fori(0, NG) as g:
                    G = pool.snap(lay * NG + g)
                    pool.wait_ge(sem["group_free"], G + 1)
                    cw = par[:, 0:SCONV * 24].rearrange("p (j t) -> p j t", j=SCONV)
                    g_.tensor_copy(gcw[:, :, 2:6], cw[:, :, bass.ds(g * 4, 4)])
                    for b in range(2):
                        g_.tensor_copy(gcw[:, :, b:b + 1], cw[:, :, bass.ds(g + 16 + 4 * b, 1)])
                        g_.tensor_copy(gcb[:, b:b + 1], par[:, bass.ds(g + 96 + 16 + 4 * b, 1)])
                    g_.tensor_copy(gcb[:, 2:6], par[:, bass.ds(g * 4 + 96, 4)])
                    g_.tensor_copy(gdk[:, :], dcol[:, lay, bass.ds(g * 4, 4)])
                    g_.tensor_copy(ghn[:, :], par[:, bass.ds(g * 2 + 136, 2)]).then_inc(sem["group_ready"], 1)
                    for c in range(NC):
                        for b in range(2):
                            if c == b == 0:
                                pool.wait_ge(sem["dA_ready"], lay + 1)
                            pool.wait_ge(sem["seg_done"], G * 4 + (2 * c + b + 1))
                            g_.tensor_tensor(
                                R[:, b, :, :], tri_le[:, :].unsqueeze(1).broadcast_to([P, 4, P]),
                                dA[:, c, bass.ds(g * EH + 4 * b, 4)].unsqueeze(2).broadcast_to([P, 4, P]),
                                ALU.mult).then_inc(sem["r_built"], 1)
                    pool.wait_ge(sem["tok_ready"], lay * 2 + 2)
                    g_.tensor_copy(gtk[:, :].unsqueeze(2), tokc[:, :, bass.ds(g, 1)]).then_inc(sem["gtk_ready"], 1)
                    pool.wait_ge(sem["p_exp"], G + 1)
                    g_.tensor_tensor(pm[:, :, :], pm[:, :, :], tri_le[:, :].unsqueeze(1).broadcast_to([P, NC, P]),
                                     ALU.mult).then_inc(sem["pm_ready"], 1)
                    power(G + 1, "hvar_ready", hvar[:, :], "hrms_ready", hrms[:, :])
                    pool.wait_ge(sem["ysq_ready"], G + 1)
                    g_.tensor_tensor(ysum[:, :, :], ysum[:, :, :], zs[:, :, :], ALU.add).then_inc(sem["ysum_ready"], 1)
                power(lay + 1, "yvar_ready", var[:, :], "yrms_ready", rms[:, :])
                row_norm(lay * 4 + 3)
                g_.memset(ysum[:, :, :], 0.0)
                row_norm(lay * 4 + 4)
            row_norm(DEPTH * 4 + 1)

        @block.scalar
        def _(act):
            a_ = nc.scalar
            act.dma_start(x_tok[:, :, :], T["x"][0].rearrange("(c t) d -> t c d", t=P)).then_inc(sem["in_loaded"], 16)
            act.dma_start(par_rows[0:96, :, 0, :],
                          T["conv_w"].rearrange("l j (t c) -> (j t) l c", c=P)).then_inc(sem["par_loaded"], 16)
            r0 = 0
            for n, w in ((24, T["conv_b"]), (16, T["g_ssm_out"]), (8, T["g_mlstm_head"].rearrange("l h v -> l (h v)")),
                         (8, T["g_ffn1"]), (8, T["g_mix"]), (8, T["g_ffn2"]), (8, T["g_ple"])):
                act.dma_start(par_rows[r0:r0 + n, :, 1, :],
                              w.rearrange("l (t c) -> t l c", c=P)).then_inc(sem["par_loaded"], 16)
                r0 += n
            act.dma_start(gf_row[:, :], T["g_final"].rearrange("(t c) -> t c", c=P)).then_inc(sem["par_loaded"], 16)
            r0 = 0
            for w in (T["b_igate"], T["b_fgate"], T["dt_bias"], T["a_log"], T["d_skip"]):
                n = w.shape[1]
                act.dma_start(row_one[0:1, :, r0:r0 + n], w.unsqueeze(0)).then_inc(sem["rows_done"], 16)
                r0 += n

            def hi(lay, k, k3, slot):
                act.wait_ge(w_raw[slot], (lay * (NU // RING) + k3 + 1) * 32)
                act.wait_ge(sem["unit_done"], lay * NU + k + 1)
                a_.activation(whi[slot][:, :, :], raw[slot][:, :, :], ACT.Copy).then_inc(sem["w_hi"], 1)

            def shi(lay, k):
                if k < NU:
                    hi(lay, k, k // RING, k % RING)

            def done(lay, k):
                act.wait_ge(sem["unit_done"], lay * NU + k + (RING + 1))

            def norm(lay, n):
                N = lay * 4 + n
                for i in range(4):
                    act.wait_ge(sem["h_ready"], N * 4 + (i + 1))
                    a_.activation(u32[:, 2 * i:2 * i + 2, :], h[:, 2 * i:2 * i + 2, :],
                                  ACT.Square).then_inc(sem["sq_ready"], 1)

            def norm_hi(lay, n):
                N = lay * 4 + n
                for k in range(KD):
                    act.wait_ge(sem["u32_ready"], N * KD + (k + 1))
                    a_.activation(u_hi[:, k, :], u32[:, k, :], ACT.Copy).then_inc(sem["u_hi_ready"], 1)

            def ffn(lay, f, k0):
                F = lay * 2 + f
                shi(lay, k0 + 2)
                done(lay, k0)
                a_.activation(sa[:, :, :], two(4), ACT.Silu).then_inc(sem["silu_done"], 1)
                shi(lay, k0 + 3)
                b3 = (k0 + 2) // RING
                with nc.scalar.Fori(0, FT - 1) as j:
                    def sh(r):
                        k = k0 + 4 + r
                        hi(lay, k + j * 3, k // RING + j, k % RING)
                    act.wait_ge(sem["prod_done"], F * FT + j + 1)
                    a_.activation(h1_hi[:, :, :], h1f[:, :, :], ACT.Copy).then_inc(sem["h1_hi_ready"], 1)
                    sh(0)
                    act.wait_ge(sem["unit_done"], lay * NU + j * 3 + (k0 + 2 + RING + 1))
                    a_.activation(sa[:, :, :], two(4), ACT.Silu).then_inc(sem["silu_done"], 1)
                    sh(1)
                    sh(2)
                act.wait_ge(sem["prod_done"], (F + 1) * FT)
                a_.activation(h1_hi[:, :, :], h1f[:, :, :], ACT.Copy).then_inc(sem["h1_hi_ready"], 1)
                shi(lay, k0 + U_FFN + 1)

            def groups(lay):
                def body(g, first):
                    G = act.snap(lay * NG + g)

                    def step(p):
                        k = K_MIX + p + 2
                        hi(lay, g * GU + k, g * (GU // RING) + k // RING, k % RING)

                    def gdone(p):
                        act.wait_ge(sem["unit_done"], lay * NU + g * GU + (K_MIX + p + RING + 1))

                    def tanh_conv(i, dst):
                        act.wait_ge(sem["conv_done"], G * 3 + (i + 1))
                        a_.activation(cth[:, :, :], dst, ACT.Tanh).then_inc(sem["tanh_done"], 1)

                    def decay(c):
                        for b in range(2):
                            act.wait_ge(sem["seg_done"], G * 4 + (2 * c + b + 3))
                            a_.activation(seg[:, c, 4 * b:4 * b + 4, :],
                                          bank[4 + 2 * c + b][:, :].rearrange("p (e t) -> p e t", e=4),
                                          ACT.Exp).then_inc(sem["exp_done"], 1)

                    def decay_from_start():
                        for b in range(2):
                            act.wait_ge(sem["acs_done"], G * 2 + (b + 1))
                            a_.activation(cs[:, 4 * b:4 * b + 4, :], bank[4 + b][:, :].rearrange("p (e t) -> p e t", e=4),
                                          ACT.Exp).then_inc(sem["acs_exp"], 1)

                    def score_exp():
                        act.wait_ge(sem["d_ready"], G + 1)
                        a_.activation(pm[:, :, :], pm[:, :, :], ACT.Exp, scale=-1.0).then_inc(sem["p_exp"], 1)

                    step(0)
                    gdone(BC)
                    a_.activation(xin[:, 0, :, 3:], two(0), ACT.Copy).then_inc(sem["act_evac"], 1)
                    if first:
                        act.wait_ge(sem["small_done"], lay + 1)
                        a_.activation(pre_row[:, :], bank[7][0:40, 0:S], ACT.Copy).then_inc(sem["pre_row_ready"], 1)
                    step(1)
                    tanh_conv(0, bcv[:, :, :])
                    gdone(QK)
                    a_.activation(qT[:, :], bank[1][:, 0:S], ACT.Copy, scale=MQK ** -0.5)
                    a_.activation(kT[:, :], bank[1][:, S:2 * S], ACT.Copy).then_inc(sem["act_evac"], 1)
                    if first:
                        act.wait_ge(sem["x_abs"], lay + 1)
                        a_.activation(sp_b[:, :, :], sp_a[:, :, :], ACT.Exp, scale=-1.0).then_inc(sem["sp_exp"], 1)
                        act.wait_ge(sem["row_bcast"], 1)
                        a_.activation(e_a[:, :], row_all[:, lay, 40:72], ACT.Exp).then_inc(sem["ea_ready"], 1)
                    step(2)
                    if not first:
                        decay(0)
                    gdone(X01)
                    a_.activation(xin[:, 1, :, 3:], two(2), ACT.Copy).then_inc(sem["act_evac"], 1)
                    step(3)
                    if first:
                        act.wait_ge(sem["cum_done"], lay + 1)
                        a_.activation(w_end[:, :], bank[7][:, 0:SH], ACT.Exp).then_inc(sem["cum_exp"], 1)
                        tanh_conv(1, xcv[:, 0:2, :])
                        decay(0)
                    else:
                        decay(1)
                        decay_from_start()
                        tanh_conv(1, xcv[:, 0:2, :])
                        score_exp()
                    gdone(X23)
                    a_.activation(xin[:, 0, :, 3:], two(0), ACT.Copy).then_inc(sem["act_evac"], 1)
                    step(4)
                    if first:
                        act.wait_ge(sem["row_back"], lay + 1)
                        tk = bank[6][:, 0:24].rearrange("p (a h) -> p a h", a=6)
                        a_.activation(tokc[:, 0:2, :], tk[:, 0:2, :], ACT.Copy).then_inc(sem["tok_ready"], 1)
                        a_.activation(tokc[:, 2:6, :], tk[:, 2:6, :], ACT.Exp).then_inc(sem["tok_ready"], 1)
                        decay(1)
                        decay_from_start()
                    tanh_conv(2, xcv[:, 2:4, :])
                    if first:
                        score_exp()
                    act.wait_ge(sem["gtk_ready"], G + 1)
                    act.wait_ge(sem["cbm_done"], G + 1)
                    a_.activation(ktok[:, :], bank[5][:, 384:512], ACT.Copy, scale=gtk[:, 5:6])
                    a_.activation(btok[:, :], bank[5][:, 256:384], ACT.Copy).then_inc(sem["btok_ready"], 1)
                    gdone(V)
                    a_.activation(vtok[:, :, 0:MV], two(1), ACT.Copy).then_inc(sem["act_evac"], 1)
                    step(5)
                    gdone(Z0)
                    a_.activation(zth[:, :, :], two(2), ACT.Tanh, scale=0.5).then_inc(sem["act_evac"], 1)
                    step(6)
                    act.wait_ge(sem["heads_done"], G + 1)
                    a_.activation(cst[:, 0:257], bank[3][:, 0:257], ACT.Copy).then_inc(sem["cst_ready"], 1)
                    a_.activation(num[:, 0, 0:257], bank[4][:, 0:257], ACT.Copy).then_inc(sem["num0_ready"], 1)
                    gdone(Z1)
                    act.wait_ge(sem["zth_ready"], G * 2 + 1)
                    a_.activation(zth[:, :, :], two(0), ACT.Tanh, scale=0.5).then_inc(sem["act_evac"], 1)
                    step(7)
                    act.wait_ge(sem["im_done"], G + 1)
                    a_.activation(inter[:, 0:257], bank[3][:, 0:257], ACT.Copy, scale=gtk[:, 4:5]).then_inc(sem["inter_ready"], 1)
                    act.wait_ge(sem["yi_done"], G + 1)
                    a_.activation(st[:, :], bank[4][:, :], ACT.Copy).then_inc(sem["st_ready"], 1)
                    act.wait_ge(sem["num1_ready"], G + 1)
                    for c in range(NC):
                        squares = (pm, scT)[c][:, :, :].rearrange("p a b -> p (a b)")
                        i = a_.activation(squares, num[:, c, 0:MV], ACT.Square, accum_out=nss[:, c:c + 1])
                    i.then_inc(sem["nsq_ready"], 1)
                    gdone(O)
                    a_.activation(osg[:, :, :], two(1), ACT.Tanh, scale=0.5).then_inc(sem["act_evac"], 1)
                    step(8)
                    act.wait_ge(sem["ha32_ready"], G + 1)
                    a_.activation(ha_hi[:, bass.ds(g * 2, 2), :], osg[:, :, :], ACT.Copy).then_inc(sem["ha_hi_ready"], 1)
                    act.wait_ge(sem["y_ready"], G + 1)
                    a_.activation(zs[:, :, :], y_feat[:, bass.ds(g * 4, 4), :], ACT.Square).then_inc(sem["ysq_ready"], 1)
                    gdone(GA)
                    a_.activation(gate_a[:, bass.ds(g * 2, 2), :], two(2), ACT.Tanh, scale=0.5).then_inc(sem["act_evac"], 1)

                body(0, True)
                with nc.scalar.Fori(1, NG) as g:
                    body(g, False)

            with nc.scalar.Fori(0, DEPTH) as lay:
                act.dma_start(wsm[:, :, 0:8], T["w_in"][lay].rearrange("(k p) m -> p k m", p=P)[:, :, C_IF:C_IF + 8],
                              ).then_inc(sem["wsm_loaded"], 16)
                act.dma_start(wsm[:, :, 8:40], T["w_in"][lay].rearrange("(k p) m -> p k m", p=P)[:, :, C_DT:C_DT + SH],
                              ).then_inc(sem["wsm_loaded"], 16)
                shi(lay, 0)
                shi(lay, 1)
                norm(lay, 0)
                norm_hi(lay, 0)
                ffn(lay, 0, 0)
                norm(lay, 1)
                norm_hi(lay, 1)
                act.wait_ge(sem["wsm_loaded"], lay * 32 + 32)
                a_.activation(wsm_hi[:, :, :], wsm[:, :, :], ACT.Copy).then_inc(sem["wsm_hi_ready"], 1)
                groups(lay)
                act.wait_ge(sem["group_free"], lay * NG + NG + 1)
                act.wait_ge(sem["ysum_ready"], lay * NG + NG + 1)
                for q in range(4):
                    shi(lay, K_GB + q + 2)
                    for t in range(4 * q, 4 * q + 4):
                        i = a_.activation(yb_hi[:, t, :], y_feat[:, t, :], ACT.Copy, scale=par[:, 120 + t:121 + t])
                    i.then_inc(sem["yb_hi_ready"], 1)
                    done(lay, K_GB + q)
                    a_.activation(gate_b[:, 2 * q:2 * q + 2, :], two(q % 3), ACT.Tanh, scale=0.5)\
                        .then_inc(sem["act_evac"], 1)
                act.wait_ge(sem["yB_done"], lay + 1)
                a_.activation(rB_y[:, :], bank[7][:, 0:S], ACT.Copy).then_inc(sem["yB_ready"], 1)
                with nc.scalar.Fori(0, 4) as m:
                    for r in range(3):
                        k = K_MERGE + r + 2
                        hi(lay, m * 3 + k, m + k // RING, k % RING)
                    act.wait_ge(sem["mrg_ready"], lay * 4 + m + 1)
                    a_.activation(u_hi[:, bass.ds(m * 2, 2), :], mrg[:, :, :], ACT.Copy).then_inc(sem["m_hi_ready"], 1)
                act.wait_ge(sem["m_lo_ready"], lay * 4 + 4)
                act.dma_start(w_ple, T["w_ple"][lay].rearrange("(k p) m -> p k m", p=P)).then_inc(sem["p_loaded"], 16)
                act.dma_start(p_tok, T["p"][lay, 0].rearrange("(c t) d -> t c d", t=P)).then_inc(sem["p_loaded"], 16)
                for q in range(4):
                    shi(lay, K_OUT + q + 2)
                act.wait_ge(sem["pt_done"], lay + 1)
                a_.activation(p_feat, two(3), ACT.Copy).then_inc(sem["pt_ready"], 1)
                norm(lay, 2)
                for q in range(4):
                    act.wait_ge(sem["pp_done"], lay * 4 + q + 1)
                    a_.activation(p_proj[:, 2 * q:2 * q + 2, :], two(4 + q % 2), ACT.Copy).then_inc(sem["pp_ready"], 1)
                norm_hi(lay, 2)
                ffn(lay, 1, K_FFN2)
                norm(lay, 3)
                norm_hi(lay, 3)
                for q in range(4):
                    shi(lay, K_PLE + q + 2)
                    done(lay, K_PLE + q)
                    if q >= 2:
                        act.wait_ge(sem["h_ready"], lay * 16 + 16 + (q - 1))
                    a_.activation(sa[:, :, :] if q % 2 == 0 else h1f[:, :, :], two(q % 3), ACT.Tanh,
                                  scale=0.5).then_inc(sem["ple_tanh"], 1)
            norm(DEPTH, 0)

        @block.vector
        def _(dve):
            v_ = nc.vector
            ch = Chain(dve, sem["dve_chain"])
            dve.sem_inc(sem["w_lo"], RING)
            dve.sem_inc(sem["unit_done"], RING)
            dve.sem_inc(sem["act_evac"], RING)
            dve.sem_inc(sem["seg_done"], 2)
            dve.sem_inc(sem["group_free"], 1)
            dve.sem_inc(sem["merge_read"], 2)
            dve.sem_inc(sem["ysum_ready"], 1)
            v_.memset(zeros[:, :], 0.0).then_inc(sem["const_ready"], 1)

            def lo(lay, k, slot):
                dve.wait_ge(sem["w_hi"], lay * NU + k + 1)
                v_.tensor_tensor(wlo[slot][:, :, :], raw[slot][:, :, :], whi[slot][:, :, :].bitcast(F32),
                                 ALU.subtract).then_inc(sem["w_lo"], 1)

            def slo(lay, k):
                if k < NU:
                    lo(lay, k, k % RING)

            def done(lay, k):
                dve.wait_ge(sem["unit_done"], lay * NU + k + (RING + 1))

            def scale_column(sums, scale, ready):
                for c in range(NC):
                    ch.add(v_.scalar_tensor_tensor(out=mdiag[:, c, :], in0=sums[:, c * P:(c + 1) * P], scalar=scale,
                                                   in1=ident[:, :], op0=ALU.mult, op1=ALU.mult,
                                                   accum_out=var[:, c:c + 1]))
                ch.wait()
                v_.tensor_scalar(var[:, :], var[:, :], EPS, None, ALU.add).then_inc(sem[ready], 1)

            def scale_diagonal(ready):
                for c in range(NC):
                    i = v_.tensor_scalar(rdiag[:, c, :], ident[:, :], rms[:, c:c + 1], None, ALU.mult)
                i.then_inc(sem[ready], 1)

            def norm(lay, n, final=False):
                N = lay * 4 + n
                dve.wait_ge(sem["ss_done"], N + 1)
                scale_column(bank[6], 1.0 / D, "var_ready")
                dve.wait_ge(sem["rms_ready"], N + 1)
                scale_diagonal("rdiag_ready")
                dve.wait_ge(sem["rB_done"], N + 1)

                def low(k):
                    dve.wait_ge(sem["u_hi_ready"], N * KD + (k + 1))
                    v_.tensor_tensor(u_lo[:, k, :], u32[:, k, :], u_hi[:, k, :].bitcast(F32),
                                     ALU.subtract).then_inc(sem["u_lo_ready"], 1)

                for k in range(KD):
                    gk = g_fin[:, k:k + 1] if final else par[:, 144 + 8 * n + k:145 + 8 * n + k]
                    v_.scalar_tensor_tensor(out=u32[:, k, :], in0=h[:, k, :], scalar=gk, in1=bank[7][:, 0:S],
                                            op0=ALU.mult, op1=ALU.mult).then_inc(sem["u32_ready"], 1)
                    if not final and k:
                        low(k - 1)
                if not final:
                    low(KD - 1)

            def ffn(lay, f, k0):
                F = lay * 2 + f

                def product(done_value, silu_value):
                    dve.wait_ge(sem["unit_done"], done_value)
                    dve.wait_ge(sem["silu_done"], silu_value)
                    v_.tensor_tensor(h1f[:, :, :], sa[:, :, :], two(5), ALU.mult).then_inc(sem["prod_done"], 1)

                def h1_low(n):
                    dve.wait_ge(sem["h1_hi_ready"], n)
                    v_.tensor_tensor(h1_lo[:, :, :], h1f[:, :, :], h1_hi[:, :, :].bitcast(F32),
                                     ALU.subtract).then_inc(sem["h1_ready"], 1)

                slo(lay, k0 + 2)
                slo(lay, k0 + 3)
                product(lay * NU + (k0 + 1 + RING + 1), F * FT + 1)
                with nc.vector.Fori(0, FT - 1) as j:
                    h1_low(F * FT + j + 1)
                    for r in range(3):
                        k = k0 + 4 + r
                        lo(lay, j * 3 + k, k % RING)
                    product(lay * NU + j * 3 + (k0 + 4 + RING + 1), F * FT + j + 2)
                h1_low((F + 1) * FT)
                slo(lay, k0 + U_FFN + 1)
                for i in range(4):
                    if i < 3:
                        dve.wait_ge(sem["down_done"], F * 3 + (i + 1))
                    else:
                        done(lay, k0 + U_FFN - 1)
                    v_.scalar_tensor_tensor(out=h[:, 2 * i:2 * i + 2, :], in0=two(i), scalar=0.5,
                                            in1=h[:, 2 * i:2 * i + 2, :], op0=ALU.mult, op1=ALU.add)\
                        .then_inc(sem["h_ready"], 1)

            def softplus_gates(lay):
                dve.wait_ge(sem["pre_ready"], lay + 1)
                ps = bank[7][:, 0:80].rearrange("p (c n) -> p c n", c=NC)
                dve.wait_ge(sem["row_bcast"], 1)
                ch.add(v_.tensor_tensor(pre[:, :, :], ps,
                                        row_all[:, lay, 0:40].unsqueeze(1).broadcast_to([P, NC, 40]), ALU.add))
                ch.wait()
                ch.add(v_.tensor_scalar(spx[:, :, 0:4], pre[:, :, 4:8], -1.0, None, ALU.mult))
                ch.add(v_.tensor_copy(spx[:, :, 4:36], pre[:, :, 8:40]))
                ch.wait()
                v_.scalar_tensor_tensor(out=sp_a[:, :, :], in0=spx[:, :, :], scalar=-1.0, in1=spx[:, :, :],
                                        op0=ALU.mult, op1=ALU.max).then_inc(sem["x_abs"], 1)
                ch.add(v_.tensor_scalar(spx[:, :, :], spx[:, :, :], 0.0, None, ALU.max))
                dve.wait_ge(sem["sp_exp"], lay + 1)
                ch.add(v_.tensor_scalar(sp_a[:, :, :], sp_b[:, :, :], 2.0, None, ALU.add))
                ch.wait()
                ch.add(v_.reciprocal(sp_c[:, :, :], sp_a[:, :, :]))
                ch.wait()
                ch.add(v_.tensor_tensor(sp_a[:, :, :], sp_b[:, :, :], sp_c[:, :, :], ALU.mult))
                ch.wait()
                ch.add(v_.tensor_tensor(sp_b[:, :, :], sp_a[:, :, :], sp_a[:, :, :], ALU.mult))
                ch.wait()
                ch.add(v_.tensor_scalar(sp_c[:, :, :], sp_b[:, :, :], 1.0 / 17, None, ALU.mult))
                for n in (15, 13, 11, 9, 7, 5, 3):
                    ch.wait()
                    ch.add(v_.scalar_tensor_tensor(out=sp_c[:, :, :], in0=sp_c[:, :, :], scalar=1.0 / n,
                                                   in1=sp_b[:, :, :], op0=ALU.add, op1=ALU.mult))
                ch.wait()
                ch.add(v_.scalar_tensor_tensor(out=sp_c[:, :, :], in0=sp_c[:, :, :], scalar=1.0,
                                               in1=sp_a[:, :, :], op0=ALU.add, op1=ALU.mult))
                ch.wait()
                ch.add(v_.scalar_tensor_tensor(out=spx[:, :, :], in0=sp_c[:, :, :], scalar=2.0,
                                               in1=spx[:, :, :], op0=ALU.mult, op1=ALU.add))
                ch.wait()
                dve.wait_ge(sem["ea_ready"], lay + 1)
                v_.scalar_tensor_tensor(out=dA[:, :, :], in0=spx[:, :, 4:36], scalar=-1.0,
                                        in1=e_a[:, :].unsqueeze(1).broadcast_to([P, NC, SH]),
                                        op0=ALU.mult, op1=ALU.mult).then_inc(sem["dA_ready"], 1)

            def gate_rows(lay):
                dve.wait_ge(sem["row_tr"], lay + 1)
                ch.add(v_.tensor_copy(r_i[:, :], bank[6][0:MH, 0:S]))
                ch.add(v_.tensor_copy(r_f[:, :], bank[6][0:MH, S:2 * S]))
                ch.wait()
                for c in range(NC):
                    s = slice(c * P, (c + 1) * P)
                    ch.add(v_.tensor_tensor_scan(r_b[:, s], ones[0:MH, :], r_f[:, s], 0.0, ALU.mult, ALU.subtract))
                ch.wait()
                ch.add(v_.tensor_tensor(r_w[:, :], r_i[:, :], r_b[:, :], ALU.subtract))
                ch.wait()
                ch.add(v_.tensor_tensor_scan(r_m[:, 0:P], r_w[:, 0:P], r_w[:, 0:P], 0.0, ALU.max, ALU.max))
                ch.wait()
                ch.add(v_.tensor_tensor(m_start[:, :], r_b[:, P - 1:P], r_m[:, P - 1:P], ALU.add))
                ch.wait()
                ch.add(v_.tensor_tensor_scan(r_m[:, P:], r_w[:, P:], r_w[:, P:], m_start[:, :], ALU.max, ALU.max))
                ch.wait()
                ch.add(v_.tensor_copy(r_x[:, 0:2, :], r_w[:, :].rearrange("p (c t) -> p c t", c=NC)))
                ch.add(v_.scalar_tensor_tensor(out=r_x[:, 2:4, :], in0=r_b[:, :].rearrange("p (c t) -> p c t", c=NC),
                                               scalar=-1.0, in1=r_m[:, :].rearrange("p (c t) -> p c t", c=NC),
                                               op0=ALU.mult, op1=ALU.subtract))
                ch.add(v_.tensor_scalar(r_x[:, 4, :], r_m[:, P:], m_start[:, :], -1.0, ALU.subtract, ALU.mult))
                ch.add(v_.tensor_scalar(r_x[:, 5, :], r_w[:, 0:P], r_m[:, P - 1:P], None, ALU.subtract))
                v_.tensor_tensor(M4[:, :, :], r_m[:, :].unsqueeze(1).broadcast_to([MH, MH, S]),
                                 ident[0:MH, 0:MH].unsqueeze(2).broadcast_to([MH, MH, S]),
                                 ALU.mult).then_inc(sem["row_ready"], 1)

            def groups(lay):
                v_.memset(xin[:, :, :, 0:3], 0.0)
                ch.add(v_.memset(vtok[:, :, MV:MV + 1], 1.0))

                def body(g, first):
                    G = dve.snap(lay * NG + g)

                    def step(p):
                        k = K_MIX + p + 2
                        lo(lay, g * GU + k, k % RING)

                    def taken(p):
                        dve.wait_ge(sem["act_evac"], lay * NE + g * GU + (p + RING + 1))

                    def conv(i, buf, tiles, dst):
                        for j in range(SCONV):
                            for q, t in enumerate(tiles):
                                src = xin[:, buf, q, j:j + S]
                                if j == 0:
                                    ins = v_.tensor_scalar(dst[:, q, :], src, gcw[:, 0, t:t + 1], gcb[:, t:t + 1],
                                                           ALU.mult, ALU.add)
                                else:
                                    ins = v_.scalar_tensor_tensor(out=dst[:, q, :], in0=src, scalar=gcw[:, j, t:t + 1],
                                                                  in1=dst[:, q, :], op0=ALU.mult, op1=ALU.add)
                                if j < SCONV - 1 or q == 0:
                                    ch.add(ins)
                                else:
                                    ins.then_inc(sem["conv_done"], 1)
                            if j < SCONV - 1:
                                ch.wait()

                    def silu(i, dst):
                        dve.wait_ge(sem["tanh_done"], G * 3 + (i + 1))
                        v_.scalar_tensor_tensor(out=dst, in0=cth[:, :, :], scalar=1.0, in1=dst,
                                                op0=ALU.add, op1=ALU.mult).then_inc(sem["cv_ready"], 1)

                    heads = bass.ds(g * EH, EH)

                    def per_head(col):
                        return col.unsqueeze(2).broadcast_to([P, EH, HP])

                    def split_heads(x):
                        return x.rearrange("p (e d) -> p e d", e=EH)

                    def distances():
                        dve.wait_ge(sem["gtk_ready"], G + 1)
                        dve.wait_ge(sem["scores_done"], G + 1)
                        for c in range(NC):
                            i = v_.tensor_scalar(pm[:, c, :], bank[3][:, S + c * P:S + (c + 1) * P], gtk[:, c:c + 1],
                                                 0.0, ALU.subtract, ALU.max)
                        i.then_inc(sem["d_ready"], 1)

                    def weigh_scores():
                        dve.wait_ge(sem["pm_ready"], G + 1)
                        v_.tensor_tensor(scT[:, :, :], pm[:, :, :], bank[3][:, 0:S].rearrange("p (c t) -> p c t", c=NC),
                                         ALU.mult).then_inc(sem["sct_ready"], 1)

                    step(0)
                    step(1)
                    dve.wait_ge(sem["group_ready"], G + 1)
                    taken(BC)
                    conv(0, 0, (0, 1), bcv[:, :, :])
                    silu(0, bcv[:, :, :])
                    if first:
                        softplus_gates(lay)
                        step(2)
                        gate_rows(lay)
                    else:
                        step(2)
                        distances()
                    step(3)
                    taken(X01)
                    conv(1, 1, (2, 3), xcv[:, 0:2, :])
                    silu(1, xcv[:, 0:2, :])
                    if not first:
                        weigh_scores()
                    step(4)
                    if first:
                        distances()
                    taken(X23)
                    conv(2, 0, (4, 5), xcv[:, 2:4, :])
                    silu(2, xcv[:, 2:4, :])
                    if first:
                        weigh_scores()
                    dve.wait_ge(sem["cb_done"], G + 1)
                    v_.tensor_tensor(cbm[:, :, :], bank[5][:, 0:S].rearrange("p (c t) -> p c t", c=NC),
                                     tri_le[:, :].unsqueeze(1).broadcast_to([P, NC, P]), ALU.mult)\
                        .then_inc(sem["cbm_done"], 1)
                    step(5)
                    dve.wait_ge(sem["exp_done"], G * 4 + 4)
                    dve.wait_ge(sem["cbm_done"], G + 1)
                    for c in range(NC):
                        v_.tensor_tensor(seg[:, c, :, :], seg[:, c, :, :],
                                         cbm[:, c, :].unsqueeze(1).broadcast_to([P, EH, P]), ALU.mult)\
                            .then_inc(sem["m_ready"], 1)
                    dve.wait_ge(sem["acs_exp"], G * 2 + 2)
                    v_.tensor_tensor(cs[:, :, :], cs[:, :, :], bcv[:, 1, P:2 * P].unsqueeze(1).broadcast_to([P, EH, P]),
                                     ALU.mult).then_inc(sem["cs_ready"], 1)
                    step(6)
                    taken(Z0)
                    dve.wait_ge(sem["ysum_ready"], G + 1)
                    v_.scalar_tensor_tensor(out=zs[:, 0:2, :], in0=zth[:, :, :], scalar=1.0, in1=two(2),
                                            op0=ALU.add, op1=ALU.mult).then_inc(sem["zth_ready"], 1)
                    dve.wait_ge(sem["xtr_done"], G + 1)
                    for c in range(NC):
                        ch.add(v_.tensor_tensor(split_heads(xw[:, c, :]), split_heads(bank[6 + c][:, :]),
                                                per_head(spx[:, c, bass.ds(g * EH + 4, EH)]), ALU.mult))
                    ch.wait()
                    dve.wait_ge(sem["cum_exp"], lay + 1)
                    v_.tensor_tensor(split_heads(xwe[:, :]), split_heads(xw[:, 0, :]), per_head(w_end[:, heads]),
                                     ALU.mult).then_inc(sem["xw_ready"], 1)
                    step(7)
                    dve.wait_ge(sem["inter_ready"], G + 1)
                    v_.tensor_tensor(num[:, 1, 0:257], bank[5][:, 0:257], inter[:, 0:257], ALU.add)\
                        .then_inc(sem["num1_ready"], 1)
                    dve.wait_ge(sem["num1_ready"], G + 1)
                    ch.add(v_.scalar_tensor_tensor(out=den[:, :].unsqueeze(2), in0=num[:, :, MV:MV + 1], scalar=-1.0,
                                                   in1=num[:, :, MV:MV + 1], op0=ALU.mult, op1=ALU.max))
                    ch.wait()
                    ch.add(v_.tensor_tensor(den[:, :], den[:, :], gtk[:, 2:4], ALU.max))
                    ch.wait()
                    ch.add(v_.reciprocal(rden[:, :], den[:, :]))
                    dve.wait_ge(sem["nsq_ready"], G + 1)
                    ch.wait()
                    ch.add(v_.tensor_tensor(hvar[:, :], nss[:, :], rden[:, :], ALU.mult))
                    ch.wait()
                    ch.add(v_.tensor_tensor(hvar[:, :], hvar[:, :], rden[:, :], ALU.mult))
                    ch.wait()
                    v_.tensor_scalar(hvar[:, :], hvar[:, :], 1.0 / MV, EPS, ALU.mult, ALU.add).then_inc(sem["hvar_ready"], 1)
                    dve.wait_ge(sem["hrms_ready"], G + 1)
                    ch.add(v_.tensor_tensor(hsc[:, :], hrms[:, :], rden[:, :], ALU.mult))
                    ch.wait()
                    for c in range(NC):
                        i = v_.tensor_scalar(num[:, c, 0:MV], num[:, c, 0:MV], hsc[:, c:c + 1], None, ALU.mult)
                    i.then_inc(sem["hn_ready"], 1)
                    taken(Z1)
                    v_.scalar_tensor_tensor(out=zs[:, 2:4, :], in0=zth[:, :, :], scalar=1.0, in1=two(0),
                                            op0=ALU.add, op1=ALU.mult).then_inc(sem["zth_ready"], 1)
                    step(8)
                    dve.wait_ge(sem["y_done"], G + 1)
                    for t in range(4):
                        ch.add(v_.scalar_tensor_tensor(out=xcv[:, t, :], in0=xcv[:, t, :], scalar=gdk[:, t:t + 1],
                                                       in1=bank[6 + t // 2][:, (t % 2) * S:(t % 2 + 1) * S],
                                                       op0=ALU.mult, op1=ALU.add))
                    ch.wait()
                    dve.wait_ge(sem["zth_ready"], G * 2 + 2)
                    v_.scalar_tensor_tensor(out=y_feat[:, bass.ds(g * 4, 4), :].rearrange("p a b -> p (a b)"),
                                            in0=xcv[:, :, :].rearrange("p a b -> p (a b)"), scalar=0.5,
                                            in1=zs[:, :, :].rearrange("p a b -> p (a b)"),
                                            op0=ALU.mult, op1=ALU.mult).then_inc(sem["y_ready"], 1)
                    taken(O)
                    for t in range(2):
                        ch.add(v_.tensor_scalar(osg[:, t, :], osg[:, t, :], 1.0, ghn[:, t:t + 1], ALU.add, ALU.mult))
                    ch.wait()
                    dve.wait_ge(sem["hnT_done"], G + 1)
                    v_.tensor_tensor(osg[:, :, :], osg[:, :, :], two(3), ALU.mult).then_inc(sem["ha32_ready"], 1)
                    dve.wait_ge(sem["ha_hi_ready"], G + 1)
                    v_.tensor_tensor(ha_lo[:, bass.ds(g * 2, 2), :], osg[:, :, :],
                                     ha_hi[:, bass.ds(g * 2, 2), :].bitcast(F32), ALU.subtract).then_inc(sem["ha_ready"], 1)
                    dve.wait_ge(sem["ysq_ready"], G + 1)
                    dve.sem_inc(sem["group_free"], 1)
                    ch.clear()

                ch.clear()
                body(0, True)
                with nc.vector.Fori(1, NG) as g:
                    body(g, False)

            dve.wait_ge(sem["par_tr"], 1)
            for l in range(DEPTH):
                ch.add(v_.tensor_copy(par_all[:, l, 0:96], bank[4 + l][:, 0:96]))
                ch.add(v_.tensor_copy(par_all[:, l, 96:176], bank[4 + l][:, 128:208]))
            ch.add(v_.tensor_copy(g_fin[:, :], bank[4][:, 256:264]))
            dve.wait_ge(sem["row_bcast"], 1)
            for b in range(2):
                hp = slice(b * HP, (b + 1) * HP)
                ch.add(v_.tensor_copy(dcol[hp, :, :], row_all[hp, :, 72 + b:104:2]))
            ch.wait()
            for i in range(4):
                dve.wait_ge(sem["xtr_in"], i + 1)
                v_.tensor_copy(h[:, 2 * i:2 * i + 2, :], two(i)).then_inc(sem["h_ready"], 1)
            ch.clear()

            with nc.vector.Fori(0, DEPTH) as lay:
                ch.add(v_.tensor_scalar(par[:, 0:120], par_all[:, lay, 0:120], 0.5, None, ALU.mult))
                ch.add(v_.tensor_copy(par[:, 120:136], par_all[:, lay, 120:136]))
                ch.add(v_.tensor_scalar(par[:, 136:144], par_all[:, lay, 136:144], 0.5, None, ALU.mult))
                ch.add(v_.tensor_copy(par[:, 144:176], par_all[:, lay, 144:176]))
                ch.wait()
                slo(lay, 0)
                slo(lay, 1)
                norm(lay, 0)
                ffn(lay, 0, 0)
                norm(lay, 1)
                dve.wait_ge(sem["wsm_hi_ready"], lay + 1)
                v_.tensor_tensor(wsm_lo[:, :, :], wsm[:, :, :], wsm_hi[:, :, :].bitcast(F32),
                                 ALU.subtract).then_inc(sem["wsm_ready"], 1)
                groups(lay)
                for q in range(4):
                    slo(lay, K_GB + q + 2)
                    dve.wait_ge(sem["yb_hi_ready"], lay * 4 + q + 1)
                    for t in range(4 * q, 4 * q + 4):
                        i = v_.scalar_tensor_tensor(out=yb_lo[:, t, :], in0=y_feat[:, t, :], scalar=par[:, 120 + t:121 + t],
                                                    in1=yb_hi[:, t, :].bitcast(F32), op0=ALU.mult, op1=ALU.subtract)
                    i.then_inc(sem["yb_ready"], 1)
                    if q == 0:
                        dve.wait_ge(sem["yss_done"], lay + 1)
                        scale_column(bank[7], 1.0 / SI, "yvar_ready")
                    if q == 1:
                        dve.wait_ge(sem["yrms_ready"], lay + 1)
                        scale_diagonal("ydiag_ready")
                ch.clear()
                with nc.vector.Fori(0, 4) as m:
                    for r in range(2):
                        k = K_MERGE + r + 2
                        lo(lay, m * 3 + k, k % RING)
                    dve.wait_ge(sem["unit_done"], lay * NU + m * 3 + (K_MERGE + RING + 1))
                    v_.scalar_tensor_tensor(out=mtmp[:, :, :], in0=gate_a[:, bass.ds(m * 2, 2), :], scalar=1.0,
                                            in1=two(0), op0=ALU.add, op1=ALU.mult).then_inc(sem["merge_read"], 1)
                    k = K_MERGE + 4
                    lo(lay, m * 3 + k, k % RING)
                    dve.wait_ge(sem["unit_done"], lay * NU + m * 3 + (K_MERGE + 2 + RING + 1))
                    v_.scalar_tensor_tensor(out=mrg[:, :, :], in0=gate_b[:, bass.ds(m * 2, 2), :], scalar=1.0,
                                            in1=two(1), op0=ALU.add, op1=ALU.mult).then_inc(sem["merge_read"], 1)
                    dve.wait_ge(sem["merge_read"], lay * 8 + m * 2 + 4)
                    dve.wait_ge(sem["yB_ready"], lay + 1)
                    ch.add(v_.tensor_tensor(mrg[:, :, :], mrg[:, :, :],
                                            rB_y[:, :].unsqueeze(1).broadcast_to([P, 2, S]), ALU.mult))
                    ch.wait()
                    v_.tensor_tensor(mrg[:, :, :], mrg[:, :, :], mtmp[:, :, :], ALU.add).then_inc(sem["mrg_ready"], 1)
                    dve.wait_ge(sem["m_hi_ready"], lay * 4 + m + 1)
                    v_.tensor_tensor(u_lo[:, bass.ds(m * 2, 2), :], mrg[:, :, :],
                                     u_hi[:, bass.ds(m * 2, 2), :].bitcast(F32), ALU.subtract).then_inc(sem["m_lo_ready"], 1)
                    ch.clear()
                for q in range(4):
                    slo(lay, K_OUT + q + 2)
                    done(lay, K_OUT + q)
                    v_.scalar_tensor_tensor(out=h[:, 2 * q:2 * q + 2, :], in0=two(q % 3), scalar=0.5,
                                            in1=h[:, 2 * q:2 * q + 2, :], op0=ALU.mult, op1=ALU.add)\
                        .then_inc(sem["h_ready"], 1)
                norm(lay, 2)
                ffn(lay, 1, K_FFN2)
                norm(lay, 3)
                for q in range(4):
                    slo(lay, K_PLE + q + 2)
                    dve.wait_ge(sem["pp_ready"], lay * 4 + 4)
                    dve.wait_ge(sem["ple_tanh"], lay * 4 + q + 1)
                    t = sa if q % 2 == 0 else h1f
                    ch.add(v_.scalar_tensor_tensor(out=t[:, :, :], in0=t[:, :, :], scalar=1.0,
                                                   in1=p_proj[:, 2 * q:2 * q + 2, :], op0=ALU.add, op1=ALU.mult))
                    ch.wait()
                    v_.scalar_tensor_tensor(out=h[:, 2 * q:2 * q + 2, :], in0=t[:, :, :], scalar=0.5,
                                            in1=h[:, 2 * q:2 * q + 2, :], op0=ALU.mult, op1=ALU.add)\
                        .then_inc(sem["h_ready"], 1)
                ch.clear()
            norm(DEPTH, 0, final=True)
            for q in range(4):
                dve.wait_ge(sem["xt_done"], q + 1)
                c = q // 2
                v_.tensor_copy(x_tok[:, c, (q % 2) * 512:(q % 2) * 512 + 512], bank[q][:, :]).then_inc(sem["fin_done"], 1)

        @block.tensor
        def _(pe):
            mm = nc.tensor.matmul

            def weights(lay, k):
                pe.wait_ge(sem["w_lo"], lay * NU + k + (RING + 1))

            def zero_bank(b):
                mm(bank[b][:, :], zeros[:, :], zeros[:, :].unsqueeze(1).broadcast_to([P, 4, P]), start=True,
                   stop=False, skip_group_check=True)

            def feat(slot, b, xh, xl, seeded=False):
                for m in range(2):
                    o = bank[b][:, m * S:(m + 1) * S]
                    cs = slice(m * P, (m + 1) * P)
                    for k in range(KD):
                        for q, (w, x) in enumerate(((whi, xh), (whi, xl), (wlo, xh))):
                            i = mm(o, w[slot][:, k, cs], x[:, k, :], start=(k + q == 0 and not seeded),
                                   stop=(k == KD - 1 and q == 2 and not seeded), skip_group_check=seeded)
                i.then_inc(sem["unit_done"], 1)

            def feat_first(slot, b, n):
                zero_bank(b)
                for k in range(KD):
                    pe.wait_ge(sem["u_lo_ready"], n * KD + (k + 1))
                    for m in range(2):
                        cs = slice(m * P, (m + 1) * P)
                        for w, x in ((whi, u_hi), (whi, u_lo), (wlo, u_hi)):
                            i = mm(bank[b][:, m * S:(m + 1) * S], w[slot][:, k, cs], x[:, k, :], start=False, stop=False,
                                   skip_group_check=True)
                i.then_inc(sem["unit_done"], 1)

            def tok(slot, b, xh, xl):
                for c in range(NC):
                    o = bank[b][:, c * NP:(c + 1) * NP]
                    cs = slice(c * P, (c + 1) * P)
                    for k in range(KD):
                        mm(o, xh[:, k, cs], whi[slot][:, k, :], start=(k == 0), stop=False)
                        mm(o, xh[:, k, cs], wlo[slot][:, k, :], start=False, stop=False)
                        i = mm(o, xl[:, k, cs], whi[slot][:, k, :], start=False, stop=(k == KD - 1))
                i.then_inc(sem["unit_done"], 1)

            def norm(lay, n):
                N = lay * 4 + n
                for i in range(4):
                    pe.wait_ge(sem["sq_ready"], N * 4 + (i + 1))
                    for k in (2 * i, 2 * i + 1):
                        ins = mm(bank[6][:, 0:S], ones[:, :], u32[:, k, :], start=(k == 0), stop=(k == KD - 1))
                ins.then_inc(sem["ss_done"], 1)

            def norm_rows(lay, n):
                pe.wait_ge(sem["rdiag_ready"], lay * 4 + n + 1)
                for c in range(NC):
                    ins = mm(bank[7][:, c * P:(c + 1) * P], ones[:, :], rdiag[:, c, :], start=True, stop=True)
                ins.then_inc(sem["rB_done"], 1)

            def ffn(lay, f, k0):
                F = lay * 2 + f
                s = [(k0 + r) % RING for r in range(3)]
                for b in range(4):
                    zero_bank(b)

                def down(slot, last=False):
                    w = [x[slot][:, :, :].rearrange("p a b -> p (a b)").rearrange("p (k m) -> p k m", k=2)
                         for x in (whi, wlo)]
                    for m in range(KD):
                        o = bank[m // 2][:, (m % 2) * S:(m % 2 + 1) * S]
                        cs = slice(m * P, (m + 1) * P)
                        for kk in range(2):
                            for ww, xx in ((w[0], h1_hi), (w[0], h1_lo), (w[1], h1_hi)):
                                i = mm(o, ww[:, kk, cs], xx[:, kk, :], start=False, stop=False, skip_group_check=True)
                        if last and m in (1, 3, 5):
                            i.then_inc(sem["down_done"], 1)
                    i.then_inc(sem["unit_done"], 1)

                weights(lay, k0)
                if f == 1:
                    pe.wait_ge(sem["pp_ready"], lay * 4 + 4)
                feat_first(s[0], 4, lay * 4 + 2 * f)
                weights(lay, k0 + 1)
                feat(s[1], 5, u_hi, u_lo)
                with nc.tensor.Fori(0, FT - 1) as j:
                    weights(lay, j * 3 + (k0 + 2))
                    pe.wait_ge(sem["silu_done"], F * FT + j + 1)
                    feat(s[2], 4, u_hi, u_lo)
                    weights(lay, j * 3 + (k0 + 3))
                    pe.wait_ge(sem["h1_ready"], F * FT + j + 1)
                    down(s[0])
                    weights(lay, j * 3 + (k0 + 4))
                    feat(s[1], 5, u_hi, u_lo)
                weights(lay, k0 + U_FFN - 1)
                pe.wait_ge(sem["h1_ready"], (F + 1) * FT)
                down(s[2], last=True)

            def small(lay):
                pe.wait_ge(sem["wsm_ready"], lay + 1)
                for k in range(KD):
                    for q, (w, x) in enumerate(((wsm_hi, u_hi), (wsm_hi, u_lo), (wsm_lo, u_hi))):
                        i = mm(bank[7][0:40, 0:S], w[:, k, :], x[:, k, :], start=(k + q == 0), stop=(k == KD - 1 and q == 2))
                i.then_inc(sem["small_done"], 1)

            def small_back(lay):
                pe.wait_ge(sem["pre_row_ready"], lay + 1)
                for c in range(NC):
                    i = mm(bank[7][:, c * 40:(c + 1) * 40], pre_row[:, c * P:(c + 1) * P], ident[0:40, 0:40],
                           start=True, stop=True)
                i.then_inc(sem["pre_ready"], 1)

            def gates(lay):
                pe.wait_ge(sem["dA_ready"], lay + 1)
                mm(bank[7][:, 0:SH], tri_gt[:, :], dA[:, 0, :], start=True, stop=True).then_inc(sem["cum_done"], 1)
                for c in range(NC):
                    nc.tensor.transpose(bank[6][0:MH, c * P:(c + 1) * P], pre[:, c, 0:MH], ident[:, :])
                    i = nc.tensor.transpose(bank[6][0:MH, S + c * P:S + (c + 1) * P], spx[:, c, 0:MH], ident[:, :])
                i.then_inc(sem["row_tr"], 1)

            def gates_back(lay):
                pe.wait_ge(sem["row_ready"], lay + 1)
                for r in range(6):
                    i = mm(bank[6][:, r * MH:(r + 1) * MH], r_x[:, r, :], ident[0:MH, 0:MH], start=True, stop=True)
                i.then_inc(sem["row_back"], 1)

            def groups(lay):
                def body(g, first):
                    G = pe.snap(lay * NG + g)

                    def unit(p, kind):
                        weights(lay, g * GU + (K_MIX + p))
                        pe.wait_ge(sem["act_evac"], lay * NE + g * GU + (p + 1))
                        kind((K_MIX + p) % RING, p % 3, u_hi, u_lo)

                    def evac(p):
                        pe.wait_ge(sem["act_evac"], lay * NE + g * GU + (p + RING + 1))

                    def segments(c):
                        for b in range(2):
                            pe.wait_ge(sem["r_built"], G * 4 + (2 * c + b + 1))
                            mm(bank[4 + 2 * c + b][:, :], tri_gt[:, :], R[:, b, :, :], start=True, stop=True)\
                                .then_inc(sem["seg_done"], 1)

                    def from_start():
                        for b in range(2):
                            pe.wait_ge(sem["exp_done"], G * 4 + (b + 1))
                            mm(bank[4 + b][:, :], ones[:, :], R[:, b, :, :], start=True, stop=True)\
                                .then_inc(sem["acs_done"], 1)

                    def scores():
                        for c in range(NC):
                            cs_ = slice(c * P, (c + 1) * P)
                            mm(bank[3][:, cs_], kT[:, cs_], qT[:, cs_], start=True, stop=True)
                        mm(bank[3][:, S:2 * S], ones[0:MH, :], M4[:, bass.ds(g, 1), :].rearrange("p a b -> p (a b)"),
                           start=True, stop=True).then_inc(sem["scores_done"], 1)

                    if first:
                        weights(lay, K_MIX)
                        pe.wait_ge(sem["act_evac"], lay * NE + 1)
                        feat_first(K_MIX % RING, 0, lay * 4 + 1)
                        small(lay)
                        unit(QK, feat)
                        small_back(lay)
                        unit(X01, feat)
                        gates(lay)
                        segments(0)
                        unit(X23, feat)
                        gates_back(lay)
                        pe.wait_ge(sem["tok_ready"], lay * 2 + 2)
                        segments(1)
                        from_start()
                        scores()
                    else:
                        pe.wait_ge(sem["zth_ready"], G * 2)
                        unit(BC, feat)
                        unit(QK, feat)
                        segments(0)
                        unit(X01, feat)
                        segments(1)
                        evac(QK)
                        from_start()
                        scores()
                        unit(X23, feat)
                    pe.wait_ge(sem["cv_ready"], G * 3 + 1)
                    pe.wait_ge(sem["acs_exp"], G * 2 + 2)
                    for c in range(NC):
                        cs_ = slice(c * P, (c + 1) * P)
                        mm(bank[5][:, cs_], bcv[:, 0, cs_], bcv[:, 1, cs_], start=True, stop=True)
                    nc.tensor.transpose(bank[5][:, 256:384], bcv[:, 0, 0:P], ident[:, :])
                    nc.tensor.transpose(bank[5][:, 384:512], kT[:, 0:P], ident[:, :]).then_inc(sem["cb_done"], 1)
                    unit(V, tok)
                    unit(Z0, feat)
                    pe.wait_ge(sem["sct_ready"], G + 1)
                    pe.wait_ge(sem["btok_ready"], G + 1)
                    evac(V)
                    mm(bank[3][:, 0:257], ktok[:, :], vtok[:, 0, 0:257], start=True, stop=True)
                    mm(bank[4][:, 0:257], scT[:, 0, :], vtok[:, 0, 0:257], start=True, stop=True)
                    mm(bank[5][:, 0:257], scT[:, 1, :], vtok[:, 1, 0:257], start=True, stop=True)\
                        .then_inc(sem["heads_done"], 1)
                    pe.wait_ge(sem["cv_ready"], G * 3 + 3)
                    pe.wait_ge(sem["exp_done"], G * 4 + 4)
                    for c in range(NC):
                        for t in range(4):
                            i = nc.tensor.transpose(bank[6 + c][:, t * P:(t + 1) * P], xcv[:, t, c * P:(c + 1) * P],
                                                    ident[:, :])
                    i.then_inc(sem["xtr_done"], 1)
                    unit(Z1, feat)
                    pe.wait_ge(sem["cst_ready"], G + 1)
                    mm(bank[3][:, 0:257], qT[:, P:2 * P], cst[:, 0:257], start=True, stop=True).then_inc(sem["im_done"], 1)
                    pe.wait_ge(sem["m_ready"], G * 2 + 2)
                    pe.wait_ge(sem["xw_ready"], G + 1)
                    pe.wait_ge(sem["num0_ready"], G + 1)
                    mm(bank[4][:, :], btok[:, :], xwe[:, :], start=True, stop=True).then_inc(sem["yi_done"], 1)
                    for c in range(NC):
                        if c == 1:
                            unit(O, feat)
                            pe.wait_ge(sem["st_ready"], G + 1)
                        for e in range(EH):
                            es = slice(e * HP, (e + 1) * HP)
                            t = e // 2
                            o = bank[6 + t // 2][(e % 2) * HP:(e % 2 + 1) * HP, (t % 2) * S + c * P:(t % 2) * S + (c + 1) * P]
                            i = mm(o, xw[:, c, es], seg[:, c, e, :], start=True, stop=(c == 0))
                            if c == 1:
                                i = mm(o, st[:, es], cs[:, e, :], start=False, stop=True)
                    i.then_inc(sem["y_done"], 1)
                    pe.wait_ge(sem["hn_ready"], G + 1)
                    for t in range(2):
                        for c in range(NC):
                            i = nc.tensor.transpose(bank[3][:, t * S + c * P:t * S + (c + 1) * P],
                                                    num[:, c, t * P:(t + 1) * P], ident[:, :])
                    i.then_inc(sem["hnT_done"], 1)
                    unit(GA, feat)

                body(0, True)
                with nc.tensor.Fori(1, NG) as g:
                    body(g, False)

            pe.wait_ge(sem["const_ready"], 2)
            pe.wait_ge(sem["par_loaded"], 16 * 9)
            for l in range(DEPTH):
                nc.tensor.transpose(bank[4 + l][:, 0:96], par_rows[0:96, l, 0, :], ident[0:96, 0:96])
                nc.tensor.transpose(bank[4 + l][:, 128:208], par_rows[0:80, l, 1, :], ident[0:80, 0:80])
            nc.tensor.transpose(bank[4][:, 256:264], gf_row[:, :], ident[0:KD, 0:KD]).then_inc(sem["par_tr"], 1)
            pe.wait_ge(sem["in_loaded"], 16)
            for i in range(4):
                for q in range(2):
                    for c in range(NC):
                        ins = nc.tensor.transpose(bank[i][:, q * S + c * P:q * S + (c + 1) * P],
                                                  x_tok[:, c, (2 * i + q) * P:(2 * i + q + 1) * P], ident[:, :])
                ins.then_inc(sem["xtr_in"], 1)

            with nc.tensor.Fori(0, DEPTH) as lay:
                norm(lay, 0)
                norm_rows(lay, 0)
                ffn(lay, 0, 0)
                norm(lay, 1)
                norm_rows(lay, 1)
                groups(lay)
                for q in range(4):
                    weights(lay, K_GB + q)
                    pe.wait_ge(sem["act_evac"], lay * NE + (NG * GU + q + 1))
                    if q == 0:
                        pe.wait_ge(sem["zth_ready"], (lay * NG + NG) * 2)
                    feat((K_GB + q) % RING, q % 3, u_hi, u_lo)
                    if q == 0:
                        pe.wait_ge(sem["ysum_ready"], lay * NG + NG + 1)
                        for t in range(4):
                            i = mm(bank[7][:, 0:S], ones[:, :], ysum[:, t, :], start=(t == 0), stop=(t == 3))
                        i.then_inc(sem["yss_done"], 1)
                pe.wait_ge(sem["ydiag_ready"], lay + 1)
                for c in range(NC):
                    i = mm(bank[7][:, c * P:(c + 1) * P], ones[:, :], rdiag[:, c, :], start=True, stop=True)
                i.then_inc(sem["yB_done"], 1)
                with nc.tensor.Fori(0, 4) as m:
                    pe.wait_ge(sem["ha_ready"], lay * NG + NG)
                    pe.wait_ge(sem["yB_ready"], lay + 1)
                    weights(lay, m * 3 + K_MERGE)
                    pe.wait_ge(sem["merge_read"], lay * 8 + m * 2 + 1)
                    feat(K_MERGE % RING, 0, ha_hi, ha_lo)
                    pe.wait_ge(sem["yb_ready"], lay * 4 + 4)
                    pe.wait_ge(sem["merge_read"], lay * 8 + m * 2 + 2)
                    zero_bank(1)
                    for kh in range(2):
                        weights(lay, m * 3 + (K_MERGE + 1 + kh))
                        feat((K_MERGE + 1 + kh) % RING, 1, yb_hi[:, kh * KD:(kh + 1) * KD, :],
                             yb_lo[:, kh * KD:(kh + 1) * KD, :], seeded=True)
                for q in range(4):
                    weights(lay, K_OUT + q)
                    if q == 0:
                        pe.wait_ge(sem["m_lo_ready"], lay * 4 + 4)
                    if q == 3:
                        pe.wait_ge(sem["h_ready"], lay * 16 + 9)
                    feat((K_OUT + q) % RING, q % 3, u_hi, u_lo)
                pe.wait_ge(sem["p_loaded"], lay * 32 + 32)
                for k in range(2):
                    for c in range(NC):
                        i = nc.tensor.transpose(bank[3][:, k * S + c * P:k * S + (c + 1) * P],
                                                p_tok[:, c, k * P:(k + 1) * P], ident[:, :])
                i.then_inc(sem["pt_done"], 1)

                def p_project(q):
                    for m in (2 * q, 2 * q + 1):
                        for k in range(2):
                            i = mm(bank[4 + q % 2][:, (m % 2) * S:(m % 2 + 1) * S], w_ple[:, k, m * P:(m + 1) * P],
                                   p_feat[:, k, :], start=(k == 0), stop=(k == 1))
                    i.then_inc(sem["pp_done"], 1)

                pe.wait_ge(sem["pt_ready"], lay + 1)
                p_project(0)
                p_project(1)
                norm(lay, 2)
                for q in (2, 3):
                    pe.wait_ge(sem["pp_ready"], lay * 4 + q - 1)
                    p_project(q)
                norm_rows(lay, 2)
                ffn(lay, 1, K_FFN2)
                norm(lay, 3)
                norm_rows(lay, 3)
                for q in range(4):
                    weights(lay, K_PLE + q)
                    if q == 3:
                        pe.wait_ge(sem["ple_tanh"], lay * 4 + 1)
                    if q == 0:
                        feat_first(K_PLE % RING, 0, lay * 4 + 3)
                    else:
                        feat((K_PLE + q) % RING, q % 3, u_hi, u_lo)
            norm(DEPTH, 0)
            norm_rows(DEPTH, 0)
            pe.wait_ge(sem["u32_ready"], (DEPTH * 4 + 1) * KD)
            for q in range(4):
                c = q // 2
                for t in range(4):
                    k = (q % 2) * 4 + t
                    i = nc.tensor.transpose(bank[q][:, t * P:(t + 1) * P], u32[:, k, c * P:(c + 1) * P], ident[:, :])
                i.then_inc(sem["xt_done"], 1)


_INS = ["x", "p", "g_ffn1", "w1_ffn1", "w3_ffn1", "w2_ffn1", "g_mix", "w_in", "b_igate", "b_fgate", "g_mlstm_head",
        "conv_w", "conv_b", "dt_bias", "a_log", "d_skip", "g_ssm_out", "w_branch_a", "w_branch_b", "w_out", "g_ffn2",
        "w1_ffn2", "w3_ffn2", "w2_ffn2", "g_ple", "w_ple_gate", "w_ple", "g_final"]


def kernel(**inputs):
    import numpy as _np
    import concourse.bacc as _bacc
    from concourse import mybir as _mybir
    from concourse.bass_utils import run_bass_kernel_spmd as _run

    nc = _bacc.Bacc("TRN2", target_bir_lowering=False, num_devices=1)
    arrays, tensors = {}, {}
    for name in _INS:
        a = _np.ascontiguousarray(inputs[name])
        arrays[f"in_{name}_dram"] = a
        tensors[name] = nc.dram_tensor(f"in_{name}_dram", a.shape, _mybir.dt.from_np(a.dtype),
                                       kind="ExternalInput").ap()
    out = nc.dram_tensor("out_0_dram", inputs["x"].shape, _mybir.dt.float32, kind="ExternalOutput").ap()
    trunk(nc, tensors, out)
    r = _run(nc, [arrays], core_ids=[0])
    return r.results[0]["out_0_dram"]
```

```python
from contextlib import ExitStack

import concourse.bass as bass
from concourse import mybir

F32 = mybir.dt.float32
F32R = mybir.dt.float32r
BF16 = mybir.dt.bfloat16
ALU = mybir.AluOpType
ACT = mybir.ActivationFunctionType
AX_X = mybir.AxisListType.X

P = 128
EPS = 1e-6
RING = 3


def trunk(nc, T, out):
    DEPTH, D, FF = T["w1_ffn1"].shape
    S = T["x"].shape[1]
    CH = 128
    NC = S // CH
    D_IN = T["w_in"].shape[2]
    MH = T["b_igate"].shape[1]
    MV = T["g_mlstm_head"].shape[2]
    MQK = 128
    SH = T["dt_bias"].shape[1]
    SI = T["g_ssm_out"].shape[1]
    HP = SI // SH
    SCONV, CDIM = T["conv_w"].shape[1:]
    NG = 4
    EH = SH // NG
    PLE = T["p"].shape[3]
    KD = D // P
    NP = 2 * P
    FT = FF // NP
    assert NC == 2 and MH == NG and MV == 2 * P and EH * HP == 4 * P and PLE == 2 * P and S == NP
    assert D_IN == 2 * MH * MQK + 2 * MH * MV + 2 * MH + SI + CDIM + SH + 2 * D

    C_Q, C_K = 0, MH * MQK
    C_V = 2 * MH * MQK
    C_O = C_V + MH * MV
    C_IF = C_O + MH * MV
    C_Z = C_IF + 2 * MH
    C_X = C_Z + SI
    C_B = C_X + SI
    C_C = C_B + NG * P
    C_DT = C_X + CDIM
    C_G = C_DT + SH

    U_FFN = 3 * FT
    GU = 9
    BC, QK, X01, X23, V, Z0, Z1, O, GA = range(GU)
    K_MIX = U_FFN
    K_GB = K_MIX + NG * GU
    K_MERGE = K_GB + 4
    K_OUT = K_MERGE + 12
    K_FFN2 = K_OUT + 4
    K_PLE = K_FFN2 + U_FFN
    NU = K_PLE + 4
    NE = NG * GU + 4
    assert NU % RING == 0 and GU % RING == 0 and U_FFN % RING == 0 and FT % 2 == 1

    ctx = ExitStack()
    with ctx:
        top = [nc.sbuf_base + 64 if isinstance(nc.sbuf_base, int) else 1024]
        top[0] = (top[0] + 63) // 64 * 64

        def at(name, shape, dt, off):
            n = 1
            for d in shape[1:]:
                n *= d
            n *= 2 if dt == BF16 else 4
            return nc.alloc_sbuf_tensor_at(name, shape, dt, offset=off), off + (n + 31) // 32 * 32

        def sb(name, shape, dt=F32):
            t, top[0] = at(name, shape, dt, top[0])
            return t

        raw = [sb(f"w_raw{i}", [P, KD, NP]) for i in range(RING)]
        whi = [sb(f"w_hi{i}", [P, KD, NP], F32R) for i in range(RING)]
        wlo = [sb(f"w_lo{i}", [P, KD, NP], F32R) for i in range(RING)]
        h = sb("h", [P, KD, S])
        u_hi = sb("u_hi", [P, KD, S], F32R)
        u_lo = sb("u_lo", [P, KD, S], F32R)
        gate_a = sb("gate_a", [P, KD, S])
        ha_hi = sb("ha_hi", [P, 2 * MH, S], F32R)
        ha_lo = sb("ha_lo", [P, 2 * MH, S], F32R)
        y_feat = sb("y_feat", [P, SI // P, S])
        U_HI, U_LO = (u_hi, u_hi, ha_hi, ha_hi), (u_lo, u_lo, ha_lo, ha_lo)
        w_ple = y_feat[:, 0:8, :].rearrange("p a b -> p (a b)").rearrange("p (k m) -> p k m", k=2)
        p_proj = y_feat[:, 8:16, :]
        hg = y_feat[:, 0:8, :]
        p_tok = gate_a[:, 0:2, :]
        p_feat = gate_a[:, 2:4, :]

        ident = sb("ident", [P, P])
        tri_le = sb("tri_le", [P, P])
        tri_gt = sb("tri_gt", [P, P])
        ones = sb("ones", [P, P])
        tri_gt_r = sb("tri_gt_r", [P, P], F32R)
        ones_r = sb("ones_r", [P, P], F32R)
        zeros = sb("zeros", [P, P], BF16)
        m_half = sb("m_half", [P, 1])
        par_all = sb("par_all", [P, DEPTH, 176])
        par = sb("par", [P, 176])
        g_fin = sb("g_fin", [P, KD])
        row_all = sb("row_all", [P, DEPTH, 104])
        wsm = sb("wsm", [P, KD, 40])
        pre = sb("pre", [P, NC, 40])
        spx = sb("spx", [P, NC, 36])
        sp_a = sb("sp_a", [P, NC, 36])
        sp_b = sb("sp_b", [P, NC, 36])
        sp_c = sb("sp_c", [P, NC, 36])
        dA = sb("dA", [P, NC, SH])
        dA_hi = sb("dA_hi", [P, NC, SH], F32R)
        dA_lo = sb("dA_lo", [P, NC, SH], F32R)
        e_a = sb("e_a", [P, SH])
        dcol = sb("dcol", [P, SI // P])
        w_end = sb("w_end", [P, SH])
        tokc = sb("tokc", [P, 6, MH])
        M4 = sb("M4", [MH, MH, S])
        gcw = sb("gcw", [P, SCONV, 6])
        gcb = sb("gcb", [P, 6])
        gdk = sb("gdk", [P, 4])
        m_start = sb("m_start", [MH, 1])
        ghn = sb("ghn", [P, 2])
        gtk = sb("gtk", [P, 6])
        var = sb("var", [P, NC])
        rms = sb("rms", [P, NC])
        rdiag = sb("rdiag", [P, NC, P])
        mdiag = rdiag
        rB = sb("rB", [P, S])
        den = sb("den", [P, 2])
        rden = sb("rden", [P, 2])
        nss = sb("nss", [P, 2])
        hvar = sb("hvar", [P, 2])
        hrms = sb("hrms", [P, 2])
        hsc = sb("hsc", [P, 2])

        base = top[0]
        a = base
        seg, a = at("seg", [P, NC, EH, P], F32, a)
        xcv, a = at("xcv", [P, 4, S], F32, a)
        bcv, a = at("bcv", [P, 2, S], F32, a)
        R, _ = at("R", [P, 2, 2, 2, P], F32R, a)
        cs, a = at("cs", [P, EH, P], F32, a)
        qT, a = at("qT", [P, S], F32, a)
        kT, a = at("kT", [P, S], F32, a)
        pm, a = at("pm", [P, NC, P], F32, a)
        scT, a = at("scT", [P, NC, P], F32, a)
        cth, a = at("cth", [P, 2, S], F32, a)
        late = a
        xw, a = at("xw", [P, NC, EH * HP], F32, a)
        xwe, a = at("xwe", [P, EH * HP], F32, a)
        zs, a = at("zs", [P, 4, S], F32, a)
        num, a = at("num", [P, NC, 258], F32, a)
        osg, a = at("osg", [P, 2, S], F32, a)
        late_end = a
        st, a = at("st", [P, EH * HP], F32, a)
        xin, a = at("xin", [P, 2, 2, S + 3], F32, a)
        zth, a = at("zth", [P, 2, S], F32, a)
        vtok, a = at("vtok", [P, NC, 258], F32, a)
        ktok, a = at("ktok", [P, P], F32, a)
        cst, a = at("cst", [P, 258], F32, a)
        inter = cst
        cbm, a = at("cbm", [P, NC, P], F32, a)
        btok, a = at("btok", [P, P], F32, a)
        ysum, a = at("ysum", [P, 4, S], F32, a)
        a2 = base
        yb_hi, a2 = at("yb_hi", [P, SI // P, S], F32R, a2)
        yb_lo, a2 = at("yb_lo", [P, SI // P, S], F32R, a2)
        gate_b, a2 = at("gate_b", [P, KD, S], F32, a2)
        mtmp, a2 = at("mtmp", [P, 2, S], F32, a2)
        mrg, a2 = at("mrg", [P, 2, S], F32, a2)
        a3 = base
        sq, a3 = at("sq", [P, KD, S], F32, a3)
        sa, a3 = at("sa", [P, 2, S], F32, a3)
        h1f, a3 = at("h1f", [P, 2, S], F32, a3)
        x_tok, _ = at("x_tok", [P, NC, D], F32, a3)
        h1_hi, h1_lo = [None] * 2, [None] * 2
        for b in range(2):
            h1_hi[b], a3 = at(f"h1_hi{b}", [P, 2, S], F32R, a3)
            h1_lo[b], a3 = at(f"h1_lo{b}", [P, 2, S], F32R, a3)
        a4 = base + 4 * KD * S
        par_rows, a4 = at("par_rows", [P, DEPTH, 2, P], F32, a4)
        row_one, a4 = at("row_one", [1, DEPTH, 104], F32, a4)
        gf_row, a4 = at("gf_row", [KD, P], F32, a4)
        a5 = late
        wsm_hi, a5 = at("wsm_hi", [P, KD, 40], F32R, a5)
        wsm_lo, a5 = at("wsm_lo", [P, KD, 40], F32R, a5)
        pre_row, a5 = at("pre_row", [40, S], F32, a5)
        r_i, a5 = at("r_i", [MH, S], F32, a5)
        r_f, a5 = at("r_f", [MH, S], F32, a5)
        r_b, a5 = at("r_b", [MH, S], F32, a5)
        r_w, a5 = at("r_w", [MH, S], F32, a5)
        r_m, a5 = at("r_m", [MH, S], F32, a5)
        r_x, a5 = at("r_x", [MH, 6, P], F32, a5)
        assert a5 <= late_end
        top_all = max(a, a2, a3, a4, a5)
        assert top_all <= nc.sbuf_usable_end

        bank = [ctx.enter_context(nc.psum_tensor(f"bank{i}", [P, 512], F32)) for i in range(8)]

        def two(b):
            return bank[b][:, :].rearrange("p (m s) -> p m s", m=2)

        names = """hg_ready fin_act sq_added rB_ready up_scaled gated z_tanh o_tanh gate_tanh evac par_ready ple_scaled rdiag_ready rB_done ydiag_ready yB_done yB_ready wsm_hi_ready wsm_ready pre_row_ready pre_ready down_done acs_exp cs_ready y_done ysum_ready
            gtk_ready w_raw0 w_raw1 w_raw2 w_hi w_lo unit_done const_ready in_loaded par_loaded
            wsm_loaded p_loaded out_stored rows_done par_tr h_ready sq_ready ss_done var_ready rms_ready
             u_hi_ready u_lo_ready silu_done prod_done h1_hi_ready h1_ready small_done x_abs sp_exp
            dA_ready ea_ready cum_done cum_exp row_tr row_ready row_back tok_ready r_built seg_done exp_done
            conv_done tanh_done cv_ready scores_done d_ready p_exp pm_ready sct_ready cb_done cbm_done
            btok_ready m_ready xtr_done xw_ready heads_done cst_ready num0_ready yi_done im_done st_ready
            inter_ready num1_ready nsq_ready hvar_ready hrms_ready hn_ready hnT_done y_ready zth_ready
            ha32_ready ha_hi_ready ha_ready group_ready group_free ysq_ready yb_hi_ready yb_ready yss_done
            yvar_ready yrms_ready merge_read mrg_ready m_hi_ready m_lo_ready ple_tanh pt_done pt_ready pp_done
            pp_ready xt_done fin_done row_bcast dve_chain pool_chain xtr_in""".split()
        sem = {n: ctx.enter_context(nc.semaphore(n)) for n in names}
        w_raw = [sem["w_raw0"], sem["w_raw1"], sem["w_raw2"]]
        block = ctx.enter_context(nc.Block())

        class Chain:

            def __init__(self, eng, s):
                self.eng, self.s, self.n = eng, s, 0

            def add(self, ins):
                ins.then_inc(self.s, 1)
                self.n += 1

            def wait(self):
                if self.n:
                    self.eng.wait_ge(self.s, self.n)

            def clear(self):
                if self.n:
                    self.eng.wait_ge(self.s, self.n)
                    self.eng.sem_clear(self.s)
                self.n = 0

        @block.sync
        def _(sp):
            def load(k, slot, src, dst, lay):
                sp.wait_ge(sem["w_lo"], lay * NU + k + 1)
                n = src.shape[1] // 2
                sp.dma_start(dst[:, 0:n], src[:, 0:n]).then_inc(w_raw[slot], 16)
                sp.dma_start(dst[:, n:], src[:, n:]).then_inc(w_raw[slot], 16)

            def cols(w, lay, c0, slot):
                src = w[lay].rearrange("(k p) m -> p k m", p=P)[:, :, c0:c0 + NP]
                return src, raw[slot][:, :, :]

            def dcols(w, lay, c0, slot):
                src = w[lay].rearrange("(k p) m -> p k m", p=P)[:, :, bass.ds(c0, NP)]
                return src, raw[slot][:, :, :]

            def rows2(w, lay, j, slot):
                src = w[lay, bass.ds(j * NP, NP), :].rearrange("(k p) m -> p k m", p=P)
                return src, raw[slot][:, :, :].rearrange("p a b -> p (a b)").rearrange("p (k m) -> p k m", k=2)

            def ffn(k0, w1, w3, w2, lay):
                s = k0 % RING
                load(k0, s, *cols(w1, lay, 0, s), lay)
                s = (k0 + 1) % RING
                load(k0 + 1, s, *cols(w3, lay, 0, s), lay)
                with nc.sync.Fori(0, FT - 1) as j:
                    a, b, c = [(k0 + 2 + r) % RING for r in range(3)]
                    load(k0 + 2 + j * 3, a, *dcols(w1, lay, (j + 1) * NP, a), lay)
                    load(k0 + 3 + j * 3, b, *dcols(w3, lay, (j + 1) * NP, b), lay)
                    load(k0 + 4 + j * 3, c, *rows2(w2, lay, j, c), lay)
                s = (k0 + U_FFN - 1) % RING
                load(k0 + U_FFN - 1, s, *rows2(w2, lay, FT - 1, s), lay)

            W = T["w_in"]
            sp.dma_start(x_tok[:, :, :], T["x"][0].rearrange("(c t) d -> t c d", t=P)).then_inc(sem["in_loaded"], 16)
            with nc.sync.Fori(0, DEPTH) as lay:
                ffn(0, T["w1_ffn1"], T["w3_ffn1"], T["w2_ffn1"], lay)
                with nc.sync.Fori(0, NG) as g:
                    def two_cols(p, ca):
                        s = (K_MIX + p) % RING
                        wv = W[lay].rearrange("(k p) m -> p k m", p=P)
                        sp.wait_ge(sem["w_lo"], lay * NU + g * GU + (K_MIX + p + 1))
                        sp.dma_start(raw[s][:, :, 0:P], wv[:, :, bass.ds(ca, P)]).then_inc(w_raw[s], 16)
                        sp.dma_start(raw[s][:, :, P:NP], wv[:, :, bass.ds(ca + NG * P, P)]).then_inc(w_raw[s], 16)

                    def one(p, c):
                        s = (K_MIX + p) % RING
                        load(K_MIX + g * GU + p, s, *dcols(W, lay, c, s), lay)

                    two_cols(BC, g * P + C_B)
                    two_cols(QK, g * P + C_Q)
                    one(X01, g * (4 * P) + C_X)
                    one(X23, g * (4 * P) + C_X + NP)
                    one(V, g * NP + C_V)
                    one(Z0, g * (4 * P) + C_Z)
                    one(Z1, g * (4 * P) + C_Z + NP)
                    one(O, g * NP + C_O)
                    one(GA, g * NP + C_G)
                for i in range(4):
                    s = (K_GB + i) % RING
                    load(K_GB + i, s, *cols(W, lay, C_G + D + i * NP, s), lay)
                with nc.sync.Fori(0, 4) as m:
                    s = K_MERGE % RING
                    load(K_MERGE + m * 3, s, *dcols(T["w_branch_a"], lay, m * NP, s), lay)
                    for kh in range(2):
                        s = (K_MERGE + 1 + kh) % RING
                        src = T["w_branch_b"][lay, kh * D:(kh + 1) * D, :].rearrange("(k p) m -> p k m", p=P)
                        load(K_MERGE + 1 + kh + m * 3, s, src[:, :, bass.ds(m * NP, NP)], raw[s][:, :, :], lay)
                for i in range(4):
                    s = (K_OUT + i) % RING
                    load(K_OUT + i, s, *cols(T["w_out"], lay, i * NP, s), lay)
                ffn(K_FFN2, T["w1_ffn2"], T["w3_ffn2"], T["w2_ffn2"], lay)
                for i in range(4):
                    s = (K_PLE + i) % RING
                    load(K_PLE + i, s, *cols(T["w_ple_gate"], lay, i * NP, s), lay)
            sp.wait_ge(sem["fin_done"], 2)
            sp.dma_start(out[0, P:2 * P], x_tok[:, 1, :]).then_inc(sem["out_stored"], 16)
            sp.wait_ge(sem["out_stored"], 32)

        @block.gpsimd
        def _(pool):
            g_ = nc.gpsimd
            ch = Chain(pool, sem["pool_chain"])
            ch.add(g_.memset(ident[:, :], 0.0))
            ch.add(g_.memset(ones[:, :], 1.0))
            ch.add(g_.memset(m_half[:, :], -0.5))
            ch.wait()
            ch.add(g_.affine_select(out=ident[:, :], in_=ident[:, :], compare_op=ALU.not_equal, fill=1.0,
                                    base=0, pattern=[[-1, P]], channel_multiplier=1))
            ch.add(g_.affine_select(out=tri_le[:, :], in_=ones[:, :], compare_op=ALU.is_ge, fill=0.0,
                                    base=0, pattern=[[1, P]], channel_multiplier=-1))
            g_.affine_select(out=tri_gt[:, :], in_=ones[:, :], compare_op=ALU.is_gt, fill=0.0,
                             base=0, pattern=[[-1, P]], channel_multiplier=1).then_inc(sem["const_ready"], 1)
            pool.wait_ge(sem["rows_done"], 16 * 5)
            g_.partition_broadcast(row_all[:, :, :].rearrange("p a b -> p (a b)"),
                                   row_one[0:1, :, :].rearrange("p a b -> p (a b)")).then_inc(sem["row_bcast"], 1)
            ch.add(g_.memset(ysum[:, :, :], 0.0))
            ch.clear()

            def power(n, ready, src, done, dst):
                pool.wait_ge(sem[ready], n)
                g_.tensor_tensor(dst, src, m_half[:, :].broadcast_to([P, dst.shape[1]]), ALU.pow).then_inc(sem[done], 1)

            def row_norm(n, final=False):
                for i in range(0 if final else 1, 0 if final else 4):
                    pool.wait_ge(sem["sq_ready"], n * 4 + (i - 3))
                    if i > 1:
                        pool.wait_ge(sem["sq_added"], n * 3 + (i - 4))
                    g_.tensor_tensor(sq[:, 0:2, :], sq[:, 0:2, :], sq[:, 2 * i:2 * i + 2, :], ALU.add)\
                        .then_inc(sem["sq_added"], 1)
                power(n, "var_ready", var[:, :], "rms_ready", rms[:, :])

            def ffn(lay, f):
                with nc.gpsimd.Fori(0, FT) as j:
                    pool.wait_ge(sem["silu_done"], (lay * 2 + f) * FT + j + 1)
                    g_.tensor_tensor(sa[:, :, :], sa[:, :, :], rB[:, :].unsqueeze(1).broadcast_to([P, 2, S]),
                                     ALU.mult).then_inc(sem["gated"], 1)

            with nc.gpsimd.Fori(0, DEPTH) as lay:
                row_norm(lay * 4 + 1)
                ffn(lay, 0)
                row_norm(lay * 4 + 2)
                with nc.gpsimd.Fori(0, NG) as g:
                    G = pool.snap(lay * NG + g)
                    pool.wait_ge(sem["group_free"], G + 1)
                    cw = par[:, 0:SCONV * 24].rearrange("p (j t) -> p j t", j=SCONV)
                    g_.tensor_copy(gcw[:, :, 2:6], cw[:, :, bass.ds(g * 4, 4)])
                    for b in range(2):
                        g_.tensor_copy(gcw[:, :, b:b + 1], cw[:, :, bass.ds(g + 16 + 4 * b, 1)])
                        g_.tensor_copy(gcb[:, b:b + 1], par[:, bass.ds(g + 96 + 16 + 4 * b, 1)])
                    g_.tensor_copy(gcb[:, 2:6], par[:, bass.ds(g * 4 + 96, 4)])
                    g_.tensor_copy(gdk[:, :], dcol[:, bass.ds(g * 4, 4)])
                    g_.tensor_copy(ghn[:, :], par[:, bass.ds(g * 2 + 136, 2)]).then_inc(sem["group_ready"], 1)
                    for c in range(NC):
                        for b in range(4):
                            if c == b == 0:
                                pool.wait_ge(sem["dA_ready"], lay + 1)
                            pool.wait_ge(sem["seg_done"], G * 8 + (4 * c + b + 1))
                            for q, part in enumerate((dA_hi, dA_lo)):
                                i = g_.tensor_tensor(
                                    R[:, b % 2, q, :, :], tri_le[:, :].unsqueeze(1).broadcast_to([P, 2, P]),
                                    part[:, c, bass.ds(g * EH + 2 * b, 2)].bitcast(F32).unsqueeze(2).broadcast_to([P, 2, P]),
                                    ALU.mult)
                            i.then_inc(sem["r_built"], 1)
                        if c == 0:
                            pool.wait_ge(sem["tok_ready"], lay * 2 + 2)
                            g_.tensor_copy(gtk[:, :].unsqueeze(2), tokc[:, :, bass.ds(g, 1)]).then_inc(sem["gtk_ready"], 1)
                    pool.wait_ge(sem["p_exp"], G + 1)
                    g_.tensor_tensor(pm[:, :, :], pm[:, :, :], tri_le[:, :].unsqueeze(1).broadcast_to([P, NC, P]),
                                     ALU.mult).then_inc(sem["pm_ready"], 1)
                    pool.wait_ge(sem["cbm_done"], G + 1)
                    for c in range(NC):
                        pool.wait_ge(sem["exp_done"], G * 4 + (2 * c + 2))
                        g_.tensor_tensor(seg[:, c, :, :], seg[:, c, :, :],
                                         cbm[:, c, :].unsqueeze(1).broadcast_to([P, EH, P]), ALU.mult)\
                            .then_inc(sem["m_ready"], 1)
                    pool.wait_ge(sem["acs_exp"], G * 2 + 2)
                    g_.tensor_tensor(cs[:, :, :], cs[:, :, :], bcv[:, 1, P:2 * P].unsqueeze(1).broadcast_to([P, EH, P]),
                                     ALU.mult).then_inc(sem["cs_ready"], 1)
                    power(G + 1, "hvar_ready", hvar[:, :], "hrms_ready", hrms[:, :])
                    pool.wait_ge(sem["ysq_ready"], G + 1)
                    g_.tensor_tensor(ysum[:, :, :], ysum[:, :, :], zs[:, :, :], ALU.add).then_inc(sem["ysum_ready"], 1)
                power(lay + 1, "yvar_ready", var[:, :], "yrms_ready", rms[:, :])
                row_norm(lay * 4 + 3)
                g_.memset(ysum[:, :, :], 0.0)
                ffn(lay, 1)
                row_norm(lay * 4 + 4)
            row_norm(DEPTH * 4 + 1, final=True)

        @block.scalar
        def _(act):
            a_ = nc.scalar
            act.dma_start(par_rows[0:96, :, 0, :],
                          T["conv_w"].rearrange("l j (t c) -> (j t) l c", c=P)).then_inc(sem["par_loaded"], 16)
            r0 = 0
            for n, w in ((24, T["conv_b"]), (16, T["g_ssm_out"]), (8, T["g_mlstm_head"].rearrange("l h v -> l (h v)")),
                         (8, T["g_ffn1"]), (8, T["g_mix"]), (8, T["g_ffn2"]), (8, T["g_ple"])):
                act.dma_start(par_rows[r0:r0 + n, :, 1, :],
                              w.rearrange("l (t c) -> t l c", c=P)).then_inc(sem["par_loaded"], 16)
                r0 += n
            act.dma_start(gf_row[:, :], T["g_final"].rearrange("(t c) -> t c", c=P)).then_inc(sem["par_loaded"], 16)
            r0 = 0
            for w in (T["b_igate"], T["b_fgate"], T["dt_bias"], T["a_log"], T["d_skip"]):
                n = w.shape[1]
                act.dma_start(row_one[0:1, :, r0:r0 + n], w.unsqueeze(0)).then_inc(sem["rows_done"], 16)
                r0 += n

            def hi(lay, k, k3, slot):
                act.wait_ge(w_raw[slot], (lay * (NU // RING) + k3 + 1) * 32)
                act.wait_ge(sem["unit_done"], lay * NU + k + 1)
                a_.activation(whi[slot][:, :, :], raw[slot][:, :, :], ACT.Copy).then_inc(sem["w_hi"], 1)

            def shi(lay, k):
                if k < NU:
                    hi(lay, k, k // RING, k % RING)

            def norm(lay, n, i):
                N = lay * 4 + n
                act.wait_ge(sem["h_ready"], N * 4 + (i + 1))
                if n < 4:
                    for k in (2 * i, 2 * i + 1):
                        a_.activation(U_HI[n][:, k, :], h[:, k, :], ACT.Copy,
                                      scale=par[:, 144 + 8 * n + k:145 + 8 * n + k]).then_inc(sem["u_hi_ready"], 1)
                a_.activation(sq[:, 2 * i:2 * i + 2, :], h[:, 2 * i:2 * i + 2, :],
                              ACT.Square).then_inc(sem["sq_ready"], 1)

            def row_scale(lay, n):
                act.wait_ge(sem["rB_done"], lay * 4 + n + 1)
                a_.activation(rB[:, :], bank[6][:, S:2 * S], ACT.Copy).then_inc(sem["rB_ready"], 1)

            def ffn(lay, f, k0):
                F = lay * 2 + f
                shi(lay, k0 + 2)
                shi(lay, k0 + 3)
                row_scale(lay, 2 * f)
                act.wait_ge(sem["up_scaled"], F * FT + 1)
                a_.activation(sa[:, :, :], sa[:, :, :], ACT.Silu).then_inc(sem["silu_done"], 1)
                act.wait_ge(sem["prod_done"], F * FT + 1)
                a_.activation(h1_hi[0][:, :, :], h1f[:, :, :], ACT.Copy).then_inc(sem["h1_hi_ready"], 1)
                with nc.scalar.Fori(0, (FT - 1) // 2) as jj:
                    for b in range(2):
                        j = jj * 2 + b

                        def sh(r):
                            k = k0 + 4 + 3 * b + r
                            hi(lay, k + jj * 6, k // RING + jj * 2, k % RING)

                        sh(0)
                        act.wait_ge(sem["up_scaled"], F * FT + j + 2)
                        a_.activation(sa[:, :, :], sa[:, :, :], ACT.Silu).then_inc(sem["silu_done"], 1)
                        sh(1)
                        act.wait_ge(sem["prod_done"], F * FT + j + 2)
                        a_.activation(h1_hi[1 - b][:, :, :], h1f[:, :, :], ACT.Copy).then_inc(sem["h1_hi_ready"], 1)
                        sh(2)
                shi(lay, k0 + U_FFN + 1)

            def groups(lay):
                def body(g, first):
                    G = act.snap(lay * NG + g)

                    def step(p):
                        k = K_MIX + p + 2
                        hi(lay, g * GU + k, g * (GU // RING) + k // RING, k % RING)

                    def scaled(p):
                        act.wait_ge(sem["evac"], lay * NE + g * GU + (p + RING + 1))

                    def tanh_conv(i, dst):
                        act.wait_ge(sem["conv_done"], G * 3 + (i + 1))
                        a_.activation(cth[:, :, :], dst, ACT.Tanh).then_inc(sem["tanh_done"], 1)

                    def decay(c):
                        for b in range(2):
                            act.wait_ge(sem["seg_done"], G * 8 + (4 * c + 2 * b + 4))
                            a_.activation(seg[:, c, 4 * b:4 * b + 4, :],
                                          bank[4 + 2 * c + b][:, :].rearrange("p (e t) -> p e t", e=4),
                                          ACT.Exp).then_inc(sem["exp_done"], 1)

                    def decay_from_start():
                        for b in range(2):
                            act.wait_ge(sem["seg_done"], G * 8 + 10)
                            a_.activation(cs[:, 4 * b:4 * b + 4, :], bank[4 + b][:, :].rearrange("p (e t) -> p e t", e=4),
                                          ACT.Exp).then_inc(sem["acs_exp"], 1)

                    def score_exp():
                        act.wait_ge(sem["d_ready"], G + 1)
                        a_.activation(pm[:, :, :], pm[:, :, :], ACT.Exp, scale=-1.0).then_inc(sem["p_exp"], 1)

                    step(0)
                    step(1)
                    if first:
                        row_scale(lay, 1)
                    tanh_conv(0, bcv[:, :, :])
                    if first:
                        act.wait_ge(sem["x_abs"], lay + 1)
                        a_.activation(sp_b[:, :, :], sp_a[:, :, :], ACT.Exp, scale=-1.0).then_inc(sem["sp_exp"], 1)
                        act.wait_ge(sem["row_bcast"], 1)
                        a_.activation(e_a[:, :], row_all[:, lay, 40:72], ACT.Exp).then_inc(sem["ea_ready"], 1)
                    step(2)
                    if not first:
                        decay(0)
                    step(3)
                    if first:
                        act.wait_ge(sem["cum_done"], lay + 1)
                        a_.activation(w_end[:, :], bank[7][:, 0:SH], ACT.Exp).then_inc(sem["cum_exp"], 1)
                        decay(0)
                        act.wait_ge(sem["row_back"], lay + 1)
                        tk = bank[6][:, 0:24].rearrange("p (a h) -> p a h", a=6)
                        a_.activation(tokc[:, 0:2, :], tk[:, 0:2, :], ACT.Copy).then_inc(sem["tok_ready"], 1)
                        a_.activation(tokc[:, 2:6, :], tk[:, 2:6, :], ACT.Exp).then_inc(sem["tok_ready"], 1)
                        tanh_conv(1, xcv[:, 0:2, :])
                    else:
                        tanh_conv(1, xcv[:, 0:2, :])
                        score_exp()
                        decay(1)
                        decay_from_start()
                    step(4)
                    if first:
                        score_exp()
                    tanh_conv(2, xcv[:, 2:4, :])
                    if first:
                        decay(1)
                        decay_from_start()
                    act.wait_ge(sem["gtk_ready"], G + 1)
                    act.wait_ge(sem["cbm_done"], G + 1)
                    a_.activation(ktok[:, :], bank[5][:, 384:512], ACT.Copy, scale=gtk[:, 5:6])
                    a_.activation(btok[:, :], bank[5][:, 256:384], ACT.Copy).then_inc(sem["btok_ready"], 1)
                    step(5)
                    scaled(Z0)
                    a_.activation(zth[:, :, :], zs[:, 0:2, :], ACT.Tanh, scale=0.5).then_inc(sem["z_tanh"], 1)
                    step(6)
                    act.wait_ge(sem["heads_done"], G + 1)
                    a_.activation(cst[:, 0:257], bank[3][:, 0:257], ACT.Copy).then_inc(sem["cst_ready"], 1)
                    a_.activation(num[:, 0, 0:257], bank[4][:, 0:257], ACT.Copy).then_inc(sem["num0_ready"], 1)
                    step(7)
                    scaled(Z1)
                    act.wait_ge(sem["zth_ready"], G * 2 + 1)
                    a_.activation(zth[:, :, :], zs[:, 2:4, :], ACT.Tanh, scale=0.5).then_inc(sem["z_tanh"], 1)
                    act.wait_ge(sem["im_done"], G + 1)
                    a_.activation(inter[:, 0:257], bank[3][:, 0:257], ACT.Copy, scale=gtk[:, 4:5]).then_inc(sem["inter_ready"], 1)
                    act.wait_ge(sem["yi_done"], G + 1)
                    a_.activation(st[:, :], bank[4][:, :], ACT.Copy).then_inc(sem["st_ready"], 1)
                    act.wait_ge(sem["num1_ready"], G + 1)
                    for c in range(NC):
                        squares = (pm, scT)[c][:, :, :].rearrange("p a b -> p (a b)")
                        i = a_.activation(squares, num[:, c, 0:MV], ACT.Square, accum_out=nss[:, c:c + 1])
                    i.then_inc(sem["nsq_ready"], 1)
                    step(8)
                    scaled(O)
                    a_.activation(osg[:, :, :], osg[:, :, :], ACT.Tanh, scale=0.5).then_inc(sem["o_tanh"], 1)
                    act.wait_ge(sem["ha32_ready"], G + 1)
                    a_.activation(ha_hi[:, bass.ds(g * 2, 2), :], osg[:, :, :], ACT.Copy).then_inc(sem["ha_hi_ready"], 1)
                    act.wait_ge(sem["y_ready"], G + 1)
                    a_.activation(zs[:, :, :], y_feat[:, bass.ds(g * 4, 4), :], ACT.Square).then_inc(sem["ysq_ready"], 1)
                    scaled(GA)
                    a_.activation(gate_a[:, bass.ds(g * 2, 2), :], gate_a[:, bass.ds(g * 2, 2), :], ACT.Tanh,
                                  scale=0.5).then_inc(sem["gate_tanh"], 1)

                body(0, True)
                with nc.scalar.Fori(1, NG) as g:
                    body(g, False)

            with nc.scalar.Fori(0, DEPTH) as lay:
                shi(lay, 0)
                act.wait_ge(sem["par_ready"], lay + 1)
                for i in range(4):
                    norm(lay, 0, i)
                shi(lay, 1)
                act.dma_start(wsm[:, :, 0:8], T["w_in"][lay].rearrange("(k p) m -> p k m", p=P)[:, :, C_IF:C_IF + 8],
                              ).then_inc(sem["wsm_loaded"], 16)
                act.dma_start(wsm[:, :, 8:40], T["w_in"][lay].rearrange("(k p) m -> p k m", p=P)[:, :, C_DT:C_DT + SH],
                              ).then_inc(sem["wsm_loaded"], 16)
                ffn(lay, 0, 0)
                for i in range(4):
                    norm(lay, 1, i)
                act.wait_ge(sem["wsm_loaded"], lay * 32 + 32)
                a_.activation(wsm_hi[:, :, :], wsm[:, :, :], ACT.Copy).then_inc(sem["wsm_hi_ready"], 1)
                groups(lay)
                act.wait_ge(sem["group_free"], lay * NG + NG + 1)
                act.wait_ge(sem["ysum_ready"], lay * NG + NG + 1)
                for q in range(4):
                    shi(lay, K_GB + q + 2)
                    for t in range(4 * q, 4 * q + 4):
                        i = a_.activation(yb_hi[:, t, :], y_feat[:, t, :], ACT.Copy, scale=par[:, 120 + t:121 + t])
                    i.then_inc(sem["yb_hi_ready"], 1)
                    act.wait_ge(sem["evac"], lay * NE + (NG * GU + q + RING + 1))
                    a_.activation(gate_b[:, 2 * q:2 * q + 2, :], gate_b[:, 2 * q:2 * q + 2, :], ACT.Tanh, scale=0.5)\
                        .then_inc(sem["gate_tanh"], 1)
                act.wait_ge(sem["yB_done"], lay + 1)
                a_.activation(rB[:, :], bank[7][:, 0:S], ACT.Copy).then_inc(sem["yB_ready"], 1)
                with nc.scalar.Fori(0, 4) as m:
                    for r in range(3):
                        k = K_MERGE + r + 2
                        hi(lay, m * 3 + k, m + k // RING, k % RING)
                    act.wait_ge(sem["mrg_ready"], lay * 4 + m + 1)
                    a_.activation(u_hi[:, bass.ds(m * 2, 2), :], mrg[:, :, :], ACT.Copy).then_inc(sem["m_hi_ready"], 1)
                act.wait_ge(sem["m_lo_ready"], lay * 4 + 4)
                act.dma_start(w_ple, T["w_ple"][lay].rearrange("(k p) m -> p k m", p=P)).then_inc(sem["p_loaded"], 16)
                act.dma_start(p_tok, T["p"][lay, 0].rearrange("(c t) d -> t c d", t=P)).then_inc(sem["p_loaded"], 16)
                for q in range(4):
                    shi(lay, K_OUT + q + 2)
                    if q:
                        norm(lay, 2, q - 1)
                act.wait_ge(sem["pt_done"], lay + 1)
                a_.activation(p_feat, two(3), ACT.Copy).then_inc(sem["pt_ready"], 1)
                norm(lay, 2, 3)
                for q in range(4):
                    act.wait_ge(sem["pp_done"], lay * 4 + q + 1)
                    a_.activation(p_proj[:, 2 * q:2 * q + 2, :], two(4 + q % 2), ACT.Copy).then_inc(sem["pp_ready"], 1)
                ffn(lay, 1, K_FFN2)
                for i in range(4):
                    norm(lay, 3, i)
                shi(lay, K_PLE + 2)
                shi(lay, K_PLE + 3)
                row_scale(lay, 3)
                for q in range(4):
                    act.wait_ge(sem["ple_scaled"], lay * 4 + q + 1)
                    t = (sa, h1f)[q % 2][:, :, :]
                    a_.activation(t, t, ACT.Tanh, scale=0.5).then_inc(sem["ple_tanh"], 1)
            for i in range(4):
                norm(DEPTH - 1, 4, i)
            act.wait_ge(sem["rms_ready"], DEPTH * 4 + 1)
            act.wait_ge(sem["xt_done"], 4)
            for q in (0, 1):
                a_.activation(x_tok[:, 0, q * 512:(q + 1) * 512], bank[q][:, :], ACT.Copy,
                              scale=rms[:, 0:1]).then_inc(sem["fin_act"], 1)
            act.wait_ge(sem["fin_act"], 2)
            act.dma_start(out[0, 0:P], x_tok[:, 0, :]).then_inc(sem["out_stored"], 16)

        @block.vector
        def _(dve):
            v_ = nc.vector
            ch = Chain(dve, sem["dve_chain"])
            dve.sem_inc(sem["w_lo"], RING)
            dve.sem_inc(sem["unit_done"], RING)
            dve.sem_inc(sem["evac"], RING)
            dve.sem_inc(sem["seg_done"], 2)
            dve.sem_inc(sem["group_free"], 1)
            dve.sem_inc(sem["merge_read"], 2)
            dve.sem_inc(sem["ysum_ready"], 1)
            v_.memset(zeros[:, :], 0.0).then_inc(sem["const_ready"], 1)

            def lo(lay, k, slot):
                dve.wait_ge(sem["w_hi"], lay * NU + k + 1)
                v_.tensor_tensor(wlo[slot][:, :, :], raw[slot][:, :, :], whi[slot][:, :, :].bitcast(F32),
                                 ALU.subtract).then_inc(sem["w_lo"], 1)

            def slo(lay, k):
                if k < NU:
                    lo(lay, k, k % RING)

            def done(lay, k):
                dve.wait_ge(sem["unit_done"], lay * NU + k + (RING + 1))

            def scale_column(sums, scale, ready):
                for c in range(NC):
                    ch.add(v_.scalar_tensor_tensor(out=mdiag[:, c, :], in0=sums[:, c * P:(c + 1) * P], scalar=scale,
                                                   in1=ident[:, :], op0=ALU.mult, op1=ALU.mult,
                                                   accum_out=var[:, c:c + 1]))
                ch.wait()
                v_.tensor_scalar(var[:, :], var[:, :], EPS, None, ALU.add).then_inc(sem[ready], 1)

            def scale_diagonal(ready):
                for c in range(NC):
                    i = v_.tensor_scalar(rdiag[:, c, :], ident[:, :], rms[:, c:c + 1], None, ALU.mult)
                i.then_inc(sem[ready], 1)

            def low(lay, n, i):
                N = lay * 4 + n
                for k in (2 * i, 2 * i + 1):
                    dve.wait_ge(sem["u_hi_ready"], N * KD + (k + 1))
                    v_.scalar_tensor_tensor(out=U_LO[n][:, k, :], in0=h[:, k, :], scalar=par[:, 144 + 8 * n + k:145 + 8 * n + k],
                                            in1=U_HI[n][:, k, :].bitcast(F32), op0=ALU.mult, op1=ALU.subtract)\
                        .then_inc(sem["u_lo_ready"], 1)

            def row_scale(lay, n):
                N = lay * 4 + n
                dve.wait_ge(sem["ss_done"], N + 1)
                scale_column(bank[6], 1.0 / D, "var_ready")
                dve.wait_ge(sem["rms_ready"], N + 1)
                scale_diagonal("rdiag_ready")
            def by_token(x):
                return x.unsqueeze(1).broadcast_to([P, 2, S])

            def ffn(lay, f, k0):
                F = lay * 2 + f

                def scale_up(done_value):
                    dve.wait_ge(sem["unit_done"], done_value)
                    v_.tensor_tensor(sa[:, :, :], two(4), by_token(rB[:, :]), ALU.mult).then_inc(sem["up_scaled"], 1)

                def product(done_value, gated_value):
                    dve.wait_ge(sem["unit_done"], done_value)
                    dve.wait_ge(sem["gated"], gated_value)
                    v_.tensor_tensor(h1f[:, :, :], sa[:, :, :], two(5), ALU.mult).then_inc(sem["prod_done"], 1)

                def h1_low(n, b):
                    dve.wait_ge(sem["h1_hi_ready"], n)
                    v_.tensor_tensor(h1_lo[b][:, :, :], h1f[:, :, :], h1_hi[b][:, :, :].bitcast(F32),
                                     ALU.subtract).then_inc(sem["h1_ready"], 1)

                slo(lay, k0 + 2)
                slo(lay, k0 + 3)
                row_scale(lay, 2 * f)
                dve.wait_ge(sem["rB_ready"], lay * 4 + 2 * f + 1)
                scale_up(lay * NU + (k0 + RING + 1))
                product(lay * NU + (k0 + 1 + RING + 1), F * FT + 1)
                h1_low(F * FT + 1, 0)
                with nc.vector.Fori(0, (FT - 1) // 2) as jj:
                    for b in range(2):
                        j = jj * 2 + b
                        k = k0 + 4 + 3 * b
                        lo(lay, jj * 6 + k, k % RING)
                        scale_up(lay * NU + jj * 6 + (3 * b + k0 + 2 + RING + 1))
                        lo(lay, jj * 6 + (k + 1), (k + 1) % RING)
                        product(lay * NU + jj * 6 + (3 * b + k0 + 3 + RING + 1), F * FT + j + 2)
                        h1_low(F * FT + j + 2, 1 - b)
                        lo(lay, jj * 6 + (k + 2), (k + 2) % RING)
                slo(lay, k0 + U_FFN + 1)
                for i in range(4):
                    if i < 3:
                        dve.wait_ge(sem["down_done"], F * 3 + (i + 1))
                    else:
                        done(lay, k0 + U_FFN - 1)
                    v_.scalar_tensor_tensor(out=h[:, 2 * i:2 * i + 2, :], in0=two(i), scalar=0.5,
                                            in1=h[:, 2 * i:2 * i + 2, :], op0=ALU.mult, op1=ALU.add)\
                        .then_inc(sem["h_ready"], 1)
                    if i:
                        low(lay, 2 * f + 1, i - 1)
                low(lay, 2 * f + 1, 3)

            def softplus_gates(lay):
                dve.wait_ge(sem["pre_ready"], lay + 1)
                ps = bank[7][:, 0:80].rearrange("p (c n) -> p c n", c=NC)
                dve.wait_ge(sem["row_bcast"], 1)
                ch.add(v_.tensor_tensor(pre[:, :, :], ps,
                                        row_all[:, lay, 0:40].unsqueeze(1).broadcast_to([P, NC, 40]), ALU.add))
                ch.wait()
                ch.add(v_.tensor_scalar(spx[:, :, 0:4], pre[:, :, 4:8], -1.0, None, ALU.mult))
                ch.add(v_.tensor_copy(spx[:, :, 4:36], pre[:, :, 8:40]))
                ch.wait()
                v_.scalar_tensor_tensor(out=sp_a[:, :, :], in0=spx[:, :, :], scalar=-1.0, in1=spx[:, :, :],
                                        op0=ALU.mult, op1=ALU.max).then_inc(sem["x_abs"], 1)
                ch.add(v_.tensor_scalar(spx[:, :, :], spx[:, :, :], 0.0, None, ALU.max))
                dve.wait_ge(sem["sp_exp"], lay + 1)
                ch.add(v_.tensor_scalar(sp_a[:, :, :], sp_b[:, :, :], 2.0, None, ALU.add))
                ch.wait()
                ch.add(v_.reciprocal(sp_c[:, :, :], sp_a[:, :, :]))
                ch.wait()
                ch.add(v_.tensor_tensor(sp_a[:, :, :], sp_b[:, :, :], sp_c[:, :, :], ALU.mult))
                ch.wait()
                ch.add(v_.tensor_tensor(sp_b[:, :, :], sp_a[:, :, :], sp_a[:, :, :], ALU.mult))
                ch.wait()
                ch.add(v_.tensor_scalar(sp_c[:, :, :], sp_b[:, :, :], 1.0 / 17, None, ALU.mult))
                for n in (15, 13, 11, 9, 7, 5, 3):
                    ch.wait()
                    ch.add(v_.scalar_tensor_tensor(out=sp_c[:, :, :], in0=sp_c[:, :, :], scalar=1.0 / n,
                                                   in1=sp_b[:, :, :], op0=ALU.add, op1=ALU.mult))
                ch.wait()
                ch.add(v_.scalar_tensor_tensor(out=sp_c[:, :, :], in0=sp_c[:, :, :], scalar=1.0,
                                               in1=sp_a[:, :, :], op0=ALU.add, op1=ALU.mult))
                ch.wait()
                ch.add(v_.scalar_tensor_tensor(out=spx[:, :, :], in0=sp_c[:, :, :], scalar=2.0,
                                               in1=spx[:, :, :], op0=ALU.mult, op1=ALU.add))
                ch.wait()
                dve.wait_ge(sem["ea_ready"], lay + 1)
                ch.add(v_.scalar_tensor_tensor(out=dA[:, :, :], in0=spx[:, :, 4:36], scalar=-1.0,
                                               in1=e_a[:, :].unsqueeze(1).broadcast_to([P, NC, SH]),
                                               op0=ALU.mult, op1=ALU.mult))
                ch.wait()
                ch.add(v_.tensor_copy(dA_hi[:, :, :], dA[:, :, :]))
                ch.wait()
                v_.tensor_tensor(dA_lo[:, :, :], dA[:, :, :], dA_hi[:, :, :].bitcast(F32), ALU.subtract)\
                    .then_inc(sem["dA_ready"], 1)

            def gate_rows(lay):
                dve.wait_ge(sem["row_tr"], lay + 1)
                ch.add(v_.tensor_copy(r_i[:, :], bank[6][0:MH, 0:S]))
                ch.add(v_.tensor_copy(r_f[:, :], bank[6][0:MH, S:2 * S]))
                ch.wait()
                for c in range(NC):
                    s = slice(c * P, (c + 1) * P)
                    ch.add(v_.tensor_tensor_scan(r_b[:, s], ones[0:MH, :], r_f[:, s], 0.0, ALU.mult, ALU.subtract))
                ch.wait()
                ch.add(v_.tensor_tensor(r_w[:, :], r_i[:, :], r_b[:, :], ALU.subtract))
                ch.wait()
                ch.add(v_.tensor_tensor_scan(r_m[:, 0:P], r_w[:, 0:P], r_w[:, 0:P], 0.0, ALU.max, ALU.max))
                ch.wait()
                ch.add(v_.tensor_tensor(m_start[:, :], r_b[:, P - 1:P], r_m[:, P - 1:P], ALU.add))
                ch.wait()
                ch.add(v_.tensor_tensor_scan(r_m[:, P:], r_w[:, P:], r_w[:, P:], m_start[:, :], ALU.max, ALU.max))
                ch.wait()
                ch.add(v_.tensor_copy(r_x[:, 0:2, :], r_w[:, :].rearrange("p (c t) -> p c t", c=NC)))
                ch.add(v_.scalar_tensor_tensor(out=r_x[:, 2:4, :], in0=r_b[:, :].rearrange("p (c t) -> p c t", c=NC),
                                               scalar=-1.0, in1=r_m[:, :].rearrange("p (c t) -> p c t", c=NC),
                                               op0=ALU.mult, op1=ALU.subtract))
                ch.add(v_.tensor_scalar(r_x[:, 4, :], r_m[:, P:], m_start[:, :], -1.0, ALU.subtract, ALU.mult))
                ch.add(v_.tensor_scalar(r_x[:, 5, :], r_w[:, 0:P], r_m[:, P - 1:P], None, ALU.subtract))
                v_.tensor_tensor(M4[:, :, :], r_m[:, :].unsqueeze(1).broadcast_to([MH, MH, S]),
                                 ident[0:MH, 0:MH].unsqueeze(2).broadcast_to([MH, MH, S]),
                                 ALU.mult).then_inc(sem["row_ready"], 1)

            def groups(lay):
                v_.memset(xin[:, :, :, 0:3], 0.0)
                ch.add(v_.memset(vtok[:, :, MV:MV + 1], 1.0))

                def body(g, first):
                    G = dve.snap(lay * NG + g)

                    def step(p):
                        k = K_MIX + p + 2
                        lo(lay, g * GU + k, k % RING)

                    def unit_done(p):
                        dve.wait_ge(sem["unit_done"], lay * NU + g * GU + (K_MIX + p + RING + 1))

                    def evac(p, dst):
                        unit_done(p)
                        v_.tensor_tensor(dst, two(p % 3), by_token(rB[:, :]), ALU.mult).then_inc(sem["evac"], 1)

                    def taken(p):
                        dve.wait_ge(sem["evac"], lay * NE + g * GU + (p + RING + 1))

                    def conv(i, buf, tiles, dst):
                        for j in range(SCONV):
                            for q, t in enumerate(tiles):
                                src = xin[:, buf, q, j:j + S]
                                if j == 0:
                                    ins = v_.tensor_scalar(dst[:, q, :], src, gcw[:, 0, t:t + 1], gcb[:, t:t + 1],
                                                           ALU.mult, ALU.add)
                                else:
                                    ins = v_.scalar_tensor_tensor(out=dst[:, q, :], in0=src, scalar=gcw[:, j, t:t + 1],
                                                                  in1=dst[:, q, :], op0=ALU.mult, op1=ALU.add)
                                if j < SCONV - 1 or q == 0:
                                    ch.add(ins)
                                else:
                                    ins.then_inc(sem["conv_done"], 1)
                            if j < SCONV - 1:
                                ch.wait()

                    def silu(i, dst):
                        dve.wait_ge(sem["tanh_done"], G * 3 + (i + 1))
                        v_.scalar_tensor_tensor(out=dst, in0=cth[:, :, :], scalar=1.0, in1=dst,
                                                op0=ALU.add, op1=ALU.mult).then_inc(sem["cv_ready"], 1)

                    heads = bass.ds(g * EH, EH)

                    def per_head(col):
                        return col.unsqueeze(2).broadcast_to([P, EH, HP])

                    def split_heads(x):
                        return x.rearrange("p (e d) -> p e d", e=EH)

                    def distances():
                        dve.wait_ge(sem["gtk_ready"], G + 1)
                        dve.wait_ge(sem["scores_done"], G + 1)
                        for c in range(NC):
                            i = v_.tensor_scalar(pm[:, c, :], bank[3][:, S + c * P:S + (c + 1) * P], gtk[:, c:c + 1],
                                                 0.0, ALU.subtract, ALU.max)
                        i.then_inc(sem["d_ready"], 1)

                    def mask_cb():
                        dve.wait_ge(sem["cb_done"], G + 1)
                        v_.tensor_tensor(cbm[:, :, :], bank[5][:, 0:S].rearrange("p (c t) -> p c t", c=NC),
                                         tri_le[:, :].unsqueeze(1).broadcast_to([P, NC, P]), ALU.mult)\
                            .then_inc(sem["cbm_done"], 1)

                    def weigh_scores():
                        dve.wait_ge(sem["pm_ready"], G + 1)
                        v_.tensor_tensor(scT[:, :, :], pm[:, :, :], bank[3][:, 0:S].rearrange("p (c t) -> p c t", c=NC),
                                         ALU.mult).then_inc(sem["sct_ready"], 1)

                    step(0)
                    step(1)
                    if first:
                        row_scale(lay, 1)
                        dve.wait_ge(sem["rB_ready"], lay * 4 + 2)
                        dve.wait_ge(sem["small_done"], lay + 1)
                        v_.tensor_tensor(pre_row[:, :], bank[7][0:40, 0:S], rB[0:40, :], ALU.mult)\
                            .then_inc(sem["pre_row_ready"], 1)
                    dve.wait_ge(sem["group_ready"], G + 1)
                    evac(BC, xin[:, 0, :, 3:])
                    taken(BC)
                    conv(0, 0, (0, 1), bcv[:, :, :])
                    unit_done(QK)
                    v_.scalar_tensor_tensor(out=qT[:, :], in0=bank[1][:, 0:S], scalar=MQK ** -0.5, in1=rB[:, :],
                                            op0=ALU.mult, op1=ALU.mult)
                    v_.tensor_tensor(kT[:, :], bank[1][:, S:2 * S], rB[:, :], ALU.mult).then_inc(sem["evac"], 1)
                    silu(0, bcv[:, :, :])
                    if first:
                        softplus_gates(lay)
                        step(2)
                        gate_rows(lay)
                    else:
                        step(2)
                        distances()
                    step(3)
                    evac(X01, xin[:, 1, :, 3:])
                    taken(X01)
                    conv(1, 1, (2, 3), xcv[:, 0:2, :])
                    silu(1, xcv[:, 0:2, :])
                    if not first:
                        weigh_scores()
                    else:
                        distances()
                    evac(X23, xin[:, 0, :, 3:])
                    taken(X23)
                    conv(2, 0, (4, 5), xcv[:, 2:4, :])
                    unit_done(V)
                    for c in range(NC):
                        i = v_.tensor_scalar(vtok[:, c, 0:MV], bank[1][:, c * MV:(c + 1) * MV], rms[:, c:c + 1],
                                             None, ALU.mult)
                    i.then_inc(sem["evac"], 1)
                    silu(2, xcv[:, 2:4, :])
                    if first:
                        weigh_scores()
                    mask_cb()
                    step(4)
                    dve.wait_ge(sem["ysum_ready"], G + 1)
                    evac(Z0, zs[:, 0:2, :])
                    step(5)
                    dve.wait_ge(sem["xtr_done"], G + 1)
                    for c in range(NC):
                        ch.add(v_.tensor_tensor(split_heads(xw[:, c, :]), split_heads(bank[6 + c][:, :]),
                                                per_head(spx[:, c, bass.ds(g * EH + 4, EH)]), ALU.mult))
                    ch.wait()
                    dve.wait_ge(sem["cum_exp"], lay + 1)
                    v_.tensor_tensor(split_heads(xwe[:, :]), split_heads(xw[:, 0, :]), per_head(w_end[:, heads]),
                                     ALU.mult).then_inc(sem["xw_ready"], 1)
                    dve.wait_ge(sem["z_tanh"], G * 2 + 1)
                    v_.scalar_tensor_tensor(out=zs[:, 0:2, :], in0=zth[:, :, :], scalar=1.0, in1=zs[:, 0:2, :],
                                            op0=ALU.add, op1=ALU.mult).then_inc(sem["zth_ready"], 1)
                    step(6)
                    evac(Z1, zs[:, 2:4, :])
                    step(7)
                    dve.wait_ge(sem["inter_ready"], G + 1)
                    v_.tensor_tensor(num[:, 1, 0:257], bank[5][:, 0:257], inter[:, 0:257], ALU.add)\
                        .then_inc(sem["num1_ready"], 1)
                    dve.wait_ge(sem["num1_ready"], G + 1)
                    ch.add(v_.scalar_tensor_tensor(out=den[:, :].unsqueeze(2), in0=num[:, :, MV:MV + 1], scalar=-1.0,
                                                   in1=num[:, :, MV:MV + 1], op0=ALU.mult, op1=ALU.max))
                    ch.wait()
                    ch.add(v_.tensor_tensor(den[:, :], den[:, :], gtk[:, 2:4], ALU.max))
                    ch.wait()
                    ch.add(v_.reciprocal(rden[:, :], den[:, :]))
                    dve.wait_ge(sem["nsq_ready"], G + 1)
                    ch.wait()
                    ch.add(v_.tensor_tensor(hvar[:, :], nss[:, :], rden[:, :], ALU.mult))
                    ch.wait()
                    ch.add(v_.tensor_tensor(hvar[:, :], hvar[:, :], rden[:, :], ALU.mult))
                    ch.wait()
                    v_.tensor_scalar(hvar[:, :], hvar[:, :], 1.0 / MV, EPS, ALU.mult, ALU.add).then_inc(sem["hvar_ready"], 1)
                    dve.wait_ge(sem["hrms_ready"], G + 1)
                    ch.add(v_.tensor_tensor(hsc[:, :], hrms[:, :], rden[:, :], ALU.mult))
                    ch.wait()
                    for c in range(NC):
                        i = v_.tensor_scalar(num[:, c, 0:MV], num[:, c, 0:MV], hsc[:, c:c + 1], None, ALU.mult)
                    i.then_inc(sem["hn_ready"], 1)
                    dve.wait_ge(sem["z_tanh"], G * 2 + 2)
                    v_.scalar_tensor_tensor(out=zs[:, 2:4, :], in0=zth[:, :, :], scalar=1.0, in1=zs[:, 2:4, :],
                                            op0=ALU.add, op1=ALU.mult).then_inc(sem["zth_ready"], 1)
                    evac(O, osg[:, :, :])
                    step(8)
                    dve.wait_ge(sem["y_done"], G + 1)
                    for t in range(4):
                        ch.add(v_.scalar_tensor_tensor(out=xcv[:, t, :], in0=xcv[:, t, :], scalar=gdk[:, t:t + 1],
                                                       in1=bank[6 + t // 2][:, (t % 2) * S:(t % 2 + 1) * S],
                                                       op0=ALU.mult, op1=ALU.add))
                    ch.wait()
                    dve.wait_ge(sem["zth_ready"], G * 2 + 2)
                    v_.scalar_tensor_tensor(out=y_feat[:, bass.ds(g * 4, 4), :].rearrange("p a b -> p (a b)"),
                                            in0=xcv[:, :, :].rearrange("p a b -> p (a b)"), scalar=0.5,
                                            in1=zs[:, :, :].rearrange("p a b -> p (a b)"),
                                            op0=ALU.mult, op1=ALU.mult).then_inc(sem["y_ready"], 1)
                    dve.wait_ge(sem["o_tanh"], G + 1)
                    for t in range(2):
                        ch.add(v_.tensor_scalar(osg[:, t, :], osg[:, t, :], 1.0, ghn[:, t:t + 1], ALU.add, ALU.mult))
                    ch.wait()
                    dve.wait_ge(sem["hnT_done"], G + 1)
                    v_.tensor_tensor(osg[:, :, :], osg[:, :, :], two(3), ALU.mult).then_inc(sem["ha32_ready"], 1)
                    dve.wait_ge(sem["ha_hi_ready"], G + 1)
                    v_.tensor_tensor(ha_lo[:, bass.ds(g * 2, 2), :], osg[:, :, :],
                                     ha_hi[:, bass.ds(g * 2, 2), :].bitcast(F32), ALU.subtract).then_inc(sem["ha_ready"], 1)
                    evac(GA, gate_a[:, bass.ds(g * 2, 2), :])
                    dve.wait_ge(sem["ysq_ready"], G + 1)
                    dve.sem_inc(sem["group_free"], 1)
                    ch.clear()

                ch.clear()
                body(0, True)
                with nc.vector.Fori(1, NG) as g:
                    body(g, False)

            dve.wait_ge(sem["const_ready"], 2)
            ch.add(v_.tensor_copy(tri_gt_r[:, :], tri_gt[:, :]))
            ch.add(v_.tensor_copy(ones_r[:, :], ones[:, :]))
            for i in range(4):
                dve.wait_ge(sem["xtr_in"], i + 1)
                v_.tensor_copy(h[:, 2 * i:2 * i + 2, :], two(i)).then_inc(sem["h_ready"], 1)
            dve.wait_ge(sem["par_tr"], 1)
            for l in range(DEPTH):
                ch.add(v_.tensor_copy(par_all[:, l, 0:96], bank[4 + l][:, 0:96]))
                ch.add(v_.tensor_copy(par_all[:, l, 96:176], bank[4 + l][:, 128:208]))
            ch.add(v_.tensor_copy(g_fin[:, :], bank[4][:, 256:264]))
            ch.clear()

            with nc.vector.Fori(0, DEPTH) as lay:
                v_.tensor_copy(par[:, 144:176], par_all[:, lay, 144:176]).then_inc(sem["par_ready"], 1)
                dve.wait_ge(sem["par_ready"], lay + 1)
                slo(lay, 0)
                for i in range(4):
                    low(lay, 0, i)
                slo(lay, 1)
                ch.add(v_.tensor_scalar(par[:, 0:120], par_all[:, lay, 0:120], 0.5, None, ALU.mult))
                ch.add(v_.tensor_copy(par[:, 120:136], par_all[:, lay, 120:136]))
                ch.add(v_.tensor_scalar(par[:, 136:144], par_all[:, lay, 136:144], 0.5, None, ALU.mult))
                dve.wait_ge(sem["row_bcast"], 1)
                for b in range(2):
                    hp = slice(b * HP, (b + 1) * HP)
                    ch.add(v_.tensor_copy(dcol[hp, :], row_all[hp, lay, 72 + b:104:2]))
                ffn(lay, 0, 0)
                dve.wait_ge(sem["wsm_hi_ready"], lay + 1)
                v_.tensor_tensor(wsm_lo[:, :, :], wsm[:, :, :], wsm_hi[:, :, :].bitcast(F32),
                                 ALU.subtract).then_inc(sem["wsm_ready"], 1)
                groups(lay)
                dve.wait_ge(sem["ysum_ready"], lay * NG + NG + 1)
                for q in range(4):
                    done(lay, K_GB + q)
                    v_.tensor_tensor(gate_b[:, 2 * q:2 * q + 2, :], two(q % 3), by_token(rB[:, :]), ALU.mult)\
                        .then_inc(sem["evac"], 1)
                    slo(lay, K_GB + q + 2)
                    dve.wait_ge(sem["yb_hi_ready"], lay * 4 + q + 1)
                    for t in range(4 * q, 4 * q + 4):
                        i = v_.scalar_tensor_tensor(out=yb_lo[:, t, :], in0=y_feat[:, t, :], scalar=par[:, 120 + t:121 + t],
                                                    in1=yb_hi[:, t, :].bitcast(F32), op0=ALU.mult, op1=ALU.subtract)
                    i.then_inc(sem["yb_ready"], 1)
                    if q == 0:
                        dve.wait_ge(sem["yss_done"], lay + 1)
                        scale_column(bank[7], 1.0 / SI, "yvar_ready")
                    if q == 1:
                        dve.wait_ge(sem["yrms_ready"], lay + 1)
                        scale_diagonal("ydiag_ready")
                ch.clear()
                with nc.vector.Fori(0, 4) as m:
                    for r in range(2):
                        k = K_MERGE + r + 2
                        lo(lay, m * 3 + k, k % RING)
                    dve.wait_ge(sem["gate_tanh"], (lay + 1) * 2 * NG)
                    dve.wait_ge(sem["unit_done"], lay * NU + m * 3 + (K_MERGE + RING + 1))
                    v_.scalar_tensor_tensor(out=mtmp[:, :, :], in0=gate_a[:, bass.ds(m * 2, 2), :], scalar=1.0,
                                            in1=two(0), op0=ALU.add, op1=ALU.mult).then_inc(sem["merge_read"], 1)
                    k = K_MERGE + 4
                    lo(lay, m * 3 + k, k % RING)
                    dve.wait_ge(sem["unit_done"], lay * NU + m * 3 + (K_MERGE + 2 + RING + 1))
                    v_.scalar_tensor_tensor(out=mrg[:, :, :], in0=gate_b[:, bass.ds(m * 2, 2), :], scalar=1.0,
                                            in1=two(1), op0=ALU.add, op1=ALU.mult).then_inc(sem["merge_read"], 1)
                    dve.wait_ge(sem["merge_read"], lay * 8 + m * 2 + 4)
                    dve.wait_ge(sem["yB_ready"], lay + 1)
                    ch.add(v_.tensor_tensor(mrg[:, :, :], mrg[:, :, :],
                                            by_token(rB[:, :]), ALU.mult))
                    ch.wait()
                    v_.tensor_tensor(mrg[:, :, :], mrg[:, :, :], mtmp[:, :, :], ALU.add).then_inc(sem["mrg_ready"], 1)
                    dve.wait_ge(sem["m_hi_ready"], lay * 4 + m + 1)
                    v_.tensor_tensor(u_lo[:, bass.ds(m * 2, 2), :], mrg[:, :, :],
                                     u_hi[:, bass.ds(m * 2, 2), :].bitcast(F32), ALU.subtract).then_inc(sem["m_lo_ready"], 1)
                    ch.clear()
                for q in range(4):
                    slo(lay, K_OUT + q + 2)
                    done(lay, K_OUT + q)
                    v_.scalar_tensor_tensor(out=h[:, 2 * q:2 * q + 2, :], in0=two(q % 3), scalar=0.5,
                                            in1=h[:, 2 * q:2 * q + 2, :], op0=ALU.mult, op1=ALU.add)\
                        .then_inc(sem["h_ready"], 1)
                    if q:
                        low(lay, 2, q - 1)
                low(lay, 2, 3)
                ffn(lay, 1, K_FFN2)
                slo(lay, K_PLE + 2)
                slo(lay, K_PLE + 3)
                row_scale(lay, 3)
                dve.wait_ge(sem["pp_ready"], lay * 4 + 4)
                dve.wait_ge(sem["rB_ready"], lay * 4 + 4)
                for q in range(4):
                    done(lay, K_PLE + q)
                    v_.tensor_tensor((sa, h1f)[q % 2][:, :, :], two(q % 3), by_token(rB[:, :]), ALU.mult)\
                        .then_inc(sem["ple_scaled"], 1)
                    dve.wait_ge(sem["ple_tanh"], lay * 4 + q + 1)
                    t = sa if q % 2 == 0 else h1f
                    ch.add(v_.scalar_tensor_tensor(out=t[:, :, :], in0=t[:, :, :], scalar=1.0,
                                                   in1=p_proj[:, 2 * q:2 * q + 2, :], op0=ALU.add, op1=ALU.mult))
                    ch.wait()
                    v_.scalar_tensor_tensor(out=h[:, 2 * q:2 * q + 2, :], in0=t[:, :, :], scalar=0.5,
                                            in1=h[:, 2 * q:2 * q + 2, :], op0=ALU.mult, op1=ALU.add)\
                        .then_inc(sem["h_ready"], 1)
                ch.clear()
            for k in range(KD):
                dve.wait_ge(sem["h_ready"], DEPTH * 16 + k // 2 + 1)
                v_.tensor_scalar(hg[:, k, :], h[:, k, :], g_fin[:, k:k + 1], None, ALU.mult).then_inc(sem["hg_ready"], 1)
            dve.wait_ge(sem["ss_done"], DEPTH * 4 + 1)
            scale_column(bank[6], 1.0 / D, "var_ready")
            dve.wait_ge(sem["rms_ready"], DEPTH * 4 + 1)
            dve.wait_ge(sem["xt_done"], 4)
            for q in (2, 3):
                v_.tensor_scalar(x_tok[:, 1, (q % 2) * 512:(q % 2) * 512 + 512], bank[q][:, :], rms[:, 1:2], None,
                                 ALU.mult).then_inc(sem["fin_done"], 1)

        @block.tensor
        def _(pe):
            mm = nc.tensor.matmul

            def weights(lay, k):
                pe.wait_ge(sem["w_lo"], lay * NU + k + (RING + 1))

            def zero_bank(b):
                mm(bank[b][:, :], zeros[:, :], zeros[:, :].unsqueeze(1).broadcast_to([P, 4, P]), start=True,
                   stop=False, skip_group_check=True)

            def feat(slot, b, xh, xl, seeded=False, between=None):
                for m in range(2):
                    o = bank[b][:, m * S:(m + 1) * S]
                    cs = slice(m * P, (m + 1) * P)
                    for k in range(KD):
                        if between and m == 1 and k == KD // 2:
                            between()
                        for q, (w, x) in enumerate(((whi, xh), (whi, xl), (wlo, xh))):
                            i = mm(o, w[slot][:, k, cs], x[:, k, :], start=(k + q == 0 and not seeded),
                                   stop=(k == KD - 1 and q == 2 and not seeded), skip_group_check=seeded)
                i.then_inc(sem["unit_done"], 1)

            def feat_early(slot, b, xh, xl, ready):
                for k in range(KD):
                    ready(k)
                    if k == 0:
                        zero_bank(b)
                    for m in range(2):
                        cs = slice(m * P, (m + 1) * P)
                        for w, x in ((whi, xh), (whi, xl), (wlo, xh)):
                            i = mm(bank[b][:, m * S:(m + 1) * S], w[slot][:, k, cs], x[:, k, :], start=False, stop=False,
                                   skip_group_check=True)
                i.then_inc(sem["unit_done"], 1)

            def feat_first(slot, b, lay, n):
                feat_early(slot, b, U_HI[n], U_LO[n],
                           lambda k: pe.wait_ge(sem["u_lo_ready"], (lay * 4 + n) * KD + (k + 1)))

            def tok(slot, b, xh, xl, between=None):
                for c in range(NC):
                    if c and between:
                        between()
                    o = bank[b][:, c * NP:(c + 1) * NP]
                    cs = slice(c * P, (c + 1) * P)
                    for k in range(KD):
                        mm(o, xh[:, k, cs], whi[slot][:, k, :], start=(k == 0), stop=False)
                        mm(o, xh[:, k, cs], wlo[slot][:, k, :], start=False, stop=False)
                        i = mm(o, xl[:, k, cs], whi[slot][:, k, :], start=False, stop=(k == KD - 1))
                i.then_inc(sem["unit_done"], 1)

            def norm(lay, n):
                N = lay * 4 + n
                pe.wait_ge(sem["sq_added"], N * 3 + 3)
                for k in range(2):
                    ins = mm(bank[6][:, 0:S], ones[:, :], sq[:, k, :], start=(k == 0), stop=(k == 1))
                ins.then_inc(sem["ss_done"], 1)

            def norm_rows(lay, n):
                pe.wait_ge(sem["rdiag_ready"], lay * 4 + n + 1)
                for c in range(NC):
                    ins = mm(bank[6][:, S + c * P:S + (c + 1) * P], ones[:, :], rdiag[:, c, :], start=True, stop=True)
                ins.then_inc(sem["rB_done"], 1)

            def ffn(lay, f, k0):
                F = lay * 2 + f
                s = [(k0 + r) % RING for r in range(3)]

                def down(slot, b, last=False):
                    w = [x[slot][:, :, :].rearrange("p a b -> p (a b)").rearrange("p (k m) -> p k m", k=2)
                         for x in (whi, wlo)]
                    for m in range(KD):
                        o = bank[m // 2][:, (m % 2) * S:(m % 2 + 1) * S]
                        cs = slice(m * P, (m + 1) * P)
                        for kk in range(2):
                            for ww, xx in ((w[0], h1_hi[b]), (w[0], h1_lo[b]), (w[1], h1_hi[b])):
                                i = mm(o, ww[:, kk, cs], xx[:, kk, :], start=False, stop=False, skip_group_check=True)
                        if last and m in (1, 3, 5):
                            i.then_inc(sem["down_done"], 1)
                    i.then_inc(sem["unit_done"], 1)

                weights(lay, k0)
                if f == 1:
                    pe.wait_ge(sem["pp_ready"], lay * 4 + 4)
                xh, xl = U_HI[2 * f], U_LO[2 * f]
                feat_first(s[0], 4, lay, 2 * f)
                norm(lay, 2 * f)
                for b in range(4):
                    zero_bank(b)
                weights(lay, k0 + 1)
                feat(s[1], 5, xh, xl, between=lambda: norm_rows(lay, 2 * f))
                with nc.tensor.Fori(0, (FT - 1) // 2) as jj:
                    for b in range(2):
                        j = jj * 2 + b
                        weights(lay, jj * 6 + (3 * b + k0 + 2))
                        pe.wait_ge(sem["up_scaled"], F * FT + j + 1)
                        feat(s[2], 4, xh, xl)
                        weights(lay, jj * 6 + (3 * b + k0 + 3))
                        pe.wait_ge(sem["prod_done"], F * FT + j + 1)
                        feat(s[0], 5, xh, xl)
                        weights(lay, jj * 6 + (3 * b + k0 + 4))
                        pe.wait_ge(sem["h1_ready"], F * FT + j + 1)
                        down(s[1], b)
                weights(lay, k0 + U_FFN - 1)
                pe.wait_ge(sem["h1_ready"], (F + 1) * FT)
                down(s[2], 0, last=True)

            def small(lay):
                pe.wait_ge(sem["wsm_ready"], lay + 1)
                for k in range(KD):
                    for q, (w, x) in enumerate(((wsm_hi, u_hi), (wsm_hi, u_lo), (wsm_lo, u_hi))):
                        i = mm(bank[7][0:40, 0:S], w[:, k, :], x[:, k, :], start=(k + q == 0), stop=(k == KD - 1 and q == 2))
                i.then_inc(sem["small_done"], 1)

            def small_back(lay):
                pe.wait_ge(sem["pre_row_ready"], lay + 1)
                for c in range(NC):
                    i = mm(bank[7][:, c * 40:(c + 1) * 40], pre_row[:, c * P:(c + 1) * P], ident[0:40, 0:40],
                           start=True, stop=True)
                i.then_inc(sem["pre_ready"], 1)

            def gates(lay):
                pe.wait_ge(sem["dA_ready"], lay + 1)
                mm(bank[7][:, 0:SH], tri_gt[:, :], dA[:, 0, :], start=True, stop=True).then_inc(sem["cum_done"], 1)
                for c in range(NC):
                    nc.tensor.transpose(bank[6][0:MH, c * P:(c + 1) * P], pre[:, c, 0:MH], ident[:, :])
                    i = nc.tensor.transpose(bank[6][0:MH, S + c * P:S + (c + 1) * P], spx[:, c, 0:MH], ident[:, :])
                i.then_inc(sem["row_tr"], 1)

            def gates_back(lay):
                pe.wait_ge(sem["row_ready"], lay + 1)
                for r in range(6):
                    i = mm(bank[6][:, r * MH:(r + 1) * MH], r_x[:, r, :], ident[0:MH, 0:MH], start=True, stop=True)
                i.then_inc(sem["row_back"], 1)

            def groups(lay):
                def body(g, first):
                    G = pe.snap(lay * NG + g)

                    def unit(p, kind):
                        weights(lay, g * GU + (K_MIX + p))
                        pe.wait_ge(sem["evac"], lay * NE + g * GU + (p + 1))
                        kind((K_MIX + p) % RING, p % 3, u_hi, u_lo)

                    def evac(p):
                        pe.wait_ge(sem["evac"], lay * NE + g * GU + (p + RING + 1))

                    def segments(c, half):
                        for b in (2 * half, 2 * half + 1):
                            pe.wait_ge(sem["r_built"], G * 8 + (4 * c + b + 1))
                            todo = [(4 + 2 * c + half, tri_gt_r)]
                            if c == 1:
                                pe.wait_ge(sem["exp_done"], G * 4 + (half + 1))
                                todo.append((4 + half, ones_r))
                            for bk, w in todo:
                                for q in range(2):
                                    i = mm(bank[bk][:, (b % 2) * S:(b % 2 + 1) * S], w[:, :],
                                           R[:, b % 2, q, :, :], start=(q == 0), stop=(q == 1))
                            i.then_inc(sem["seg_done"], 1)

                    def cb():
                        pe.wait_ge(sem["cv_ready"], G * 3 + 1)
                        pe.wait_ge(sem["acs_exp"], G * 2 + 2)
                        for c in range(NC):
                            cs_ = slice(c * P, (c + 1) * P)
                            mm(bank[5][:, cs_], bcv[:, 0, cs_], bcv[:, 1, cs_], start=True, stop=True)
                        nc.tensor.transpose(bank[5][:, 256:384], bcv[:, 0, 0:P], ident[:, :])
                        nc.tensor.transpose(bank[5][:, 384:512], kT[:, 0:P], ident[:, :]).then_inc(sem["cb_done"], 1)

                    def scores():
                        for c in range(NC):
                            cs_ = slice(c * P, (c + 1) * P)
                            mm(bank[3][:, cs_], kT[:, cs_], qT[:, cs_], start=True, stop=True)
                        mm(bank[3][:, S:2 * S], ones[0:MH, :], M4[:, bass.ds(g, 1), :].rearrange("p a b -> p (a b)"),
                           start=True, stop=True).then_inc(sem["scores_done"], 1)

                    if first:
                        weights(lay, K_MIX)
                        pe.wait_ge(sem["evac"], lay * NE + 1)
                        feat_first(K_MIX % RING, 0, lay, 1)
                        norm(lay, 1)
                        small(lay)
                        unit(QK, lambda *a: feat(*a, between=lambda: norm_rows(lay, 1)))
                        small_back(lay)
                        unit(X01, feat)
                        unit(X23, lambda *a: feat(*a, between=lambda: gates(lay)))
                        segments(0, 0)
                        gates_back(lay)
                        segments(0, 1)
                        scores()
                        pe.wait_ge(sem["tok_ready"], lay * 2 + 2)
                        unit(V, lambda *a: tok(*a, between=lambda: segments(1, 0)))
                        segments(1, 1)
                        cb()
                    else:
                        unit(BC, feat)
                        unit(QK, feat)
                        segments(0, 0)
                        unit(X01, lambda *a: feat(*a, between=lambda: segments(0, 1)))
                        segments(1, 0)
                        evac(QK)
                        scores()
                        unit(X23, lambda *a: feat(*a, between=lambda: segments(1, 1)))
                        unit(V, tok)
                        cb()
                    unit(Z0, feat)
                    pe.wait_ge(sem["sct_ready"], G + 1)
                    pe.wait_ge(sem["btok_ready"], G + 1)
                    evac(V)
                    mm(bank[3][:, 0:257], ktok[:, :], vtok[:, 0, 0:257], start=True, stop=True)
                    mm(bank[4][:, 0:257], scT[:, 0, :], vtok[:, 0, 0:257], start=True, stop=True)
                    mm(bank[5][:, 0:257], scT[:, 1, :], vtok[:, 1, 0:257], start=True, stop=True)\
                        .then_inc(sem["heads_done"], 1)
                    pe.wait_ge(sem["cv_ready"], G * 3 + 3)
                    pe.wait_ge(sem["exp_done"], G * 4 + 4)
                    for c in range(NC):
                        for t in range(4):
                            i = nc.tensor.transpose(bank[6 + c][:, t * P:(t + 1) * P], xcv[:, t, c * P:(c + 1) * P],
                                                    ident[:, :])
                    i.then_inc(sem["xtr_done"], 1)
                    unit(Z1, feat)
                    pe.wait_ge(sem["cst_ready"], G + 1)
                    mm(bank[3][:, 0:257], qT[:, P:2 * P], cst[:, 0:257], start=True, stop=True).then_inc(sem["im_done"], 1)
                    pe.wait_ge(sem["m_ready"], G * 2 + 2)
                    pe.wait_ge(sem["xw_ready"], G + 1)
                    pe.wait_ge(sem["num0_ready"], G + 1)
                    mm(bank[4][:, :], btok[:, :], xwe[:, :], start=True, stop=True).then_inc(sem["yi_done"], 1)
                    for c in range(NC):
                        if c == 1:
                            unit(O, feat)
                            pe.wait_ge(sem["st_ready"], G + 1)
                            pe.wait_ge(sem["cs_ready"], G + 1)
                        for e in range(EH):
                            es = slice(e * HP, (e + 1) * HP)
                            t = e // 2
                            o = bank[6 + t // 2][(e % 2) * HP:(e % 2 + 1) * HP, (t % 2) * S + c * P:(t % 2) * S + (c + 1) * P]
                            i = mm(o, xw[:, c, es], seg[:, c, e, :], start=True, stop=(c == 0))
                            if c == 1:
                                i = mm(o, st[:, es], cs[:, e, :], start=False, stop=True)
                    i.then_inc(sem["y_done"], 1)
                    pe.wait_ge(sem["hn_ready"], G + 1)
                    for t in range(2):
                        for c in range(NC):
                            i = nc.tensor.transpose(bank[3][:, t * S + c * P:t * S + (c + 1) * P],
                                                    num[:, c, t * P:(t + 1) * P], ident[:, :])
                    i.then_inc(sem["hnT_done"], 1)
                    unit(GA, feat)

                body(0, True)
                with nc.tensor.Fori(1, NG) as g:
                    body(g, False)

            pe.wait_ge(sem["const_ready"], 2)
            pe.wait_ge(sem["in_loaded"], 16)
            for i in range(4):
                for q in range(2):
                    for c in range(NC):
                        ins = nc.tensor.transpose(bank[i][:, q * S + c * P:q * S + (c + 1) * P],
                                                  x_tok[:, c, (2 * i + q) * P:(2 * i + q + 1) * P], ident[:, :])
                ins.then_inc(sem["xtr_in"], 1)
            pe.wait_ge(sem["par_loaded"], 16 * 9)
            for l in range(DEPTH):
                nc.tensor.transpose(bank[4 + l][:, 0:96], par_rows[0:96, l, 0, :], ident[0:96, 0:96])
                nc.tensor.transpose(bank[4 + l][:, 128:208], par_rows[0:80, l, 1, :], ident[0:80, 0:80])
            nc.tensor.transpose(bank[4][:, 256:264], gf_row[:, :], ident[0:KD, 0:KD]).then_inc(sem["par_tr"], 1)

            with nc.tensor.Fori(0, DEPTH) as lay:
                ffn(lay, 0, 0)
                groups(lay)
                for q in range(4):
                    weights(lay, K_GB + q)
                    pe.wait_ge(sem["evac"], lay * NE + (NG * GU + q + 1))
                    feat((K_GB + q) % RING, q % 3, u_hi, u_lo)
                    if q == 0:
                        pe.wait_ge(sem["ysum_ready"], lay * NG + NG + 1)
                        for t in range(4):
                            i = mm(bank[7][:, 0:S], ones[:, :], ysum[:, t, :], start=(t == 0), stop=(t == 3))
                        i.then_inc(sem["yss_done"], 1)
                pe.wait_ge(sem["ydiag_ready"], lay + 1)
                for c in range(NC):
                    i = mm(bank[7][:, c * P:(c + 1) * P], ones[:, :], rdiag[:, c, :], start=True, stop=True)
                i.then_inc(sem["yB_done"], 1)
                with nc.tensor.Fori(0, 4) as m:
                    pe.wait_ge(sem["ha_ready"], lay * NG + NG)
                    pe.wait_ge(sem["yB_ready"], lay + 1)
                    weights(lay, m * 3 + K_MERGE)
                    pe.wait_ge(sem["merge_read"], lay * 8 + m * 2 + 1)
                    feat(K_MERGE % RING, 0, ha_hi, ha_lo)
                    pe.wait_ge(sem["yb_ready"], lay * 4 + 4)
                    pe.wait_ge(sem["merge_read"], lay * 8 + m * 2 + 2)
                    zero_bank(1)
                    for kh in range(2):
                        weights(lay, m * 3 + (K_MERGE + 1 + kh))
                        feat((K_MERGE + 1 + kh) % RING, 1, yb_hi[:, kh * KD:(kh + 1) * KD, :],
                             yb_lo[:, kh * KD:(kh + 1) * KD, :], seeded=True)
                for q in range(4):
                    weights(lay, K_OUT + q)
                    if q == 3:
                        pe.wait_ge(sem["h_ready"], lay * 16 + 9)
                    if q == 0:
                        pe.wait_ge(sem["merge_read"], lay * 8 + 9)
                        feat_early(K_OUT % RING, 0, u_hi, u_lo, lambda k: pe.wait_ge(sem["m_lo_ready"], lay * 4 + (k // 2 + 1)))
                    else:
                        feat((K_OUT + q) % RING, q % 3, u_hi, u_lo)
                pe.wait_ge(sem["p_loaded"], lay * 32 + 32)
                for k in range(2):
                    for c in range(NC):
                        i = nc.tensor.transpose(bank[3][:, k * S + c * P:k * S + (c + 1) * P],
                                                p_tok[:, c, k * P:(k + 1) * P], ident[:, :])
                i.then_inc(sem["pt_done"], 1)

                def p_project(q):
                    for m in (2 * q, 2 * q + 1):
                        for k in range(2):
                            i = mm(bank[4 + q % 2][:, (m % 2) * S:(m % 2 + 1) * S], w_ple[:, k, m * P:(m + 1) * P],
                                   p_feat[:, k, :], start=(k == 0), stop=(k == 1))
                    i.then_inc(sem["pp_done"], 1)

                pe.wait_ge(sem["pt_ready"], lay + 1)
                p_project(0)
                p_project(1)
                for q in (2, 3):
                    pe.wait_ge(sem["pp_ready"], lay * 4 + q - 1)
                    p_project(q)
                ffn(lay, 1, K_FFN2)
                for q in range(4):
                    weights(lay, K_PLE + q)
                    if q == 3:
                        pe.wait_ge(sem["ple_scaled"], lay * 4 + 1)
                    if q == 0:
                        feat_first(K_PLE % RING, 0, lay, 3)
                        norm(lay, 3)
                    else:
                        feat((K_PLE + q) % RING, q % 3, U_HI[3], U_LO[3])
                    if q == 1:
                        norm_rows(lay, 3)
            for i in range(4):
                pe.wait_ge(sem["sq_ready"], DEPTH * 16 + i + 1)
                for k in (2 * i, 2 * i + 1):
                    ins = mm(bank[6][:, 0:S], ones[:, :], sq[:, k, :], start=(k == 0), stop=(k == KD - 1))
            ins.then_inc(sem["ss_done"], 1)
            for q in range(4):
                c, half = q // 2, q % 2
                pe.wait_ge(sem["hg_ready"], half * 4 + 4)
                for t in range(4):
                    i = nc.tensor.transpose(bank[q][:, t * P:(t + 1) * P], hg[:, half * 4 + t, c * P:(c + 1) * P], ident[:, :])
                i.then_inc(sem["xt_done"], 1)


_INS = ["x", "p", "g_ffn1", "w1_ffn1", "w3_ffn1", "w2_ffn1", "g_mix", "w_in", "b_igate", "b_fgate", "g_mlstm_head",
        "conv_w", "conv_b", "dt_bias", "a_log", "d_skip", "g_ssm_out", "w_branch_a", "w_branch_b", "w_out", "g_ffn2",
        "w1_ffn2", "w3_ffn2", "w2_ffn2", "g_ple", "w_ple_gate", "w_ple", "g_final"]


def kernel(**inputs):
    import numpy as _np
    import concourse.bacc as _bacc
    from concourse import mybir as _mybir
    from concourse.bass_utils import run_bass_kernel_spmd as _run

    nc = _bacc.Bacc("TRN2", target_bir_lowering=False, num_devices=1)
    arrays, tensors = {}, {}
    for name in _INS:
        a = _np.ascontiguousarray(inputs[name])
        arrays[f"in_{name}_dram"] = a
        tensors[name] = nc.dram_tensor(f"in_{name}_dram", a.shape, _mybir.dt.from_np(a.dtype),
                                       kind="ExternalInput").ap()
    out = nc.dram_tensor("out_0_dram", inputs["x"].shape, _mybir.dt.float32, kind="ExternalOutput").ap()
    trunk(nc, tensors, out)
    r = _run(nc, [arrays], core_ids=[0])
    return r.results[0]["out_0_dram"]
```
